# Optimizing a Trainium2 kernel written in Bass

```python
import math
import jax, jax.numpy as jnp
from jax import lax
import numpy as np

D_MODEL = 1024
BATCH = 1
SEQ = 128
DEPTH = 2
DEC_BATCH = 1
DEC_SEQ = 512
PAST_LEN = 128

GRID_W = 64
HEAD_DIM = 64
H_A = 4
H_B = 8
H_C = 8
KV_C = 2
NA_KH = 8
NA_KW = 16
ROPE_THETA = 10000.0
N_EXPERTS = 16
N_GROUPS = 4
EXPERTS_PER_GROUP = N_EXPERTS // N_GROUPS
TOP_K = 2
D_EXPERT = 256
Q_BLOCK = 128
N_BRANCH = 3
BRANCH_W = H_B * HEAD_DIM
LN_EPS = 1e-5
RMS_EPS = 1e-6
IN_SPLITS = (2 * H_A * HEAD_DIM, 2 * H_A * HEAD_DIM, H_A * 2 * HEAD_DIM,
             H_B * HEAD_DIM, H_B * HEAD_DIM, H_B * HEAD_DIM,
             H_C * HEAD_DIM, KV_C * HEAD_DIM, KV_C * HEAD_DIM)
V_PIECES = (2, 5, 8)

kernel_name = 'hybrid_diffusion_parallel_mixer_step'

def _in_offsets():
    offs = []
    acc = 0
    for s in IN_SPLITS[:-1]:
        acc += s
        offs.append(acc)
    return offs

def _rms(x, w):
    xf = x.astype(jnp.float32)
    y = xf * lax.rsqrt(jnp.mean(xf * xf, axis=-1, keepdims=True) + RMS_EPS) * w.astype(jnp.float32)
    return y.astype(x.dtype)

def _layernorm(x, g, b):
    xf = x.astype(jnp.float32)
    mu = jnp.mean(xf, axis=-1, keepdims=True)
    var = jnp.mean(jnp.square(xf - mu), axis=-1, keepdims=True)
    y = (xf - mu) * lax.rsqrt(var + LN_EPS) * g.astype(jnp.float32) + b.astype(jnp.float32)
    return y.astype(x.dtype)

def _rope_2d(t_len):
    t = jnp.arange(t_len)
    row = (t // GRID_W).astype(jnp.float32)
    col = (t % GRID_W).astype(jnp.float32)
    n = HEAD_DIM // 4
    freqs = ROPE_THETA ** (-jnp.arange(n, dtype=jnp.float32) / n)
    ang = jnp.concatenate([row[:, None] * freqs, col[:, None] * freqs], axis=-1)
    return jnp.cos(ang), jnp.sin(ang)

def _apply_rope(x, cos, sin):
    shape = (1, x.shape[1]) + (1,) * (x.ndim - 3) + (HEAD_DIM // 2,)
    c = cos.reshape(shape)
    s = sin.reshape(shape)
    xf = x.astype(jnp.float32).reshape(x.shape[:-1] + (HEAD_DIM // 2, 2))
    x1, x2 = xf[..., 0], xf[..., 1]
    out = jnp.stack([x1 * c - x2 * s, x1 * s + x2 * c], axis=-1).reshape(x.shape)
    return out.astype(x.dtype)

def _diff_lambda(lam_l, layer):
    lam_init = 0.8 - 0.6 * math.exp(-0.3 * layer)
    lf = lam_l.astype(jnp.float32)
    lam_v = jnp.exp(jnp.sum(lf[0] * lf[1])) - jnp.exp(jnp.sum(lf[2] * lf[3])) + lam_init
    return lam_v, lam_init

def _diff_attend(q, k, v, lam_v):
    s = jnp.einsum('bqmhd,bkmhd->bmhqk', q, k, preferred_element_type=jnp.float32) * (HEAD_DIM ** -0.5)
    p = jax.nn.softmax(s, axis=-1)
    a = p[:, 0] - lam_v * p[:, 1]
    return jnp.einsum('bhqk,bkhe->bqhe', a.astype(v.dtype), v)

def _diff_out(o, subln_w, lam_init):
    b, t = o.shape[0], o.shape[1]
    return (_rms(o, subln_w) * (1.0 - lam_init)).reshape(b, t, BRANCH_W)

def _mha_attend(q, k, v):
    s = jnp.einsum('bqhd,bkhd->bhqk', q, k, preferred_element_type=jnp.float32) * (HEAD_DIM ** -0.5)
    p = jax.nn.softmax(s, axis=-1)
    return jnp.einsum('bhqk,bkhd->bqhd', p.astype(v.dtype), v)

def _gqa_attend(q, k, v):
    s = jnp.einsum('bqngd,bknd->bngqk', q, k, preferred_element_type=jnp.float32) * (HEAD_DIM ** -0.5)
    p = jax.nn.softmax(s, axis=-1)
    return jnp.einsum('bngqk,bknd->bqngd', p.astype(v.dtype), v)

def _blockwise(fn, q):
    b, t = q.shape[0], q.shape[1]
    nb = t // Q_BLOCK
    qb = jnp.moveaxis(q.reshape((b, nb, Q_BLOCK) + q.shape[2:]), 1, 0)
    o = jnp.moveaxis(lax.map(fn, qb), 0, 1)
    return o.reshape((b, t) + o.shape[3:])

def _neighbourhood_attend(q, k_lat, v_lat, k_ctx, v_ctx, rpb_l):
    b, t, h, d = q.shape
    rows = t // GRID_W
    kh = min(NA_KH, rows)
    r = jnp.arange(rows)
    row_start = jnp.clip(r - kh // 2, 0, rows - kh)
    row_keys = row_start[:, None] + jnp.arange(kh)[None, :]
    dy = row_keys - r[:, None]
    cidx = jnp.arange(GRID_W)
    col_start = jnp.clip(cidx - NA_KW // 2, 0, GRID_W - NA_KW)
    col_keys = col_start[:, None] + jnp.arange(NA_KW)[None, :]
    dx = col_keys - cidx[:, None]
    n_loc = kh * NA_KW
    scale = HEAD_DIM ** -0.5
    q_rows = jnp.moveaxis(q.reshape(b, rows, GRID_W, h, d), 1, 0)

    def row_body(args):
        q_r, rk, dy_r = args
        idx = (rk[None, :, None] * GRID_W + col_keys[:, None, :]).reshape(GRID_W, n_loc)
        k_sel = k_lat[:, idx]
        v_sel = v_lat[:, idx]
        bias = rpb_l[:, dy_r[None, :, None] + (NA_KH - 1), dx[:, None, :] + (NA_KW - 1)]
        bias = bias.reshape(h, GRID_W, n_loc).astype(jnp.float32)
        s_loc = jnp.einsum('bqhd,bqkhd->bhqk', q_r, k_sel, preferred_element_type=jnp.float32) * scale + bias[None]
        s_ctx = jnp.einsum('bqhd,bkhd->bhqk', q_r, k_ctx, preferred_element_type=jnp.float32) * scale
        p = jax.nn.softmax(jnp.concatenate([s_loc, s_ctx], axis=-1), axis=-1).astype(v_lat.dtype)
        return (jnp.einsum('bhqk,bqkhd->bqhd', p[..., :n_loc], v_sel)
                + jnp.einsum('bhqk,bkhd->bqhd', p[..., n_loc:], v_ctx))

    o = lax.map(row_body, (q_rows, row_keys, dy))
    return jnp.moveaxis(o, 0, 1).reshape(b, t, h, d)

def _moe(h, w_router, router_bias, w1, w3, w2):
    shp = h.shape
    xt = h.reshape(-1, D_MODEL)
    scores = jax.nn.sigmoid(jnp.dot(xt, w_router, preferred_element_type=jnp.float32))
    sel = scores + router_bias.astype(jnp.float32)
    gscore = jnp.sum(lax.top_k(sel.reshape(-1, N_GROUPS, EXPERTS_PER_GROUP), TOP_K)[0], axis=-1)
    best = jnp.argmax(gscore, axis=-1)
    gmask = jnp.arange(N_GROUPS)[None, :] == best[:, None]
    emask = jnp.repeat(gmask, EXPERTS_PER_GROUP, axis=-1)
    _, idx = lax.top_k(jnp.where(emask, sel, -jnp.inf), TOP_K)
    wts = jnp.take_along_axis(scores, idx, axis=-1)
    wts = wts / jnp.sum(wts, axis=-1, keepdims=True)
    comb = jnp.sum(jax.nn.one_hot(idx, N_EXPERTS, dtype=jnp.float32) * wts[..., None], axis=-2)
    out = jnp.zeros(xt.shape, jnp.float32)
    for e in range(N_EXPERTS):
        he = jax.nn.silu(xt @ w1[e]) * (xt @ w3[e])
        out = out + comb[:, e:e + 1] * (he @ w2[e]).astype(jnp.float32)
    return out.astype(h.dtype).reshape(shp)

def _open_layer(x, cvec, w_mod_l, b_mod_l, w_in_l, c_qnorm_l, c_knorm_l):
    mod = jax.nn.silu(cvec) @ w_mod_l + b_mod_l
    sh1, sc1, g1, sh2, sc2, g2 = jnp.split(mod, 6, axis=-1)
    h = x * (1.0 + sc1) + sh1
    b, t = x.shape[0], x.shape[1]
    qa, ka, va, qb, kb, vb, qc, kc, vc = jnp.split(h @ w_in_l, _in_offsets(), axis=-1)
    qa = qa.reshape(b, t, 2, H_A, HEAD_DIM)
    ka = ka.reshape(b, t, 2, H_A, HEAD_DIM)
    va = va.reshape(b, t, H_A, 2 * HEAD_DIM)
    qb = qb.reshape(b, t, H_B, HEAD_DIM)
    kb = kb.reshape(b, t, H_B, HEAD_DIM)
    vb = vb.reshape(b, t, H_B, HEAD_DIM)
    qc = _rms(qc.reshape(b, t, KV_C, H_C // KV_C, HEAD_DIM), c_qnorm_l)
    kc = _rms(kc.reshape(b, t, KV_C, HEAD_DIM), c_knorm_l)
    vc = vc.reshape(b, t, KV_C, HEAD_DIM)
    return h, (g1, sh2, sc2, g2), (qa, ka, va, qb, kb, vb, qc, kc, vc)

def _close_layer(x, h, mods, oa, ob, oc, alpha, w_gate_l, b_gate_l, w_br_l, w_o_l, ln_g_l, ln_b_l,
                 w_router, router_bias, moe_w1_l, moe_w3_l, moe_w2_l):
    g1, sh2, sc2, g2 = mods
    ga, gb, gc = jnp.split(jax.nn.sigmoid(h @ w_gate_l + b_gate_l), N_BRANCH, axis=-1)
    y = (ga * (oa @ w_br_l[0]) + gb * (ob @ w_br_l[1]) + gc * (oc @ w_br_l[2])) @ w_o_l
    x = _layernorm(alpha * x + g1 * y, ln_g_l[0], ln_b_l[0])
    h2 = x * (1.0 + sc2) + sh2
    m = _moe(h2, w_router, router_bias, moe_w1_l, moe_w3_l, moe_w2_l)
    return _layernorm(alpha * x + g2 * m, ln_g_l[1], ln_b_l[1])

def _context_layer(x, c_ctx, layer, alpha, lw, w_router, router_bias):
    (w_mod_l, b_mod_l, w_in_l, w_gate_l, b_gate_l, lam_l, a_subln_l, rpb_l, c_qnorm_l, c_knorm_l,
     w_br_l, w_o_l, ln_g_l, ln_b_l, moe_w1_l, moe_w3_l, moe_w2_l) = lw
    b, t = x.shape[0], x.shape[1]
    h, mods, (qa, ka, va, qb, kb, vb, qc, kc, vc) = _open_layer(
        x, c_ctx[None, None, :], w_mod_l, b_mod_l, w_in_l, c_qnorm_l, c_knorm_l)
    lam_v, lam_init = _diff_lambda(lam_l, layer)
    oa = _diff_out(_diff_attend(qa, ka, va, lam_v), a_subln_l, lam_init)
    ob = _mha_attend(qb, kb, vb).reshape(b, t, BRANCH_W)
    oc = _gqa_attend(qc, kc, vc).reshape(b, t, BRANCH_W)
    x = _close_layer(x, h, mods, oa, ob, oc, alpha, w_gate_l, b_gate_l, w_br_l, w_o_l, ln_g_l, ln_b_l,
                     w_router, router_bias, moe_w1_l, moe_w3_l, moe_w2_l)
    return x, (ka, va, kb, vb, kc, vc)

def _latent_layer(x, c, layer, alpha, ctx_kv, cos, sin, lw, w_router, router_bias):
    (w_mod_l, b_mod_l, w_in_l, w_gate_l, b_gate_l, lam_l, a_subln_l, rpb_l, c_qnorm_l, c_knorm_l,
     w_br_l, w_o_l, ln_g_l, ln_b_l, moe_w1_l, moe_w3_l, moe_w2_l) = lw
    ck_a, cv_a, ck_b, cv_b, ck_c, cv_c = ctx_kv
    b, t = x.shape[0], x.shape[1]
    h, mods, (qa, ka, va, qb, kb, vb, qc, kc, vc) = _open_layer(
        x, c[:, None, :], w_mod_l, b_mod_l, w_in_l, c_qnorm_l, c_knorm_l)
    qa = _apply_rope(qa, cos, sin)
    ka = _apply_rope(ka, cos, sin)
    qc = _apply_rope(qc, cos, sin)
    kc = _apply_rope(kc, cos, sin)
    lam_v, lam_init = _diff_lambda(lam_l, layer)
    k_all_a = jnp.concatenate([ck_a, ka], axis=1)
    v_all_a = jnp.concatenate([cv_a, va], axis=1)
    oa = _blockwise(lambda qq: _diff_attend(qq, k_all_a, v_all_a, lam_v), qa)
    oa = _diff_out(oa, a_subln_l, lam_init)
    ob = _neighbourhood_attend(qb, kb, vb, ck_b, cv_b, rpb_l).reshape(b, t, BRANCH_W)
    k_all_c = jnp.concatenate([ck_c, kc], axis=1)
    v_all_c = jnp.concatenate([cv_c, vc], axis=1)
    oc = _blockwise(lambda qq: _gqa_attend(qq, k_all_c, v_all_c), qc).reshape(b, t, BRANCH_W)
    return _close_layer(x, h, mods, oa, ob, oc, alpha, w_gate_l, b_gate_l, w_br_l, w_o_l, ln_g_l, ln_b_l,
                        w_router, router_bias, moe_w1_l, moe_w3_l, moe_w2_l)

def setup_inputs(seed: int = 0) -> dict:
    key = jax.random.key(seed)
    ks = jax.random.split(key, 32)
    f32 = jnp.float32
    beta = (8.0 * DEPTH) ** -0.25
    dm = D_MODEL ** -0.5

    def nrm(k, shape, s):
        return jax.random.normal(k, shape, f32) * s

    kin = jax.random.split(ks[12], len(IN_SPLITS))
    w_in = jnp.concatenate(
        [nrm(kin[i], (DEPTH, D_MODEL, s), dm * (beta if i in V_PIECES else 1.0)) for i, s in enumerate(IN_SPLITS)],
        axis=-1)
    return {
        'x_prompt': nrm(ks[0], (BATCH, SEQ, D_MODEL), 1.0),
        'x_sample': nrm(ks[1], (DEC_BATCH, DEC_SEQ, D_MODEL), 1.0),
        'c': nrm(ks[2], (DEC_BATCH, D_MODEL), 1.0),
        'cache_a_k': nrm(ks[3], (DEC_BATCH, DEPTH, PAST_LEN, 2, H_A, HEAD_DIM), 1.0),
        'cache_a_v': nrm(ks[4], (DEC_BATCH, DEPTH, PAST_LEN, H_A, 2 * HEAD_DIM), beta),
        'cache_b_k': nrm(ks[5], (DEC_BATCH, DEPTH, PAST_LEN, H_B, HEAD_DIM), 1.0),
        'cache_b_v': nrm(ks[6], (DEC_BATCH, DEPTH, PAST_LEN, H_B, HEAD_DIM), beta),
        'cache_c_k': nrm(ks[7], (DEC_BATCH, DEPTH, PAST_LEN, KV_C, HEAD_DIM), 1.0),
        'cache_c_v': nrm(ks[8], (DEC_BATCH, DEPTH, PAST_LEN, KV_C, HEAD_DIM), beta),
        'c_ctx': nrm(ks[9], (D_MODEL,), 1.0),
        'w_mod': nrm(ks[10], (DEPTH, D_MODEL, 6 * D_MODEL), 0.5 * dm),
        'b_mod': nrm(ks[11], (DEPTH, 6 * D_MODEL), 0.01),
        'w_in': w_in,
        'w_gate': nrm(ks[13], (DEPTH, D_MODEL, N_BRANCH * D_MODEL), dm),
        'b_gate': nrm(ks[14], (DEPTH, N_BRANCH * D_MODEL), 0.01),
        'lam': nrm(ks[15], (DEPTH, 4, HEAD_DIM), 0.1),
        'a_subln': 1.0 + nrm(ks[16], (DEPTH, 2 * HEAD_DIM), 0.01),
        'rpb': nrm(ks[17], (DEPTH, H_B, 2 * NA_KH - 1, 2 * NA_KW - 1), 0.02),
        'c_qnorm': 1.0 + nrm(ks[18], (DEPTH, HEAD_DIM), 0.01),
        'c_knorm': 1.0 + nrm(ks[19], (DEPTH, HEAD_DIM), 0.01),
        'w_br': nrm(ks[20], (DEPTH, N_BRANCH, BRANCH_W, D_MODEL), BRANCH_W ** -0.5 * beta),
        'w_o': nrm(ks[21], (DEPTH, D_MODEL, D_MODEL), dm * beta),
        'ln_g': 1.0 + nrm(ks[22], (DEPTH, 2, D_MODEL), 0.01),
        'ln_b': nrm(ks[23], (DEPTH, 2, D_MODEL), 0.01),
        'w_router': nrm(ks[24], (D_MODEL, N_EXPERTS), dm),
        'router_bias': nrm(ks[25], (N_EXPERTS,), 0.01),
        'moe_w1': nrm(ks[26], (DEPTH, N_EXPERTS, D_MODEL, D_EXPERT), dm),
        'moe_w3': nrm(ks[27], (DEPTH, N_EXPERTS, D_MODEL, D_EXPERT), dm * beta),
        'moe_w2': nrm(ks[28], (DEPTH, N_EXPERTS, D_EXPERT, D_MODEL), D_EXPERT ** -0.5 * beta),
    }

def reference(x_prompt, x_sample, c, cache_a_k, cache_a_v, cache_b_k, cache_b_v, cache_c_k, cache_c_v,
              c_ctx, w_mod, b_mod, w_in, w_gate, b_gate, lam, a_subln, rpb, c_qnorm, c_knorm,
              w_br, w_o, ln_g, ln_b, w_router, router_bias, moe_w1, moe_w3, moe_w2):
    alpha = (2.0 * DEPTH) ** 0.25

    def layer_weights(l):
        return (w_mod[l], b_mod[l], w_in[l], w_gate[l], b_gate[l], lam[l], a_subln[l], rpb[l],
                c_qnorm[l], c_knorm[l], w_br[l], w_o[l], ln_g[l], ln_b[l], moe_w1[l], moe_w3[l], moe_w2[l])

    y_prompt = x_prompt
    ctx = []
    for l in range(DEPTH):
        y_prompt, kv = _context_layer(y_prompt, c_ctx, l, alpha, layer_weights(l), w_router, router_bias)
        ctx.append(kv)
    new_a_k = jnp.stack([kv[0] for kv in ctx], axis=1)
    new_a_v = jnp.stack([kv[1] for kv in ctx], axis=1)
    new_b_k = jnp.stack([kv[2] for kv in ctx], axis=1)
    new_b_v = jnp.stack([kv[3] for kv in ctx], axis=1)
    new_c_k = jnp.stack([kv[4] for kv in ctx], axis=1)
    new_c_v = jnp.stack([kv[5] for kv in ctx], axis=1)

    cos, sin = _rope_2d(x_sample.shape[1])
    y_sample = x_sample
    for l in range(DEPTH):
        ctx_kv = (cache_a_k[:, l], cache_a_v[:, l], cache_b_k[:, l], cache_b_v[:, l],
                  cache_c_k[:, l], cache_c_v[:, l])
        y_sample = _latent_layer(y_sample, c, l, alpha, ctx_kv, cos, sin, layer_weights(l),
                                 w_router, router_bias)

    return (y_prompt, y_sample, new_a_k, new_a_v, new_b_k, new_b_v, new_c_k, new_c_v)


_drawn_inputs = setup_inputs


def setup_inputs(seed=0):
    import zlib

    import numpy as np

    out = dict(_drawn_inputs(seed))
    spreads = {}
    factors = {'cache_a_k': 8.0,
     'cache_a_v': 8.0,
     'cache_b_k': 8.0,
     'cache_b_v': 8.0,
     'cache_c_k': 8.0,
     'cache_c_v': 8.0,
     'b_mod': 4.188,
     'w_gate': 4.265,
     'b_gate': 32.91,
     'lam': 8.0,
     'a_subln': 42.536,
     'rpb': 64.0,
     'c_qnorm': 29.158,
     'c_knorm': 33.422,
     'ln_g': 2.762,
     'ln_b': 2.714,
     'router_bias': 4.624}
    for name, (base, spread) in spreads.items():
        noise = np.random.default_rng([zlib.crc32(name.encode()), seed]).standard_normal(out[name].shape)
        drawn = base * np.exp(spread * noise) if base else spread * noise
        out[name] = __import__('jax').numpy.asarray(drawn.astype(out[name].dtype))
    for name, factor in factors.items():
        out[name] = (out[name] * factor).astype(out[name].dtype)
    return out
```

```python
import math
import numpy as np
import concourse.bass as bass
from concourse import mybir
from contextlib import ExitStack

D = 1024
KB = D // 128
DEPTH = 2
LAT = 4
NT = LAT + 1
CTX = LAT
TOK = NT * 128
LTOK = LAT * 128
HD = 64
NE = 16
DE = 256
GRID_W, ROWS, NA_KW, NA_KH = 64, 8, 16, 8
GW = GRID_W // LAT
LN_EPS, RMS_EPS = 1e-5, 1e-6
ALPHA = (2.0 * DEPTH) ** 0.25
SLOTS = 6
PIECE = 2048
FAR = -1e30

MOD_FIRST, MOD_LATER = (0, 1, 2, 3), (4, 5, 6, 7, 8, 9, 10, 11)
CHUNKS = {0: (0, 1, 2), 1: (3, 4, 5), 2: (6, 7)}
CHUNK_TYPE = ("q", "k", "v", "q", "k", "v", "q", "kv")


def piece_order():
    order = []
    for cg in MOD_FIRST:
        order += [("mod", cg, 0), ("mod", cg, 1)]
    for br in range(3):
        for c in CHUNKS[br]:
            order += [("mod", MOD_LATER[c], 0), ("mod", MOD_LATER[c], 1)]
            order += [("in", c, 0)] + [("in", c, 1)] * (c < 7)
        for mg in range(2):
            order += [("gate", br, 2 * mg), ("gate", br, 2 * mg + 1), ("br", br, mg)]
    order += [("o", n, h) for n in range(2) for h in range(2)]
    for e in range(NE):
        order += [("w1", e), ("w3", e), ("w2", e)]
    return order


PIECES = piece_order()
NP = len(PIECES)


def key_tiles(br, r):
    return list(range(max(r - 1, 0), min(r + 2, LAT))) if br == 1 else list(range(LAT))


def units(br):
    if br == 0:
        return [("lat", h) for h in range(4)] + [("ctx", 0)]
    return [("lat", h) for h in range(8)] + [("ctx", 0), ("ctx", 1)]


def key_steps(br, u):
    if u[0] == "ctx":
        return [(CTX, 0, 4)]
    steps = [(5, 0, LAT)]
    for kt in range(LAT):
        rs = [r for r in range(LAT) if kt in key_tiles(br, r)]
        steps.append((kt, rs[0], rs[-1] + 1))
    return steps


def build_kernel(nc, A, OUT):
    f32 = mybir.dt.float32
    ALU, ACT, AX = mybir.AluOpType, mybir.ActivationFunctionType, mybir.AxisListType
    ctx = ExitStack()

    def sb(name, shape):
        return ctx.enter_context(nc.sbuf_tensor(name, shape, f32))

    sems = []

    def sem(name):
        s = ctx.enter_context(nc.semaphore(name))
        sems.append(s)
        return s

    with ctx:
        ring = sb("ring", [128, SLOTS, PIECE])
        hT = sb("hT", [128, KB, TOK])
        zT = sb("zT", [128, KB, TOK])
        ident = sb("ident", [128, 128])
        sel = sb("sel", [128, 2])
        cosT = sb("cosT", [128, LAT, HD])
        sinT = sb("sinT", [128, LAT, HD])
        mask = sb("mask", [128, LAT, 3 * GW])
        cs = sb("cs", [128, KB, 32])
        half = sb("half", [128, 16])
        wr = sb("wr", [128, KB, NE])
        rbias = sb("rbias", [128, NE])
        eidx = sb("eidx", [128, NE])
        par = sb("par", [128, 48 + 24 + 128 + 64 + 64 + 256 + 2])
        bmod, bgate = par[:, 0:48], par[:, 48:72]
        subln, qnw, knw = par[:, 72:200], par[:, 200:264], par[:, 264:328]
        lam, laminit = par[:, 328:584], par[:, 584:586]
        nlam = sb("nlam", [128, 1])
        modcol = sb("modcol", [128, 48, 2])
        graw = sb("graw", [128, 4, 512])
        nmax = sb("nmax", [128, 16])
        rsum = sb("rsum", [128, 16])
        rinv = sb("rinv", [128, 16])
        small = sb("small", [128, 64])
        comb = sb("comb", [128, NT, NE])

        R = sb("R", [128, 25984])

        def area(start, size):
            return R[:, start:start + size]

        QT = area(0, 2560).rearrange("p (b t) -> p b t", b=4)
        KT = area(2560, 6144).rearrange("p (s t) -> p s t", s=8)
        V = area(8704, 3072).rearrange("p (t e) -> p t e", t=6)
        oT = area(11776, 2560).rearrange("p (b t) -> p b t", b=4)
        P = area(14336, 5120).rearrange("p (s r k) -> p s r k", s=2, r=4)
        PT = area(19456, 1536).rearrange("p (s k) -> p s k", s=3)
        P1 = area(20992, 1280).rearrange("p (s k) -> p s k", s=2)
        MB = area(20992, 2560).rearrange("p (s k) -> p s k", s=2)
        WB = area(23552, 384).rearrange("p (r u) -> p r u", r=ROWS)
        tok = area(23936, 1024).rearrange("p (s k) -> p s k", s=2)
        tmpA, tmpB = area(24960, 512), area(25472, 512)
        sg = area(14336, 1280).rearrange("p (s k) -> p s k", s=2)
        prod = area(15616, 640)
        x = area(0, 5120).rearrange("p (t n) -> p t n", t=NT)
        rows = area(5120, 6144).rearrange("p (a n) -> p a n", a=6)
        G2 = area(11776, 2048).rearrange("p (v n) -> p v n", v=2)
        acc = area(14336, 5120).rearrange("p (t n) -> p t n", t=NT)
        G1 = area(19456, 2048).rearrange("p (v n) -> p v n", v=2)
        lnst = area(21504, 128)
        route = area(21632, 12 * NT * NE).rearrange("p (a t e) -> p a t e", a=12, t=NT)
        modraw = area(19456, 512)
        he = zT[:, 0:4, :].rearrange("p (s m) t -> p s m t", s=2)
        sig = zT[:, 4:8, :]

        ps = ctx.enter_context(nc.psum_tensor("ps", [128, 8, 512], f32))

        def flat(bank, n):
            return ps[:, bank:bank + 2, :].rearrange("p b n -> p (b n)")[:, 0:n]

        full = [sem(f"piece_loaded_{s}") for s in range(SLOTS)]
        freed = sem("pieces_used")
        consts_in = sem("constants_loaded")
        par_in = sem("layer_parameters_loaded")
        cache_k_in, cache_v_in = sem("cache_k_loaded"), sem("cache_v_loaded")
        bias_in = sem("bias_loaded")
        x_in, rows_in = sem("x_loaded"), sem("rows_loaded")
        x_out, new_k_out, new_v_out = sem("x_stored"), sem("new_k_stored"), sem("new_v_stored")
        pe_mod, pe_ext = sem("mod_rows_summed"), sem("mod_columns_summed")
        pe_xT, pe_acc, pe_tp = sem("x_transposed"), sem("projected"), sem("qk_transposed")
        pe_score, pe_pt, pe_pv = sem("scores_ready"), sem("probs_transposed"), sem("values_mixed")
        pe_at = sem("diff_out_transposed")
        pe_gate, pe_br, pe_gb, pe_y = sem("gate_ready"), sem("branch_ready"), sem("gate_rows_ready"), sem("y_ready")
        pe_rt, pe_h, pe_e = sem("router_ready"), sem("hidden_ready"), sem("expert_ready")
        a_chain, v_chain, g_chain = sem("act_chain"), sem("dve_chain"), sem("pool_chain")
        a_mod, a_hT, a_copy, a_qk = sem("mod_rows_kept"), sem("hT_ready"), sem("unit_copied"), sem("qk_kept")
        a_exp, a_pt, a_oT, a_sg = sem("exp_ready"), sem("probsT_kept"), sem("diff_oT_kept"), sem("sigmoid_ready")
        a_rt, a_esg = sem("router_sigmoid"), sem("expert_sigmoid")
        v_mod, v_unit, v_bias, v_max = sem("mod_columns_ready"), sem("unit_normed"), sem("bias_added"), sem("max_ready")
        v_rinv, v_diff, v_oev, v_anorm = sem("rinv_ready"), sem("diff_probs_ready"), sem("o_kept"), sem("diff_out_normed")
        v_sq, v_z, v_G, v_ln = sem("squares_summed"), sem("z_ready"), sem("gate_rows_kept"), sem("x_normed")
        v_lnv, v_he, v_ye, v_comb = sem("variance_ready"), sem("expert_hidden_kept"), sem("expert_added"), sem("comb_ready")
        v_lam, v_x = sem("lambda_dots"), sem("x_final")
        a_lam = sem("lambda_exps")
        g_rs, g_prow, g_mb, g_zero = sem("rstd_ready"), sem("probs_scaled"), sem("bias_masked"), sem("kT_zeroed")
        all_sems = range(sems[0].num, sems[-1].num + 1)

        class Chain:

            def __init__(self, eng):
                self.eng, self.n = eng, {}

            def step(self, ins, s, wait=True):
                ins.then_inc(s, 1)
                self.n[s.num] = self.n.get(s.num, 0) + 1
                if wait:
                    self.eng.wait_ge(s, self.n[s.num])

            def count(self, s):
                return self.n.get(s.num, 0)

        PU = [(br, c, t) for br in range(3) for c in CHUNKS[br] for t in range(NT)]
        QU = [i for i, (br, c, t) in enumerate(PU) if CHUNK_TYPE[c] != "v"]

        def by_dve(c, t):
            return c in (6, 7) or (c in (0, 1) and t < LAT)

        DU = [i for i, (br, c, t) in enumerate(PU) if by_dve(c, t)]
        AU = [i for i, (br, c, t) in enumerate(PU) if not by_dve(c, t) or c == 7]
        CG_ORDER = list(MOD_FIRST) + list(MOD_LATER)

        def copies(n):
            return sum(1 if CHUNK_TYPE[PU[QU[j]][1]] == "q" else 2 for j in range(n))

        NEW_K = [i for i, (br, c, t) in enumerate(PU) if t == CTX and CHUNK_TYPE[c] in ("k", "kv")]
        NEW = [i for i, (br, c, t) in enumerate(PU) if t == CTX and CHUNK_TYPE[c] in ("k", "v", "kv")]

        UN = [(br, i, u) for br in range(3) for i, u in enumerate(units(br))]
        FIRST_UNIT = [0, 5, 15, 25]
        RW = [(g, r) for g in range(len(UN)) for r in range(4)]
        SC = [(g, r, m) for g, r in RW for m in range(2 if UN[g][0] == 0 else 1)]
        BIAS = [(g, r) for g, r in RW if UN[g][0] == 1 and UN[g][2][0] == "lat"]
        KS = [(g, j) for g in range(len(UN)) for j in range(len(key_steps(UN[g][0], UN[g][2])))]
        sc_at = {k: i for i, k in enumerate(SC)}
        ks_at = {k: i for i, k in enumerate(KS)}
        rw_at = {k: i for i, k in enumerate(RW)}
        bias_at = {k: i for i, k in enumerate(BIAS)}

        def last_ks(g):
            return ks_at[(g, len(key_steps(UN[g][0], UN[g][2])) - 1)]

        def width(br, u, r):
            return 128 if u[0] == "ctx" else 128 * (len(key_tiles(br, r)) + 1)

        def tile_at(br, u, r, kt):
            if u[0] == "ctx":
                return 0
            tiles = key_tiles(br, r)
            return len(tiles) if kt == 5 else kt - tiles[0]

        MB_AT = [0, 256, 640, 1024]

        G_CG = (4, 5, 10, 11)
        COL_CG = [cg for cg in CG_ORDER if cg not in G_CG]
        N_UNITS = len(UN)

        G_CG = (4, 5, 10, 11)
        COL_CG = [cg for cg in CG_ORDER if cg not in G_CG]
        N_UNITS = len(UN)

        with nc.Block() as block:
            names = [("ident", ident), ("sel", sel), ("cosT", cosT), ("sinT", sinT),
                     ("mask", mask), ("wr", wr), ("rbias", rbias), ("eidx", eidx)]

            @block.sync
            def _(sp):
                sp.dma_start(cs[:], A["cs"]).then_inc(par_in, 16)
                sp.dma_start(x[:], A["x"].rearrange("t p n -> p t n")).then_inc(x_in, 16)
                for n, t in names:
                    sp.dma_start(t[:], A[n]).then_inc(consts_in, 16)
                sp.wait_ge(x_in, 16)
                sp.wait_ge(consts_in, 16 * len(names))

            @block.gpsimd
            def _(pool):
                nc.gpsimd.memset(half[:], -0.5).then_inc(g_rs, 1)

            @block.scalar
            def _(act):
                act.wait_ge(par_in, 16)
                nc.scalar.activation(hT[:, :, 0:32], cs[:], ACT.Sigmoid).then_inc(a_sg, 1)

            @block.vector
            def _(dve):
                dve.wait_ge(par_in, 16)
                dve.wait_ge(a_sg, 1)
                nc.vector.tensor_tensor(cs[:], cs[:], hT[:, :, 0:32], ALU.mult).then_inc(v_z, 1)

        nc.all_engine_barrier(sems_to_clear=all_sems)

        with nc.Fori(0, DEPTH) as layer:
            with nc.Block() as block:

                @block.sync
                def _(sp):
                    for s in range(SLOTS):
                        sp.dma_start(ring[:, s, :], A["wall"][layer, s]).then_inc(full[s], 16)
                    groups = NP // SLOTS
                    with sp.Fori(1, groups) as g:
                        for s in range(SLOTS):
                            sp.wait_ge(freed, (g - 1) * SLOTS + s + 1)
                            sp.dma_start(ring[:, s, :], A["wall"][layer, g * SLOTS + s]).then_inc(full[s], 16)
                    for i in range(groups * SLOTS, NP):
                        sp.wait_ge(freed, i - SLOTS + 1)
                        sp.dma_start(ring[:, i % SLOTS, :], A["wall"][layer, i]).then_inc(full[i % SLOTS], 16)
                    for i in range(NP - SLOTS, NP):
                        sp.wait_ge(full[i % SLOTS], 16 * (i // SLOTS + 1))

                @block.gpsimd
                def _(pool):
                    ch = Chain(pool)
                    pool.dma_start(par[:], A["par"][layer]).then_inc(par_in, 16)
                    pool.dma_start(A["x_state"].rearrange("t p n -> p t n"), x[:]).then_inc(x_out, 16)
                    pool.wait_ge(pe_xT, KB)
                    pool.wait_ge(x_out, 16)
                    for lo, par_ in ((0, 1), (64, 0)):
                        for sl in range(par_, 8, 2):
                            ch.step(nc.gpsimd.memset(KT[lo:lo + 64, sl, 0:640], 0.0), g_zero)

                    def powers(dst, src):
                        ch.step(nc.gpsimd.tensor_tensor(dst, src, half[:, 0:dst.shape[1]], ALU.pow), g_rs)

                    def masked_bias(h):
                        pool.wait_ge(bias_in, 16 * (h + 1))
                        if h >= 2:
                            pool.wait_ge(v_bias, 4 * (h - 1))
                        for g in range(LAT):
                            tiles = key_tiles(1, g)
                            n, u0 = len(tiles), GW * (tiles[0] - g + 1)
                            o = MB[:, h % 2, MB_AT[g]:MB_AT[g] + 128 * n].rearrange("p (k r c) -> p k r c", k=n, r=ROWS)
                            w = WB[:, :, u0:u0 + GW * n].rearrange("p r (k c) -> p k r c", c=GW)
                            m = mask[:, g, u0:u0 + GW * n].rearrange("p (k c) -> p k c", c=GW).unsqueeze(2).to_broadcast([128, n, ROWS, GW])
                            ch.step(nc.gpsimd.tensor_tensor(o, w, m, ALU.add), g_mb)

                    for br in range(3):
                        ns, vw = (8, 512) if br < 2 else (4, 128)
                        if br:
                            pool.wait_ge(pe_pv, last_ks(FIRST_UNIT[br] - 1) + 1)
                        pool.dma_start(KT[:, 0:ns, 640:768], A["cache_kT"][layer, br][:, 0:ns, :]).then_inc(cache_k_in, 16)
                        pool.dma_start(V[:, 5, 0:vw], A["cache_v"][layer, br][:, 0:vw]).then_inc(cache_v_in, 16)
                        if br == 1:
                            pool.wait_ge(v_diff, 4 * FIRST_UNIT[1])
                            pool.dma_start(WB[:], A["bias"][layer, 0]).then_inc(bias_in, 16)
                            masked_bias(0)
                            pool.dma_start(WB[:], A["bias"][layer, 1]).then_inc(bias_in, 16)
                        for c in CHUNKS[br]:
                            if c in (6, 7):
                                for t in range(NT):
                                    pool.wait_ge(v_sq, 5 + 5 * (c - 6) + t + 1)
                                    nh = 8 if c == 6 else 2
                                    powers(small[:, 8:8 + nh], small[:, 0:nh])
                            i = PU.index((br, c, CTX))
                            typ = CHUNK_TYPE[c]
                            if typ in ("k", "kv"):
                                q = QU.index(i)
                                if i in DU:
                                    pool.wait_ge(v_unit, DU.index(i) + 1)
                                else:
                                    pool.wait_ge(a_copy, AU.index(i) + 1)
                                if typ == "k":
                                    pool.dma_start(OUT[("ak", "bk")[br]][layer], tok[:, q % 2, 0:512]).then_inc(new_k_out, 16)
                                else:
                                    pool.dma_start(OUT["ck"][layer].rearrange("t (h d) -> t h d", h=2),
                                                   tok[:, q % 2, 0:256].rearrange("p (h a d) -> p h a d", h=2, a=2)[:, :, 0, :]).then_inc(new_k_out, 16)
                                pool.wait_ge(new_k_out, 16 * (br + 1))
                            if typ in ("v", "kv"):
                                pool.wait_ge(a_copy, AU.index(i) + 1)
                                pool.dma_start(OUT[("av", "bv", "cv")[br]][layer], V[:, CTX, 0:vw]).then_inc(new_v_out, 16)
                                pool.wait_ge(new_v_out, 16 * (br + 1))
                        n = len(units(br))
                        for ui in range(n + 2):
                            if br == 0 and ui >= 2:
                                pool.wait_ge(v_sq, ui - 1)
                                powers(small[:, 8:12], small[:, 0:4])
                            if ui < n and br:
                                g, u = FIRST_UNIT[br] + ui, units(br)[ui]
                                if br == 1 and ui < 7:
                                    masked_bias(ui + 1)
                                    if ui < 6:
                                        pool.dma_start(WB[:], A["bias"][layer, ui + 2]).then_inc(bias_in, 16)
                                for r in range(4):
                                    si = sc_at[(g, r, 0)]
                                    pool.wait_ge(v_rinv, si + 1)
                                    w = width(br, u, r)
                                    ch.step(nc.gpsimd.tensor_scalar(P[:, g % 2, r, 0:w], P[:, g % 2, r, 0:w],
                                                                    rinv[:, si % 16:si % 16 + 1], None, ALU.mult), g_prow)
                    pool.wait_ge(pe_gate, 2 * KB + 1)
                    pool.dma_start(x[:], A["x_state"].rearrange("t p n -> p t n")).then_inc(x_in, 16)
                    pool.dma_start(rows[:], A["rows"][layer]).then_inc(rows_in, 16)
                    for k in range(2 * NT):
                        pool.wait_ge(v_lnv, k + 1)
                        o = 4 * (k % 2)
                        powers(small[:, 32 + o:33 + o], small[:, 34 + o:35 + o])
                    pool.wait_ge(par_in, 16)
                    for s in (cache_k_in, cache_v_in):
                        pool.wait_ge(s, 48)
                    pool.wait_ge(bias_in, 16 * 8)
                    pool.wait_ge(x_in, 16)
                    pool.wait_ge(rows_in, 16)
                    pool.dma_reset(all_sems)

                @block.tensor
                def _(pe):
                    piece, owed, waited = [0], [0], set()

                    def take(kind, j=0):
                        i = piece[0] + j
                        assert PIECES[i][0] == kind, (PIECES[i], kind)
                        if i not in waited:
                            waited.add(i)
                            pe.wait_ge(full[i % SLOTS], 16 * (i // SLOTS + 1))
                        return ring[:, i % SLOTS, :]

                    def used(n):
                        owed[0] += n
                        piece[0] += n

                    def mm(out, w, m, start, stop, frees=True, **kw):
                        ins = nc.tensor.matmul(out, w, m, start=start, stop=stop, **kw)
                        if frees and owed[0]:
                            owed[0] -= 1
                            ins.then_inc(freed, 1)
                        return ins

                    n_cg = [0]

                    def mod_sum(cg):
                        i = n_cg[0]
                        if i:
                            pe.wait_ge(a_mod, i)
                        if cg in MOD_LATER and MOD_LATER.index(cg) in (3, 6):
                            pe.wait_ge(v_oev, FIRST_UNIT[1 if MOD_LATER.index(cg) == 3 else 2])
                        for hf in range(2):
                            w = take("mod", hf).rearrange("p (k n) -> p k n", k=4)
                            for j in range(4):
                                last = mm(ps[32 * j:32 * j + 32, 6, :], cs[:, 4 * hf + j, :], w[:, j, :], hf == 0, hf == 1, frees=hf == 0)
                        last.then_inc(pe_mod, 1)
                        n_cg[0] += 1
                        used(2)

                    def mod_columns(cg):
                        if cg in G_CG:
                            return
                        pe.wait_ge(a_mod, n_cg[0])
                        k = COL_CG.index(cg)
                        if k:
                            pe.wait_ge(v_mod, k)
                        for b in range(4):
                            last = mm(ps[:, 7, 2 * b:2 * b + 2], modraw[:, 128 * b:128 * b + 128], sel[:, 0:2], True, True, frees=b < 3)
                        last.then_inc(pe_ext, 1)

                    for cg in MOD_FIRST:
                        mod_sum(cg)
                        mod_columns(cg)

                    def transpose_x(first):
                        for k in range(KB):
                            if k >= 2:
                                pe.wait_ge(a_hT, 2 * (first + k - 1))
                            for t in range(NT):
                                last = nc.tensor.transpose(ps[:, 2 * (k % 2) + (t == CTX), 128 * (t % LAT):128 * (t % LAT) + 128],
                                                           x[:, t, 128 * k:128 * k + 128], ident[:])
                            last.then_inc(pe_xT, 1)

                    transpose_x(0)
                    pe.wait_ge(a_hT, 2 * KB)

                    def transpose_unit(q):
                        br, c, t = PU[QU[q]]
                        if QU[q] in DU:
                            pe.wait_ge(v_unit, DU.index(QU[q]) + 1)
                        else:
                            pe.wait_ge(a_copy, AU.index(QU[q]) + 1)
                        if q >= 2:
                            pe.wait_ge(a_qk, copies(q - 1))
                        for b in range(2 if c == 7 else 4):
                            last = nc.tensor.transpose(ps[:, 4 + q % 2, 128 * b:128 * b + 128],
                                                       tok[:, q % 2, 128 * b:128 * b + 128], ident[:])
                        last.then_inc(pe_tp, 1)

                    def project(br):
                        if br:
                            pe.wait_ge(v_z, KB * br)
                        for c in CHUNKS[br]:
                            mod_sum(MOD_LATER[c])
                            for t in range(NT):
                                i = PU.index((br, c, t))
                                if i >= 4:
                                    if i - 4 in DU:
                                        pe.wait_ge(v_unit, DU.index(i - 4) + 1)
                                    if i - 4 in AU:
                                        pe.wait_ge(a_copy, AU.index(i - 4) + 1)
                                w = 512 if c < 7 else 256
                                for k in range(KB):
                                    if c < 7:
                                        wk = take("in", k // 4).rearrange("p (k n) -> p k n", k=4)[:, k % 4, :]
                                    else:
                                        wk = take("in").rearrange("p (k n) -> p k n", k=8)[:, k, :]
                                    last = mm(ps[:, i % 4, 0:w], hT[:, k, 128 * t:128 * t + 128], wk, k == 0, k == KB - 1, frees=k < KB - 1)
                                last.then_inc(pe_acc, 1)
                                if t == 0:
                                    mod_columns(MOD_LATER[c])
                                if i and i - 1 in QU and PU[i - 1][0] == br:
                                    transpose_unit(QU.index(i - 1))
                            used(2 if c < 7 else 1)
                        if i in QU:
                            transpose_unit(QU.index(i))

                    def scores(g, r):
                        br, ui, u = UN[g]
                        for m in range(2 if br == 0 else 1):
                            i = sc_at[(g, r, m)]
                            if i >= 2:
                                gg, rr, _ = SC[i - 2]
                                if (gg, rr) in bias_at:
                                    pe.wait_ge(v_bias, bias_at[(gg, rr)] + 1)
                                else:
                                    pe.wait_ge(a_exp, i - 1)
                            b = 2 * (i % 2)
                            hh = (u[1] if u[0] == "lat" else r + 4 * u[1]) + 4 * m
                            slot = hh if br < 2 else 2 * (hh // 4) + hh % 2
                            t = r if u[0] == "lat" else CTX
                            q = QT[:, hh // 2, 128 * t:128 * t + 128]
                            if u[0] == "ctx":
                                last = nc.tensor.matmul(ps[:, b, 0:128], q, KT[:, slot, 512:640], start=True, stop=True)
                            else:
                                tiles = key_tiles(br, r)
                                n = 128 * len(tiles)
                                nc.tensor.matmul(ps[:, b, 0:n], q, KT[:, slot, 128 * tiles[0]:128 * tiles[0] + n], start=True, stop=True)
                                last = nc.tensor.matmul(flat(b, 1024)[:, n:n + 128], q, KT[:, slot, 640:768], start=True, stop=True)
                            last.then_inc(pe_score, 1)

                    def transpose_probs(g, j):
                        br, ui, u = UN[g]
                        i = ks_at[(g, j)]
                        if j == 0:
                            if br == 0:
                                pe.wait_ge(v_diff, 4 * g + 4)
                            else:
                                pe.wait_ge(g_prow, 4 * (g - FIRST_UNIT[1]) + 4)
                        if i >= 2:
                            pe.wait_ge(a_pt, i - 1)
                        kt, r0, r1 = key_steps(br, u)[j]
                        for r in range(r0, r1):
                            at = tile_at(br, u, r, kt)
                            last = nc.tensor.transpose(ps[:, 4 + i % 2, 128 * r:128 * r + 128],
                                                       P[:, g % 2, r, 128 * at:128 * at + 128], ident[:])
                        last.then_inc(pe_pt, 1)

                    def mix_values(g, j):
                        br, ui, u = UN[g]
                        i = ks_at[(g, j)]
                        pe.wait_ge(a_pt, i + 1)
                        if j == 0 and g >= 2:
                            pe.wait_ge(v_oev, g - 1)
                            if br == 0:
                                pe.wait_ge(a_oT, g - 1)
                        kt, r0, r1 = key_steps(br, u)[j]
                        n = len(key_steps(br, u))
                        ob = 6 + g % 2
                        if br == 0:
                            for r in range(r0, r1):
                                h = u[1] if u[0] == "lat" else r
                                last = nc.tensor.matmul(ps[:, ob, 128 * r:128 * r + 128], PT[:, i % 3, 128 * r:128 * r + 128],
                                                        V[:, kt, 128 * h:128 * h + 128],
                                                        start=j == 0 and r == 0, stop=j == n - 1, skip_group_check=True)
                        elif u[0] == "ctx":
                            for r in range(4):
                                h = 4 * u[1] + r
                                vh = h if br == 1 else h // 4
                                last = nc.tensor.matmul(ps[64 * (h % 2):64 * (h % 2) + 64, ob, 128 * (r // 2):128 * (r // 2) + 128],
                                                        V[:, kt, 64 * vh:64 * vh + 64], PT[:, i % 3, 128 * r:128 * r + 128],
                                                        start=r < 2, stop=True, skip_group_check=True)
                        else:
                            h = u[1]
                            vh = h if br == 1 else h // 4
                            last = nc.tensor.matmul(ps[64 * (h % 2):64 * (h % 2) + 64, ob, 128 * r0:128 * r1],
                                                    V[:, kt, 64 * vh:64 * vh + 64], PT[:, i % 3, 128 * r0:128 * r1],
                                                    start=j == 0, stop=j == n - 1, skip_group_check=True)
                        last.then_inc(pe_pv, 1)

                    def attend(br):
                        us = units(br)
                        n = len(us)
                        pe.wait_ge(a_qk, copies(len([q for q in QU if PU[q][0] <= br])))
                        pe.wait_ge(a_copy, len([a for a in AU if PU[a][0] <= br]))
                        pe.wait_ge(v_unit, len([a for a in DU if PU[a][0] <= br]))
                        pe.wait_ge(g_zero, 8)
                        pe.wait_ge(cache_k_in, 16 * (br + 1))
                        pe.wait_ge(cache_v_in, 16 * (br + 1))
                        pe.wait_ge(a_mod, n_cg[0])
                        pe.wait_ge(v_mod, len([cg for cg in CG_ORDER[:n_cg[0]] if cg not in G_CG]))
                        for ui in range(n + 2):
                            g = FIRST_UNIT[br] + ui
                            for i in range(5):
                                if ui < n and i < 4:
                                    scores(g, i)
                                if 1 <= ui <= n:
                                    steps = len(key_steps(br, us[ui - 1]))
                                    if i < steps:
                                        transpose_probs(g - 1, i)
                                    if 1 <= i <= steps:
                                        mix_values(g - 1, i - 1)
                                if br == 0 and ui >= 2 and i == 3:
                                    pe.wait_ge(v_anorm, g - 1)
                                    for r in range(4):
                                        last = nc.tensor.transpose(ps[:, 6 + g % 2, 128 * r:128 * r + 128],
                                                                   tok[:, g % 2, 128 * r:128 * r + 128], ident[:])
                                    last.then_inc(pe_at, 1)
                            if 1 <= ui <= n and len(key_steps(br, us[ui - 1])) == 5:
                                mix_values(g - 1, 4)

                    def merge(br):
                        for mg in range(2):
                            for gate, mm_ in ((True, 0), (True, 1), (False, 0), (False, 1), (True, 2), (True, 3), (False, 2), (False, 3)):
                                i = 8 * br + 4 * mg + mm_
                                b = 4 * (i % 2)
                                if gate:
                                    if i >= 2:
                                        pe.wait_ge(a_sg, i - 1)
                                    if i == 8 * br + 1:
                                        pe.wait_ge(v_oev, FIRST_UNIT[br + 1])
                                        pe.wait_ge(a_oT, 5)
                                    w = take("gate", mm_ // 2).rearrange("p (k n) -> p k n", k=8)
                                    for k in range(KB):
                                        wk = w[:, k, 128 * (mm_ % 2):128 * (mm_ % 2) + 128]
                                        mm(ps[:, b, :], wk, hT[:, k, 0:512], k == 0, k == KB - 1)
                                        last = mm(ps[:, b + 1, 0:128], wk, hT[:, k, 512:640], k == 0, k == KB - 1, frees=False)
                                    last.then_inc(pe_gate, 1)
                                else:
                                    if i >= 2:
                                        pe.wait_ge(v_z, i - 1)
                                    w = take("br", 2).rearrange("p (k n) -> p k n", k=4)
                                    for k in range(4):
                                        wk = w[:, k, 128 * mm_:128 * mm_ + 128]
                                        mm(ps[:, b + 2, :], wk, oT[:, k, 0:512], k == 0, k == 3)
                                        last = mm(ps[:, b + 3, 0:128], wk, oT[:, k, 512:640], k == 0, k == 3, frees=False)
                                    last.then_inc(pe_br, 1)
                            used(3)

                    for br in range(3):
                        project(br)
                        attend(br)
                        merge(br)

                    def gate_rows(first):
                        for v in range(2):
                            for n in range(2):
                                nc.tensor.matmul(ps[:, 4 + 2 * v + n, :], sel[:, v:v + 1].to_broadcast([128, 128]), graw[:, first + n, :],
                                                 start=True, stop=True).then_inc(pe_gb, 1)

                    pe.wait_ge(v_z, 3 * KB)
                    gate_rows(0)
                    for n in range(2):
                        for t in range(NT):
                            i = n * NT + t
                            if i >= 4:
                                pe.wait_ge(v_ln, i - 3)
                            for k in range(KB):
                                w = take("o", k // 4).rearrange("p (k n) -> p k n", k=4)[:, k % 4, :]
                                last = mm(ps[:, i % 4, :], zT[:, k, 128 * t:128 * t + 128], w, k == 0, k == KB - 1, frees=k < KB - 1)
                            last.then_inc(pe_y, 1)
                        used(2)
                    pe.wait_ge(v_x, NT)
                    pe.wait_ge(v_G, 4)
                    gate_rows(2)
                    transpose_x(KB)
                    pe.wait_ge(a_hT, 4 * KB)
                    pe.wait_ge(v_G, 8)
                    for t in range(NT):
                        for k in range(KB):
                            last = mm(ps[:, 6, NE * t:NE * t + NE], hT[:, k, 128 * t:128 * t + 128], wr[:, k, :], k == 0, k == KB - 1,
                                      frees=k < KB - 1)
                    last.then_inc(pe_rt, 1)
                    pe.wait_ge(a_rt, 1)
                    for e in range(NE):
                        if e:
                            pe.wait_ge(v_ye, NT * e)
                        for m in range(2):
                            for j in range(2):
                                w = take(("w1", "w3")[j], j).rearrange("p (k n) -> p k n", k=8)
                                b = 4 * m + 2 * j
                                for k in range(KB):
                                    wk = w[:, k, 128 * m:128 * m + 128]
                                    mm(ps[:, b, :], wk, hT[:, k, 0:512], k == 0, k == KB - 1)
                                    last = mm(ps[:, b + 1, 0:128], wk, hT[:, k, 512:640], k == 0, k == KB - 1, frees=False)
                            last.then_inc(pe_h, 1)
                        pe.wait_ge(v_he, 2 * e + 2)
                        w = take("w2", 2).rearrange("p (m n) -> p m n", m=2)
                        for t in range(NT):
                            if t == 4:
                                pe.wait_ge(v_ye, NT * e + 1)
                            for n in range(2):
                                for m in range(2):
                                    last = mm(ps[:, 2 * (t % 4) + n, :], he[:, e % 2, m, 128 * t:128 * t + 128],
                                              w[:, m, 512 * n:512 * n + 512], m == 0, m == 1, frees=False)
                            last.then_inc(pe_e, 1)
                        used(3)
                    assert piece[0] == NP

                @block.scalar
                def _(act):
                    ch = Chain(act)
                    act.wait_ge(v_lam, 2)
                    ch.step(nc.scalar.activation(small[:, 2:4], small[:, 0:2], ACT.Exp), a_lam)
                    n_cg = [0]

                    def keep_mod(cg):
                        act.wait_ge(pe_mod, n_cg[0] + 1)
                        dst = graw[:, G_CG.index(cg), :] if cg in G_CG else modraw[:]
                        ch.step(nc.scalar.copy(dst, ps[:, 6, :]), a_mod)
                        n_cg[0] += 1

                    for cg in MOD_FIRST:
                        keep_mod(cg)

                    def modulate(first, sc, sh):
                        for k in range(KB):
                            act.wait_ge(pe_xT, first + k + 1)
                            b = 2 * (k % 2)
                            for v, (dst, src) in enumerate(((hT[:, k, 0:512], ps[:, b, :]), (hT[:, k, 512:640], ps[:, b + 1, 0:128]))):
                                ch.step(nc.scalar.activation(dst, src, ACT.Identity, scale=modcol[:, sc + k, v:v + 1],
                                                             bias=modcol[:, sh + k, v:v + 1]), a_hT)

                    act.wait_ge(v_mod, 4)
                    modulate(0, 8, 0)
                    act.wait_ge(x_out, 16)
                    act.wait_ge(pe_xT, KB)

                    def tok_free(q):
                        if q >= 2:
                            act.wait_ge(pe_tp, q - 1)
                            n = len([i for i in NEW_K if i in QU and QU.index(i) <= q - 2])
                            if n:
                                act.wait_ge(new_k_out, 16 * n)

                    def keep_unit(q):
                        br, c, t = PU[QU[q]]
                        act.wait_ge(pe_tp, q + 1)
                        nb = 2 if c == 7 else 4
                        src = ps[:, 4 + q % 2, 0:128 * nb].rearrange("p (b t) -> p b t", b=nb)
                        if CHUNK_TYPE[c] == "q":
                            ch.step(nc.scalar.activation(QT[:, :, 128 * t:128 * t + 128], src, ACT.Copy, scale=HD ** -0.5), a_qk)
                        else:
                            for lo in (0, 64):
                                dst = KT[lo:lo + 64, 0:2 * nb, 128 * t:128 * t + 128].rearrange("p (b a) t -> p b a t", a=2)[:, :, lo // 64, :]
                                ch.step(nc.scalar.copy(dst, src[lo:lo + 64]), a_qk)

                    def project(br):
                        for c in CHUNKS[br]:
                            keep_mod(MOD_LATER[c])
                            for t in range(NT):
                                i = PU.index((br, c, t))
                                if i in AU:
                                    act.wait_ge(pe_acc, i + 1)
                                    if CHUNK_TYPE[c] in ("v", "kv"):
                                        if t == CTX and br:
                                            act.wait_ge(new_v_out, 16 * br)
                                        dst, src = (V[:, t, :], ps[:, i % 4, :]) if c < 7 else (V[:, t, 0:128], ps[:, i % 4, 128:256])
                                    else:
                                        q = QU.index(i)
                                        tok_free(q)
                                        dst, src = tok[:, q % 2, :], ps[:, i % 4, :]
                                    ch.step(nc.scalar.copy(dst, src), a_copy)
                                if i and i - 1 in QU and PU[i - 1][0] == br:
                                    keep_unit(QU.index(i - 1))
                        if i in QU:
                            keep_unit(QU.index(i))

                    def exps(g, r):
                        br, ui, u = UN[g]
                        w = width(br, u, r)
                        for m in range(2 if br == 0 else 1):
                            i = sc_at[(g, r, m)]
                            act.wait_ge(v_max, i + 1)
                            if m == 0:
                                dst = P[:, g % 2, r, 0:w]
                                if g >= 2:
                                    act.wait_ge(pe_pt, last_ks(g - 2) + 1)
                            else:
                                dst = P1[:, rw_at[(g, r)] % 2, 0:w]
                                if rw_at[(g, r)] >= 2:
                                    act.wait_ge(v_diff, rw_at[(g, r)] - 1)
                            src = dst if (g, r) in bias_at else flat(2 * (i % 2), 1024)[:, 0:w]
                            ch.step(nc.scalar.activation(dst, src, ACT.Exp, bias=nmax[:, i % 16:i % 16 + 1],
                                                         accum_out=rsum[:, i % 16:i % 16 + 1]), a_exp)

                    def keep_probs(g, j):
                        br, ui, u = UN[g]
                        i = ks_at[(g, j)]
                        act.wait_ge(pe_pt, i + 1)
                        if i >= 3:
                            act.wait_ge(pe_pv, i - 2)
                        kt, r0, r1 = key_steps(br, u)[j]
                        ch.step(nc.scalar.copy(PT[:, i % 3, 128 * r0:128 * r1], ps[:, 4 + i % 2, 128 * r0:128 * r1]), a_pt)

                    def attend(br):
                        us = units(br)
                        n = len(us)
                        for ui in range(n + 2):
                            g = FIRST_UNIT[br] + ui
                            for i in range(5):
                                if ui < n and i < 4:
                                    exps(g, i)
                                if 1 <= ui <= n and i < len(key_steps(br, us[ui - 1])):
                                    keep_probs(g - 1, i)
                                if br == 0 and ui >= 2 and i == 3:
                                    act.wait_ge(pe_at, g - 1)
                                    src = ps[:, 6 + g % 2, :]
                                    if ui - 2 < 4:
                                        ch.step(nc.scalar.copy(oT[:, ui - 2, 0:512], src), a_oT)
                                    else:
                                        ch.step(nc.scalar.copy(oT[:, :, 512:640], src.rearrange("p (b t) -> p b t", b=4)), a_oT)

                    for br in range(3):
                        project(br)
                        attend(br)
                        for m in range(KB):
                            i = 8 * br + m
                            act.wait_ge(pe_gate, i + 1)
                            if i >= 2:
                                act.wait_ge(v_z, i - 1)
                            ch.step(nc.scalar.activation(sg[:, i % 2, :], flat(4 * (i % 2), 640), ACT.Sigmoid,
                                                         bias=bgate[:, i:i + 1]), a_sg)
                    modulate(KB, 32, 24)
                    act.wait_ge(pe_rt, 1)
                    ch.step(nc.scalar.activation(route[:, 0].rearrange("p t e -> p (t e)"), ps[:, 6, 0:NT * NE], ACT.Sigmoid), a_rt)
                    for i in range(2 * NE):
                        act.wait_ge(pe_h, i + 1)
                        if i >= 2:
                            act.wait_ge(v_he, i - 1)
                        ch.step(nc.scalar.activation(sig[:, i % 2, :], flat(4 * (i % 2), 640), ACT.Sigmoid), a_esg)

                @block.vector
                def _(dve):
                    ch = Chain(dve)
                    V_ = nc.vector
                    dve.wait_ge(par_in, 16)
                    lv = lam.rearrange("p (a b n) -> p a b n", a=2, b=2)
                    lp = tmpA[:, 0:128].rearrange("p (a n) -> p a n", a=2)
                    ch.step(V_.tensor_tensor(lp, lv[:, :, 0], lv[:, :, 1], ALU.mult), v_lam)
                    ch.step(V_.reduce_sum(small[:, 0:2], lp, axis=AX.X), v_lam)
                    dve.wait_ge(a_lam, 1)
                    ch.step(V_.tensor_tensor(nlam[:], small[:, 3:4], small[:, 2:3], ALU.subtract), v_chain)
                    ch.step(V_.tensor_tensor(nlam[:], nlam[:], laminit[:, 0:1], ALU.subtract), v_chain)
                    ch.step(V_.tensor_scalar(subln, subln, laminit[:, 1:2], None, ALU.mult), v_chain)

                    def mod_columns(cg):
                        k = COL_CG.index(cg)
                        dve.wait_ge(pe_ext, k + 1)
                        dst = modcol[:, 4 * cg:4 * cg + 4, :]
                        b = bmod[:, 4 * cg:4 * cg + 4].unsqueeze(2).to_broadcast([128, 4, 2])
                        scale = cg in (2, 3, 8, 9)
                        ch.step(V_.tensor_tensor(dst, ps[:, 7, 0:8].rearrange("p (b v) -> p b v", v=2), b, ALU.add), v_chain if scale else v_mod)
                        if scale:
                            ch.step(V_.tensor_scalar(dst, dst, 1.0, None, ALU.add), v_mod)

                    for cg in MOD_FIRST:
                        mod_columns(cg)

                    def rope(dst, src, t, nh, s):
                        c = cosT[:, t, :].unsqueeze(1).to_broadcast([128, nh, HD])
                        sn = sinT[:, t, :].rearrange("p (i b) -> p i b", b=2)
                        sp2 = src.rearrange("p h (i b) -> p h i b", b=2)
                        tb = tmpB[:, 0:HD * nh].rearrange("p (h i b) -> p h i b", h=nh, b=2)
                        ch.step(V_.tensor_tensor(dst, src, c, ALU.mult), v_chain)
                        for a in range(2):
                            sa = sn[:, :, a].unsqueeze(1).to_broadcast([128, nh, HD // 2])
                            ch.step(V_.tensor_tensor(tb[:, :, :, a], sp2[:, :, :, 1 - a], sa, ALU.mult), v_chain)
                        ch.step(V_.tensor_tensor(dst, dst, tb.rearrange("p h i b -> p h (i b)"), ALU.add), s)

                    def mean_squares(n, w):
                        ch.step(V_.tensor_tensor(tmpB[:, 0:n * w], tmpA[:, 0:n * w], tmpA[:, 0:n * w], ALU.mult), v_chain)
                        ch.step(V_.reduce_sum(small[:, 0:n], tmpB[:, 0:n * w].rearrange("p (h d) -> p h d", h=n), axis=AX.X), v_chain)
                        ch.step(V_.tensor_scalar(small[:, 0:n], small[:, 0:n], 1.0 / w, RMS_EPS, ALU.mult, ALU.add), v_sq)
                        dve.wait_ge(g_rs, ch.count(v_sq))
                        a = tmpA[:, 0:n * w].rearrange("p (h d) -> p h d", h=n)
                        ch.step(V_.tensor_tensor(a, a, small[:, 8:8 + n].unsqueeze(2).to_broadcast([128, n, w]), ALU.mult), v_chain)
                        return a

                    def unit(i):
                        br, c, t = PU[i]
                        q = QU.index(i)
                        dve.wait_ge(pe_acc, i + 1)
                        if q >= 2:
                            dve.wait_ge(pe_tp, q - 1)
                            n = len([j for j in NEW_K if QU.index(j) <= q - 2])
                            if n:
                                dve.wait_ge(new_k_out, 16 * n)
                        if c in (0, 1):
                            rope(tok[:, q % 2, :].rearrange("p (h d) -> p h d", d=HD), ps[:, i % 4, :].rearrange("p (h d) -> p h d", d=HD), t, 8, v_unit)
                            return
                        nh = 8 if c == 6 else 2
                        w = (qnw if c == 6 else knw).unsqueeze(1).to_broadcast([128, nh, HD])
                        if c == 7:
                            dve.wait_ge(a_copy, AU.index(i) + 1)
                        ch.step(V_.tensor_copy(tmpA[:, 0:nh * HD], ps[:, i % 4, 0:nh * HD]), v_chain)
                        a = mean_squares(nh, HD)
                        if c == 6:
                            dst = tok[:, q % 2, :].rearrange("p (h d) -> p h d", d=HD)
                        else:
                            both = tok[:, q % 2, 0:256].rearrange("p (h a d) -> p h a d", h=2, a=2)
                            dst = both[:, :, 0, :]
                        if t == CTX:
                            ch.step(V_.tensor_tensor(dst, a, w, ALU.mult), v_unit if c == 6 else v_chain)
                        else:
                            ch.step(V_.tensor_tensor(a, a, w, ALU.mult), v_chain)
                            rope(dst, a, t, nh, v_unit if c == 6 else v_chain)
                        if c == 7:
                            ch.step(V_.tensor_copy(both[:, :, 1, :], dst), v_unit)

                    def project(br):
                        for c in CHUNKS[br]:
                            for t in range(NT):
                                i = PU.index((br, c, t))
                                if i in DU:
                                    unit(i)
                                if t == 0 and MOD_LATER[c] not in G_CG:
                                    mod_columns(MOD_LATER[c])

                    def maxima(g, r):
                        br, ui, u = UN[g]
                        w = width(br, u, r)
                        for m in range(2 if br == 0 else 1):
                            i = sc_at[(g, r, m)]
                            dve.wait_ge(pe_score, i + 1)
                            src = flat(2 * (i % 2), 1024)[:, 0:w]
                            if (g, r) in bias_at:
                                dve.wait_ge(g_mb, 4 * (u[1] + 1))
                                dve.wait_ge(pe_pt, last_ks(g - 2) + 1)
                                n = w - 128
                                row = P[:, g % 2, r, 0:w]
                                ch.step(V_.tensor_tensor(row[:, 0:n], src[:, 0:n], MB[:, u[1] % 2, MB_AT[r]:MB_AT[r] + n], ALU.add), v_chain)
                                ch.step(V_.tensor_copy(row[:, n:w], src[:, n:w]), v_bias)
                                src = row
                            ch.step(V_.tensor_reduce(nmax[:, i % 16:i % 16 + 1], src, axis=AX.X, op=ALU.max, negate=True), v_max)

                    def finish(g, r):
                        br, ui, u = UN[g]
                        w = width(br, u, r)
                        for m in range(2 if br == 0 else 1):
                            i = sc_at[(g, r, m)]
                            dve.wait_ge(a_exp, i + 1)
                            ch.step(V_.reciprocal(rinv[:, i % 16:i % 16 + 1], rsum[:, i % 16:i % 16 + 1]), v_rinv)
                        if br == 0:
                            p1 = P1[:, rw_at[(g, r)] % 2, 0:w]
                            r1 = rinv[:, i % 16:i % 16 + 1]
                            r0 = rinv[:, (i - 1) % 16:(i - 1) % 16 + 1]
                            ch.step(V_.tensor_scalar(p1, p1, r1, nlam[:], ALU.mult, ALU.mult), v_chain)
                            ch.step(V_.scalar_tensor_tensor(P[:, g % 2, r, 0:w], P[:, g % 2, r, 0:w], r0, p1, ALU.mult, ALU.add), v_diff)

                    def output(g):
                        br, ui, u = UN[g]
                        dve.wait_ge(pe_pv, last_ks(g) + 1)
                        src = ps[:, 6 + g % 2, :]
                        if br == 0:
                            if g == 0:
                                dve.wait_ge(new_k_out, 16)
                            ch.step(V_.tensor_copy(tmpA[:], src), v_oev)
                            a = mean_squares(4, 128)
                            if g >= 2:
                                dve.wait_ge(pe_at, g - 1)
                            ch.step(V_.tensor_tensor(tok[:, g % 2, :].rearrange("p (h d) -> p h d", h=4), a,
                                                     subln.unsqueeze(1).to_broadcast([128, 4, 128]), ALU.mult), v_anorm)
                        elif u[0] == "lat":
                            lo = 64 * (u[1] % 2)
                            ch.step(V_.tensor_copy(oT[lo:lo + 64, u[1] // 2, 0:512], src[lo:lo + 64, :]), v_oev)
                        else:
                            ch.step(V_.tensor_copy(oT[:, 2 * u[1]:2 * u[1] + 2, 512:640], src[:, 0:256].rearrange("p (b t) -> p b t", b=2)), v_oev)

                    def attend(br):
                        n = len(units(br))
                        for ui in range(n + 2):
                            g = FIRST_UNIT[br] + ui
                            for i in range(4):
                                if ui < n:
                                    maxima(g, i)
                                if ui < n and i:
                                    finish(g, i - 1)
                                elif ui and ui <= n and i == 0:
                                    finish(g - 1, 3)
                                if ui >= 2 and i == 1:
                                    output(g - 2)

                    for br in range(3):
                        project(br)
                        attend(br)
                        for m in range(KB):
                            i = 8 * br + m
                            dve.wait_ge(a_sg, i + 1)
                            dve.wait_ge(pe_br, i + 1)
                            src = flat(4 * (i % 2) + 2, 640)
                            if br == 0:
                                ch.step(V_.tensor_tensor(zT[:, m, :], sg[:, i % 2, :], src, ALU.mult), v_z)
                            else:
                                ch.step(V_.tensor_tensor(prod, sg[:, i % 2, :], src, ALU.mult), v_chain)
                                ch.step(V_.tensor_tensor(zT[:, m, :], zT[:, m, :], prod, ALU.add), v_z)

                    def keep_gate(G, k):
                        for j in range(4):
                            dve.wait_ge(pe_gb, 4 * k + j + 1)
                            n = j % 2
                            ch.step(V_.tensor_tensor(G[:, j // 2, 512 * n:512 * n + 512], ps[:, 4 + j, :], rows[:, k, 512 * n:512 * n + 512], ALU.add), v_G)

                    def layer_norm(t, k):
                        o = 4 * ((k * NT + t) % 2)
                        st = lnst[:, 16 * (t % 2):16 * (t % 2) + 16]
                        for n in range(2):
                            ch.step(V_.bn_stats(st[:, 6 * n:6 * n + 6], x[:, t, 512 * n:512 * n + 512]), v_chain)
                        ch.step(V_.bn_aggr(st[:, 12:14], st[:, 0:12]), v_chain)
                        ch.step(V_.tensor_scalar(small[:, 34 + o:35 + o], st[:, 13:14], LN_EPS, None, ALU.add), v_lnv)
                        dve.wait_ge(g_rs, 15 + k * NT + t + 1)
                        ch.step(V_.tensor_scalar(x[:, t, :], x[:, t, :], st[:, 12:13], small[:, 32 + o:33 + o], ALU.subtract, ALU.mult), v_chain)
                        ch.step(V_.tensor_tensor(x[:, t, :], x[:, t, :], rows[:, 2 + k, :], ALU.mult), v_chain)
                        ch.step(V_.tensor_tensor(x[:, t, :], x[:, t, :], rows[:, 4 + k, :], ALU.add), v_x)

                    dve.wait_ge(rows_in, 16)
                    dve.wait_ge(x_in, 16)
                    keep_gate(G1, 0)
                    for n in range(2):
                        for t in range(NT):
                            i = n * NT + t
                            dve.wait_ge(pe_y, i + 1)
                            cols = slice(512 * n, 512 * n + 512)
                            ch.step(V_.tensor_tensor(acc[:, t, cols], ps[:, i % 4, :], G1[:, int(t == CTX), cols], ALU.mult), v_chain)
                            ch.step(V_.scalar_tensor_tensor(x[:, t, cols], x[:, t, cols], ALPHA, acc[:, t, cols], ALU.mult, ALU.add), v_ln)
                            if n:
                                layer_norm(t, 0)
                    keep_gate(G2, 1)

                    dve.wait_ge(a_rt, 1)
                    S4 = [128, NT, 4]

                    def plane(k):
                        return route[:, k]

                    def tiny(k):
                        return route[:, 10 + k // 4, :, 4 * (k % 4):4 * (k % 4) + 4]

                    def op2(dst, a, b, op):
                        ch.step(V_.tensor_tensor(dst, a, b, op), v_chain)

                    def wide(a, n):
                        return a.to_broadcast([128, NT, n])

                    score, selv, m_, val, one, two = (plane(k) for k in range(6))
                    op2(selv, score, rbias[:].unsqueeze(1).to_broadcast([128, NT, NE]), ALU.add)
                    grp = selv.rearrange("p t (g e) -> p t g e", g=4)
                    a, b, c, d = (grp[:, :, :, k] for k in range(4))
                    T = [tiny(k) for k in range(8)]
                    op2(T[0], a, b, ALU.max)
                    op2(T[1], a, b, ALU.min)
                    op2(T[2], c, d, ALU.max)
                    op2(T[3], c, d, ALU.min)
                    op2(T[4], T[0], T[2], ALU.max)
                    op2(T[5], T[0], T[2], ALU.min)
                    op2(T[6], T[1], T[3], ALU.max)
                    op2(T[5], T[5], T[6], ALU.max)
                    op2(T[4], T[4], T[5], ALU.add)

                    def first_best(dst, v, idx, n, tmp, top):
                        ch.step(V_.reduce_max(top, v, axis=AX.X), v_chain)
                        op2(tmp, v, wide(top, n), ALU.is_equal)
                        op2(tmp, tmp, idx.unsqueeze(1).to_broadcast([128, NT, n]), ALU.mult)
                        ch.step(V_.reduce_max(top, tmp, axis=AX.X), v_chain)
                        op2(dst, tmp, wide(top, n), ALU.is_equal)

                    top = T[7][:, :, 0:1]
                    first_best(T[0], T[4], eidx[:, NE - 4:NE], 4, T[1], top)
                    ch.step(V_.tensor_scalar(T[1], T[0], -FAR, FAR, ALU.mult, ALU.add), v_chain)
                    m4 = m_.rearrange("p t (g e) -> p t g e", g=4)
                    op2(m4, grp, T[0].unsqueeze(3).to_broadcast([128, NT, 4, 4]), ALU.mult)
                    op2(m4, m4, T[1].unsqueeze(3).to_broadcast([128, NT, 4, 4]), ALU.add)
                    first_best(one, m_, eidx[:], NE, val, top)
                    ch.step(V_.tensor_scalar(val, one, 3 * FAR, None, ALU.mult), v_chain)
                    op2(m_, m_, val, ALU.add)
                    first_best(two, m_, eidx[:], NE, val, top)
                    op2(one, one, two, ALU.add)
                    op2(one, one, score, ALU.mult)
                    ch.step(V_.reduce_sum(top, one, axis=AX.X), v_chain)
                    ch.step(V_.reciprocal(top, top), v_chain)
                    op2(comb[:], one, wide(top, NE), ALU.mult)

                    for e in range(NE):
                        for m in range(2):
                            i = 2 * e + m
                            dve.wait_ge(a_esg, i + 1)
                            ch.step(V_.tensor_tensor(sig[:, i % 2, :], sig[:, i % 2, :], flat(4 * m, 640), ALU.mult), v_chain)
                            ch.step(V_.tensor_tensor(he[:, e % 2, m, :], sig[:, i % 2, :], flat(4 * m + 2, 640), ALU.mult), v_he)
                        for t in range(NT):
                            dve.wait_ge(pe_e, NT * e + t + 1)
                            src = flat(2 * (t % 4), 1024)
                            if e == 0:
                                ch.step(V_.tensor_scalar(acc[:, t, :], src, comb[:, t, e:e + 1], None, ALU.mult), v_ye)
                            else:
                                ch.step(V_.scalar_tensor_tensor(acc[:, t, :], src, comb[:, t, e:e + 1], acc[:, t, :], ALU.mult, ALU.add), v_ye)
                    for t in range(NT):
                        ch.step(V_.tensor_tensor(acc[:, t, :], acc[:, t, :], G2[:, int(t == CTX), :], ALU.mult), v_chain)
                        ch.step(V_.scalar_tensor_tensor(x[:, t, :], x[:, t, :], ALPHA, acc[:, t, :], ALU.mult, ALU.add), v_chain)
                        layer_norm(t, 1)

            nc.all_engine_barrier(sems_to_clear=all_sems)

        with nc.Block() as block:
            @block.sync
            def _(sp):
                sp.dma_start(OUT["y"].rearrange("t p n -> p t n"), x[:]).then_inc(x_out, 16)
                sp.wait_ge(x_out, 16)


def positions():
    g, r, c = np.meshgrid(np.arange(LAT), np.arange(ROWS), np.arange(GW), indexing="ij")
    return (r * GRID_W + g * GW + c).ravel()


def rope_tables():
    t = positions()
    n = HD // 4
    freqs = (np.float32(10000.0) ** (-np.arange(n, dtype=np.float32) / np.float32(n))).astype(np.float32)
    ang = np.concatenate([(t // GRID_W).astype(np.float32)[:, None] * freqs,
                          (t % GRID_W).astype(np.float32)[:, None] * freqs], -1)
    cos, sin = np.cos(ang), np.sin(ang)
    c = np.stack([cos, cos], -1).reshape(LAT, 128, HD)
    s = np.stack([-sin, sin], -1).reshape(LAT, 128, HD)
    return (np.ascontiguousarray(a.transpose(1, 0, 2).astype(np.float32)) for a in (c, s))


def window_mask():
    m = np.full((128, LAT, 3 * GW), FAR, np.float32)
    for g in range(LAT):
        for ci in range(GW):
            c = g * GW + ci
            cs = min(max(c - NA_KW // 2, 0), GRID_W - NA_KW)
            for u in range(3 * GW):
                k = GW * (g - 1) + u
                if cs <= k < cs + NA_KW:
                    m[ci::GW, g, u] = 0
    return m


def lay_out(i):
    f = np.float32
    L = DEPTH
    pos = positions()
    a = {}
    a["x"] = np.concatenate([i["x_sample"][0][pos], i["x_prompt"][0]]).reshape(NT, 128, D)
    cs = np.zeros((128, KB, 32), f)
    cs[:, :, 0] = i["c"][0].reshape(KB, 128).T
    cs[:, :, 1] = i["c_ctx"].reshape(KB, 128).T
    a["cs"] = cs
    a["ident"] = np.eye(128, dtype=f)
    sel = np.zeros((128, 2), f)
    for j in range(4):
        for v in range(2):
            sel[32 * j + v, v] = 1
    a["sel"] = sel
    a["cosT"], a["sinT"] = rope_tables()
    a["mask"] = window_mask()
    a["wr"] = i["w_router"].reshape(KB, 128, NE).transpose(1, 0, 2)
    a["rbias"] = np.broadcast_to(i["router_bias"], (128, NE))
    a["eidx"] = np.broadcast_to(np.arange(NE, 0, -1).astype(f), (128, NE))

    def kparts(w, n0, n1):
        w = w[:, n0:n1]
        return w.reshape(-1, 128, n1 - n0).transpose(1, 0, 2).reshape(128, -1)

    wall = np.empty((L, NP, 128, PIECE), f)
    for l in range(L):
        for n, p in enumerate(PIECES):
            if p[0] == "mod":
                w = i["w_mod"][l][512 * p[2]:512 * p[2] + 512]
                wall[l, n] = kparts(w, 512 * p[1], 512 * p[1] + 512)
            elif p[0] == "in":
                if p[1] < 7:
                    wall[l, n] = kparts(i["w_in"][l][512 * p[2]:512 * p[2] + 512], 512 * p[1], 512 * p[1] + 512)
                else:
                    wall[l, n] = kparts(i["w_in"][l], 3584, 3840)
            elif p[0] == "gate":
                n0 = D * p[1] + 256 * p[2]
                wall[l, n] = kparts(i["w_gate"][l], n0, n0 + 256)
            elif p[0] == "br":
                wall[l, n] = kparts(i["w_br"][l, p[1]], 512 * p[2], 512 * p[2] + 512)
            elif p[0] == "o":
                wall[l, n] = kparts(i["w_o"][l][512 * p[2]:512 * p[2] + 512], 512 * p[1], 512 * p[1] + 512)
            elif p[0] == "w1":
                wall[l, n] = kparts(i["moe_w1"][l, p[1]], 0, DE)
            elif p[0] == "w3":
                wall[l, n] = kparts(i["moe_w3"][l, p[1]], 0, DE)
            else:
                wall[l, n] = kparts(i["moe_w2"][l, p[1]], 0, D)
    a["wall"] = wall

    par = np.empty((L, 128, 586), f)
    par[:, :, 0:48] = i["b_mod"].reshape(L, 48, 128).transpose(0, 2, 1)
    par[:, :, 48:72] = i["b_gate"].reshape(L, 24, 128).transpose(0, 2, 1)
    par[:, :, 72:200] = i["a_subln"][:, None, :]
    par[:, :, 200:264] = i["c_qnorm"][:, None, :]
    par[:, :, 264:328] = i["c_knorm"][:, None, :]
    par[:, :, 328:584] = i["lam"].reshape(L, 1, 256)
    for l in range(L):
        init = 0.8 - 0.6 * math.exp(-0.3 * l)
        par[l, :, 584], par[l, :, 585] = init, 1.0 - init
    a["par"] = par
    rows = np.empty((L, 128, 6, D), f)
    rows[:, :, 0] = i["b_mod"][:, None, 2 * D:3 * D]
    rows[:, :, 1] = i["b_mod"][:, None, 5 * D:6 * D]
    rows[:, :, 2:4] = i["ln_g"][:, None]
    rows[:, :, 4:6] = i["ln_b"][:, None]
    a["rows"] = rows

    ck = np.zeros((L, 3, 128, 8, 128), f)
    cv = np.zeros((L, 3, 128, 512), f)
    ka = i["cache_a_k"][0].reshape(L, 128, 8, HD)
    kb = i["cache_b_k"][0]
    kc = i["cache_c_k"][0]
    for h in range(8):
        lo = 64 * (h % 2)
        ck[:, 0, lo:lo + 64, h] = ka[:, :, h].transpose(0, 2, 1)
        ck[:, 1, lo:lo + 64, h] = kb[:, :, h].transpose(0, 2, 1)
        if h < 4:
            ck[:, 2, lo:lo + 64, h] = kc[:, :, h // 2].transpose(0, 2, 1)
    cv[:, 0] = i["cache_a_v"][0].reshape(L, 128, 512)
    cv[:, 1] = i["cache_b_v"][0].reshape(L, 128, 512)
    cv[:, 2, :, 0:128] = i["cache_c_v"][0].reshape(L, 128, 128)
    a["cache_kT"], a["cache_v"] = ck, cv

    pad = np.full((L, 8, 15, 3 * GW + GW + 15), FAR, f)
    pad[:, :, :, 16:47] = i["rpb"]
    bias = np.empty((L, 8, ROWS, GW, ROWS, 3 * GW), f)
    for r in range(ROWS):
        for ci in range(GW):
            bias[:, :, r, ci] = pad[:, :, 7 - r:15 - r, 15 - ci:15 - ci + 3 * GW]
    a["bias"] = bias.reshape(L, 8, 128, ROWS, 3 * GW)
    return {k: np.ascontiguousarray(v) for k, v in a.items()}


def kernel(**inputs):
    import concourse.bacc as bacc
    from concourse.bass_utils import run_bass_kernel_spmd

    arrays = {"in_" + k: v for k, v in lay_out({k: np.asarray(v) for k, v in inputs.items()}).items()}
    f32 = mybir.dt.float32
    nc = bacc.Bacc("TRN2", target_bir_lowering=False, num_devices=1)
    A = {k[3:]: nc.dram_tensor(k, v.shape, f32, kind="ExternalInput").ap() for k, v in arrays.items()}
    A["x_state"] = nc.dram_tensor("x_state", (NT, 128, D), f32, kind="Internal").ap()
    shapes = {"y": (NT, 128, D), "ak": (DEPTH, 128, 512), "av": (DEPTH, 128, 512), "bk": (DEPTH, 128, 512),
              "bv": (DEPTH, 128, 512), "ck": (DEPTH, 128, 128), "cv": (DEPTH, 128, 128)}
    OUT = {k: nc.dram_tensor("out_" + k, s, f32, kind="ExternalOutput").ap() for k, s in shapes.items()}
    build_kernel(nc, A, OUT)
    r = run_bass_kernel_spmd(nc, [arrays], core_ids=[0]).results[0]
    y = r["out_y"].reshape(TOK, D)
    ys = np.empty((LTOK, D), np.float32)
    ys[positions()] = y[:LTOK]
    return (y[LTOK:][None], ys[None],
            r["out_ak"].reshape(1, DEPTH, 128, 2, 4, HD), r["out_av"].reshape(1, DEPTH, 128, 4, 2 * HD),
            r["out_bk"].reshape(1, DEPTH, 128, 8, HD), r["out_bv"].reshape(1, DEPTH, 128, 8, HD),
            r["out_ck"].reshape(1, DEPTH, 128, 2, HD), r["out_cv"].reshape(1, DEPTH, 128, 2, HD))
```

```python
import math
import numpy as np
import concourse.bass as bass
from concourse import mybir
from contextlib import ExitStack

D = 1024
KB = D // 128
DEPTH = 2
LAT = 4
NT = LAT + 1
CTX = LAT
TOK = NT * 128
LTOK = LAT * 128
HD = 64
NE = 16
DE = 256
GRID_W, ROWS, NA_KW, NA_KH = 64, 8, 16, 8
GW = GRID_W // LAT
LN_EPS, RMS_EPS = 1e-5, 1e-6
ALPHA = (2.0 * DEPTH) ** 0.25
SLOTS = 6
PIECE = 2048
FAR = -1e30

MOD_FIRST, MOD_LATER = (0, 1, 2, 3), (4, 5, 6, 7, 8, 9, 10, 11)
CHUNKS = {0: (0, 1, 2), 1: (3, 4, 5), 2: (6, 7)}
CHUNK_TYPE = ("q", "k", "v", "q", "k", "v", "q", "kv")


def piece_order():
    order = []
    for cg in MOD_FIRST:
        order += [("mod", cg, 0), ("mod", cg, 1)]
    for br in range(3):
        for c in CHUNKS[br]:
            order += [("mod", MOD_LATER[c], 0), ("mod", MOD_LATER[c], 1)]
            order += [("in", c, 0)] + [("in", c, 1)] * (c < 7)
        for mg in range(2):
            order += [("gate", br, 2 * mg), ("gate", br, 2 * mg + 1), ("br", br, mg)]
    order += [("o", n, h) for n in range(2) for h in range(2)]
    for e in range(NE):
        order += [("w1", e), ("w3", e), ("w2", e)]
    return order


BLOCKS = TOK // 128
EXTRA = (2 * TOK - 1) // 128


PIECES = piece_order()
NP = len(PIECES)
MOE0 = PIECES.index(("w1", 0))


def key_tiles(br, r):
    return list(range(max(r - 1, 0), min(r + 2, LAT))) if br == 1 else list(range(LAT))


def units(br):
    if br == 0:
        return [("lat", h) for h in range(4)] + [("ctx", 0)]
    return [("lat", h) for h in range(8)] + [("ctx", 0), ("ctx", 1)]


def key_steps(br, u):
    if u[0] == "ctx":
        return [(CTX, 0, 4)]
    steps = [(5, 0, LAT)]
    for kt in range(LAT):
        rs = [r for r in range(LAT) if kt in key_tiles(br, r)]
        steps.append((kt, rs[0], rs[-1] + 1))
    return steps


def build_kernel(nc, A, OUT):
    f32, bf16, u32, i32 = mybir.dt.float32, mybir.dt.bfloat16, mybir.dt.uint32, mybir.dt.int32
    ALU, ACT, AX = mybir.AluOpType, mybir.ActivationFunctionType, mybir.AxisListType
    ctx = ExitStack()

    def sb(name, shape):
        return ctx.enter_context(nc.sbuf_tensor(name, shape, f32))

    sems = []

    def sem(name):
        s = ctx.enter_context(nc.semaphore(name))
        sems.append(s)
        return s

    with ctx:
        ring = sb("ring", [128, SLOTS, PIECE])
        hT = sb("hT", [128, KB, TOK])
        zT = sb("zT", [128, KB, TOK])
        ident = sb("ident", [128, 128])
        sel = sb("sel", [128, 2])
        cosT = sb("cosT", [128, LAT, HD])
        sinT = sb("sinT", [128, LAT, HD])
        mask = sb("mask", [128, LAT, 3 * GW])
        cs = sb("cs", [128, KB, 32])
        half = sb("half", [128, 16])
        wr = sb("wr", [128, KB, NE])
        rbias = sb("rbias", [128, NE])
        eidx = sb("eidx", [128, NE])
        par = sb("par", [128, 48 + 24 + 128 + 64 + 64 + 256 + 2])
        bmod, bgate = par[:, 0:48], par[:, 48:72]
        subln, qnw, knw = par[:, 72:200], par[:, 200:264], par[:, 264:328]
        lam, laminit = par[:, 328:584], par[:, 584:586]
        nlam = sb("nlam", [128, 1])
        modcol = sb("modcol", [128, 48, 2])
        gsm = sb("gsm", [128, 2, 512])
        lt = ctx.enter_context(nc.sbuf_tensor("lt", [128, 128], bf16))
        ones = ctx.enter_context(nc.sbuf_tensor("ones", [128, 128], bf16))
        tokid = ctx.enter_context(nc.sbuf_tensor("tokid", [128, NT, 2], bf16))
        selbf = ctx.enter_context(nc.sbuf_tensor("selbf", [128, NT, NE], bf16))
        iota1 = sb("iota1", [128, 128])
        ebase = sb("ebase", [128, 2, NE])
        idx = ctx.enter_context(nc.sbuf_tensor("idx", [128, NE + 1], u32))
        yrow = ctx.enter_context(nc.sbuf_tensor("yrow", [128, 2, NT], u32))
        ovi = ctx.enter_context(nc.sbuf_tensor("ovi", [128, EXTRA + 1], i32))
        small_i = sb("small_i", [128, 2])
        nmax = sb("nmax", [128, 16])
        rsum = sb("rsum", [128, 16])
        rinv = sb("rinv", [128, 16])
        small = sb("small", [128, 64])

        R = sb("R", [128, 25984])

        def area(start, size):
            return R[:, start:start + size]

        QT = area(0, 2560).rearrange("p (b t) -> p b t", b=4)
        KT = area(2560, 6144).rearrange("p (s t) -> p s t", s=8)
        V = area(8704, 3072).rearrange("p (t e) -> p t e", t=6)
        oT = area(11776, 2560).rearrange("p (b t) -> p b t", b=4)
        P = area(14336, 5120).rearrange("p (s r k) -> p s r k", s=2, r=4)
        PT = area(19456, 1536).rearrange("p (s k) -> p s k", s=3)
        P1 = area(20992, 1280).rearrange("p (s k) -> p s k", s=2)
        MB = area(20992, 2560).rearrange("p (s k) -> p s k", s=2)
        WB = area(23552, 384).rearrange("p (r u) -> p r u", r=ROWS)
        tok = area(23936, 1024).rearrange("p (s k) -> p s k", s=2)
        tmpA, tmpB = area(24960, 512), area(25472, 512)
        modraw = area(19456, 512)
        sg = [area(a, 1280).rearrange("p (s k) -> p s k", s=2) for a in (14336, 14336, 20992)]
        prod = [area(a, 640) for a in (15616, 15616, 22272)]
        x = area(0, 5120).rearrange("p (t n) -> p t n", t=NT)
        rows = area(5120, 6144).rearrange("p (a n) -> p a n", a=6)
        rowsB = area(22912, 2048).rearrange("p (a n) -> p a n", a=2)
        SH = area(14336, 2048).rearrange("p (v n) -> p v n", v=2)
        SC = area(16384, 2048).rearrange("p (v n) -> p v n", v=2)
        G1 = area(18432, 2048).rearrange("p (v n) -> p v n", v=2)
        h2 = area(20992, 2048).rearrange("p (s n) -> p s n", s=2)
        yg = area(25472, 512)
        route = area(11776, 20 * NT * NE).rearrange("p (a t e) -> p a t e", a=20, t=NT)
        lnst = area(13376, 32)
        wts = area(13408, 2 * NT).rearrange("p (k t) -> p k t", k=2)
        ovf = area(13424, 2 * (EXTRA + 1)).rearrange("p (a j) -> p a j", a=2)
        ovq = area(13472, 6 * 64).rearrange("p (a c) -> p a c", a=6)
        ovt = area(16384, 2 * EXTRA * 64).rearrange("p (a j c) -> p a j c", a=2, j=EXTRA)
        G2 = area(14336, 2048).rearrange("p (v n) -> p v n", v=2)
        zf = zT[:].rearrange("p k t -> p (k t)")
        xg = zf[:, 0:3072].rearrange("p (s n) -> p s n", s=3)
        xgT = zf[:, 3072:5120].rearrange("p (s k t) -> p s k t", s=2, k=KB)
        ysb = area(18432, 2048).rearrange("p (s n) -> p s n", s=2)
        he = area(23040, 512).rearrange("p (s m t) -> p s m t", s=2, m=2)
        sig = area(23552, 256).rearrange("p (m t) -> p m t", m=2)
        hot = area(23808, 640).bitcast(bf16).rearrange("p (s t n) -> p s t n", s=2, t=NT)
        Y1 = zf.rearrange("p (t n) -> p t n", t=NT)
        Y2 = area(20480, 5120).rearrange("p (t n) -> p t n", t=NT)

        ps = ctx.enter_context(nc.psum_tensor("ps", [128, 8, 512], f32))

        def flat(bank, n):
            return ps[:, bank:bank + 2, :].rearrange("p b n -> p (b n)")[:, 0:n]

        y_init = ctx.enter_context(nc.semaphore("output_rows_filled"))
        full = [sem(f"piece_loaded_{s}") for s in range(SLOTS)]
        freed = sem("pieces_used")
        consts_in = sem("constants_loaded")
        par_in = sem("layer_parameters_loaded")
        cache_k_in, cache_v_in = sem("cache_k_loaded"), sem("cache_v_loaded")
        bias_in = sem("bias_loaded")
        x_in, rows_in = sem("x_loaded"), sem("rows_loaded")
        x_out, new_k_out, new_v_out = sem("x_stored"), sem("new_k_stored"), sem("new_v_stored")
        pe_mod, pe_ext = sem("mod_rows_summed"), sem("mod_columns_summed")
        pe_xT, pe_acc, pe_tp = sem("x_transposed"), sem("projected"), sem("qk_transposed")
        pe_score, pe_pt, pe_pv = sem("scores_ready"), sem("probs_transposed"), sem("values_mixed")
        pe_at = sem("diff_out_transposed")
        pe_gate, pe_br, pe_y = sem("gate_ready"), sem("branch_ready"), sem("y_ready")
        pe_rt, pe_h, pe_e = sem("router_ready"), sem("hidden_ready"), sem("expert_ready")
        a_chain, v_chain, g_chain = sem("act_chain"), sem("dve_chain"), sem("pool_chain")
        a_mod, a_hT, a_copy, a_qk = sem("mod_rows_kept"), sem("hT_ready"), sem("unit_copied"), sem("qk_kept")
        a_exp, a_pt, a_oT, a_sg = sem("exp_ready"), sem("probsT_kept"), sem("diff_oT_kept"), sem("sigmoid_ready")
        a_rt, a_esg = sem("router_sigmoid"), sem("expert_sigmoid")
        a_gs, mrow_out = sem("mod_rows_summed_kept"), sem("mod_rows_stored")
        g_in, g2_in = sem("modulation_rows_loaded"), sem("second_gate_loaded")
        h_out, y_out = [sem("expert_inputs_stored_0"), sem("expert_inputs_stored_1")], [sem("expert_outputs_stored_0"), sem("expert_outputs_stored_1")]
        xg_in = [sem(f"tokens_gathered_{s}") for s in range(3)]
        yt_in = [sem(f"outputs_gathered_{t}") for t in range(NT)]
        a_xg, a_y, a_ln = sem("expert_input_kept"), sem("expert_output_kept"), sem("x_scaled")
        a_w, pe_rank, pe_idx, pe_xg = sem("first_output_weighed"), sem("ranks_counted"), sem("slots_filled"), sem("tokens_transposed")
        v_h2, v_rt, v_hot, v_idx, v_nmr = sem("h2_ready"), sem("chosen_ready"), sem("slot_onehot_ready"), sem("slot_tokens_ready"), sem("mean_ready")
        v_yrow, v_ov = sem("output_rows_ready"), sem("extra_blocks_ready")
        v_mod, v_unit, v_bias, v_max = sem("mod_columns_ready"), sem("unit_normed"), sem("bias_added"), sem("max_ready")
        v_rinv, v_prow, v_oev, v_anorm = sem("rinv_ready"), sem("probs_normed"), sem("o_kept"), sem("diff_out_normed")
        v_sq, v_z, v_G, v_ln = sem("squares_summed"), sem("z_ready"), sem("gate_rows_kept"), sem("x_normed")
        v_lnv, v_he = sem("variance_ready"), sem("expert_hidden_kept")
        v_lam, v_x = sem("lambda_dots"), sem("x_final")
        a_lam = sem("lambda_exps")
        g_rs, g_mb, g_zero = sem("rstd_ready"), sem("bias_masked"), sem("kT_zeroed")
        all_sems = range(sems[0].num, sems[-1].num + 1)

        class Chain:

            def __init__(self, eng):
                self.eng, self.n = eng, {}

            def step(self, ins, s, wait=True):
                ins.then_inc(s, 1)
                self.n[s.num] = self.n.get(s.num, 0) + 1
                if wait:
                    self.eng.wait_ge(s, self.n[s.num])

            def count(self, s):
                return self.n.get(s.num, 0)

        PU = [(br, c, t) for br in range(3) for c in CHUNKS[br] for t in range(NT)]
        QU = [i for i, (br, c, t) in enumerate(PU) if CHUNK_TYPE[c] != "v"]

        def by_dve(c, t):
            return c in (6, 7) or (c in (0, 1) and t < LAT)

        DU = [i for i, (br, c, t) in enumerate(PU) if by_dve(c, t)]
        AU = [i for i, (br, c, t) in enumerate(PU) if not by_dve(c, t) or c == 7]
        CG_ORDER = list(MOD_FIRST) + list(MOD_LATER)

        def copies(n):
            return sum(1 if CHUNK_TYPE[PU[QU[j]][1]] == "q" else 2 for j in range(n))

        NEW_K = [i for i, (br, c, t) in enumerate(PU) if t == CTX and CHUNK_TYPE[c] in ("k", "kv")]
        NEW = [i for i, (br, c, t) in enumerate(PU) if t == CTX and CHUNK_TYPE[c] in ("k", "v", "kv")]

        UN = [(br, i, u) for br in range(3) for i, u in enumerate(units(br))]
        FIRST_UNIT = [0, 5, 15, 25]
        RW = [(g, r) for g in range(len(UN)) for r in range(4)]
        SCORES = [(g, r, m) for g, r in RW for m in range(2 if UN[g][0] == 0 else 1)]
        BIAS = [(g, r) for g, r in RW if UN[g][0] == 1 and UN[g][2][0] == "lat"]
        KS = [(g, j) for g in range(len(UN)) for j in range(len(key_steps(UN[g][0], UN[g][2])))]
        sc_at = {k: i for i, k in enumerate(SCORES)}
        ks_at = {k: i for i, k in enumerate(KS)}
        rw_at = {k: i for i, k in enumerate(RW)}
        bias_at = {k: i for i, k in enumerate(BIAS)}

        def last_ks(g):
            return ks_at[(g, len(key_steps(UN[g][0], UN[g][2])) - 1)]

        def width(br, u, r):
            return 128 if u[0] == "ctx" else 128 * (len(key_tiles(br, r)) + 1)

        def tile_at(br, u, r, kt):
            if u[0] == "ctx":
                return 0
            tiles = key_tiles(br, r)
            return len(tiles) if kt == 5 else kt - tiles[0]

        MB_AT = [0, 256, 640, 1024]

        G_CG = (4, 5, 10, 11)
        COL_CG = [cg for cg in CG_ORDER if cg not in G_CG]
        N_UNITS = len(UN)

        def layer_norm(dve, ch, t, k, n_lnv, n_pow):
            st = lnst[:, 16 * (t % 2):16 * (t % 2) + 16]
            o = 4 * (t % 2)
            for n in range(2):
                ch.step(nc.vector.bn_stats(st[:, 6 * n:6 * n + 6], x[:, t, 512 * n:512 * n + 512]), v_chain)
            ch.step(nc.vector.bn_aggr(st[:, 12:14], st[:, 0:12]), v_chain)
            ch.step(nc.vector.tensor_scalar(small[:, 34 + o:35 + o], st[:, 13:14], LN_EPS, None, ALU.add), v_lnv)
            dve.wait_ge(g_rs, n_pow + n_lnv)
            ch.step(nc.vector.tensor_scalar(st[:, 14:15], st[:, 12:13], small[:, 32 + o:33 + o], -1.0, ALU.mult, ALU.mult), v_nmr)
            dve.wait_ge(a_ln, n_lnv)
            ch.step(nc.vector.tensor_tensor(x[:, t, :], x[:, t, :], rows[:, 2 + k, :], ALU.mult), v_chain)
            ch.step(nc.vector.tensor_tensor(x[:, t, :], x[:, t, :], rows[:, 4 + k, :], ALU.add), v_x)

        def scale_tile(act, ch, t, n):
            act.wait_ge(v_nmr, n)
            ch.step(nc.scalar.activation(x[:, t, :], x[:, t, :], ACT.Identity, scale=small[:, 32 + 4 * (t % 2):33 + 4 * (t % 2)],
                                         bias=lnst[:, 16 * (t % 2) + 14:16 * (t % 2) + 15]), a_ln)

        def scale_power(pool, ch, n, t):
            pool.wait_ge(v_lnv, n)
            o = 4 * (t % 2)
            ch.step(nc.gpsimd.tensor_tensor(small[:, 32 + o:33 + o], small[:, 34 + o:35 + o], half[:, 0:1], ALU.pow), g_rs)


        with nc.Block() as block:
            names = [("ident", ident), ("sel", sel), ("cosT", cosT), ("sinT", sinT),
                     ("mask", mask), ("wr", wr), ("rbias", rbias), ("eidx", eidx), ("iota1", iota1), ("ebase", ebase)]

            @block.sync
            def _(sp):
                sp.dma_start(cs[:], A["cs"]).then_inc(par_in, 16)
                sp.dma_start(x[:], A["x"].rearrange("t p n -> p t n")).then_inc(x_in, 16)
                for n, t in names:
                    sp.dma_start(t[:], A[n]).then_inc(consts_in, 16)
                sp.dma_start(zf[:, 0:256 + 2 * NT], A["counting"]).then_inc(rows_in, 16)
                for lo in range(NE, NE + EXTRA, NT):
                    n = min(NT, NE + EXTRA - lo)
                    sp.dma_start(A["y_rows"][lo:lo + n], A["x"][0:n]).then_inc(y_init, 16)
                sp.wait_ge(x_in, 16)
                sp.wait_ge(consts_in, 16 * len(names))

            @block.gpsimd
            def _(pool):
                nc.gpsimd.memset(half[:], -0.5).then_inc(g_rs, 1)

            @block.scalar
            def _(act):
                act.wait_ge(par_in, 16)
                nc.scalar.activation(hT[:, :, 0:32], cs[:], ACT.Sigmoid).then_inc(a_sg, 1)

            @block.vector
            def _(dve):
                dve.wait_ge(par_in, 16)
                dve.wait_ge(a_sg, 1)
                nc.vector.tensor_tensor(cs[:], cs[:], hT[:, :, 0:32], ALU.mult).then_inc(v_z, 1)
                dve.wait_ge(rows_in, 16)
                nc.vector.tensor_copy(lt[:], zf[:, 0:128]).then_inc(v_z, 1)
                nc.vector.tensor_copy(ones[:], zf[:, 128:256]).then_inc(v_z, 1)
                nc.vector.tensor_copy(tokid[:].rearrange("p t k -> p (t k)"), zf[:, 256:256 + 2 * NT]).then_inc(v_z, 1)

        nc.all_engine_barrier(sems_to_clear=all_sems)

        with nc.Fori(0, DEPTH) as layer:
            with nc.Block() as block:

                @block.sync
                def _(sp):
                    for s in range(SLOTS):
                        sp.dma_start(ring[:, s, :], A["wall"][layer, s]).then_inc(full[s], 16)
                    groups = NP // SLOTS
                    with sp.Fori(1, groups) as g:
                        for s in range(SLOTS):
                            sp.wait_ge(freed, (g - 1) * SLOTS + s + 1)
                            sp.dma_start(ring[:, s, :], A["wall"][layer, g * SLOTS + s]).then_inc(full[s], 16)
                    for i in range(groups * SLOTS, NP):
                        sp.wait_ge(freed, i - SLOTS + 1)
                        sp.dma_start(ring[:, i % SLOTS, :], A["wall"][layer, i]).then_inc(full[i % SLOTS], 16)
                    for i in range(NP - SLOTS, NP):
                        sp.wait_ge(full[i % SLOTS], 16 * (i // SLOTS + 1))

                @block.gpsimd
                def _(pool):
                    ch = Chain(pool)
                    pool.dma_start(par[:], A["par"][layer]).then_inc(par_in, 16)
                    pool.dma_start(A["x_state"].rearrange("t p n -> p t n"), x[:]).then_inc(x_out, 16)
                    pool.wait_ge(pe_xT, KB)
                    pool.wait_ge(x_out, 16)
                    for lo, par_ in ((0, 1), (64, 0)):
                        for sl in range(par_, 8, 2):
                            ch.step(nc.gpsimd.memset(KT[lo:lo + 64, sl, 0:640], 0.0), g_zero)

                    def powers(dst, src):
                        ch.step(nc.gpsimd.tensor_tensor(dst, src, half[:, 0:dst.shape[1]], ALU.pow), g_rs)

                    def masked_bias(h):
                        pool.wait_ge(bias_in, 16 * (h + 1))
                        if h >= 2:
                            pool.wait_ge(v_bias, 4 * (h - 1))
                        for g in range(LAT):
                            tiles = key_tiles(1, g)
                            n, u0 = len(tiles), GW * (tiles[0] - g + 1)
                            o = MB[:, h % 2, MB_AT[g]:MB_AT[g] + 128 * n].rearrange("p (k r c) -> p k r c", k=n, r=ROWS)
                            w = WB[:, :, u0:u0 + GW * n].rearrange("p r (k c) -> p k r c", c=GW)
                            m = mask[:, g, u0:u0 + GW * n].rearrange("p (k c) -> p k c", c=GW).unsqueeze(2).to_broadcast([128, n, ROWS, GW])
                            ch.step(nc.gpsimd.tensor_tensor(o, w, m, ALU.add), g_mb)

                    for br in range(3):
                        ns, vw = (8, 512) if br < 2 else (4, 128)
                        if br:
                            pool.wait_ge(pe_pv, last_ks(FIRST_UNIT[br] - 1) + 1)
                        pool.dma_start(KT[:, 0:ns, 640:768], A["cache_kT"][layer, br][:, 0:ns, :]).then_inc(cache_k_in, 16)
                        pool.dma_start(V[:, 5, 0:vw], A["cache_v"][layer, br][:, 0:vw]).then_inc(cache_v_in, 16)
                        if br == 1:
                            pool.wait_ge(v_prow, 4 * FIRST_UNIT[1])
                            pool.dma_start(WB[:], A["bias"][layer, 0]).then_inc(bias_in, 16)
                            masked_bias(0)
                            pool.dma_start(WB[:], A["bias"][layer, 1]).then_inc(bias_in, 16)
                        for c in CHUNKS[br]:
                            if c in (6, 7):
                                for t in range(NT):
                                    pool.wait_ge(v_sq, 5 + 5 * (c - 6) + t + 1)
                                    nh = 8 if c == 6 else 2
                                    powers(small[:, 8:8 + nh], small[:, 0:nh])
                            i = PU.index((br, c, CTX))
                            typ = CHUNK_TYPE[c]
                            if typ in ("k", "kv"):
                                q = QU.index(i)
                                if i in DU:
                                    pool.wait_ge(v_unit, DU.index(i) + 1)
                                else:
                                    pool.wait_ge(a_copy, AU.index(i) + 1)
                                if typ == "k":
                                    pool.dma_start(OUT[("ak", "bk")[br]][layer], tok[:, q % 2, 0:512]).then_inc(new_k_out, 16)
                                else:
                                    pool.dma_start(OUT["ck"][layer].rearrange("t (h d) -> t h d", h=2),
                                                   tok[:, q % 2, 0:256].rearrange("p (h a d) -> p h a d", h=2, a=2)[:, :, 0, :]).then_inc(new_k_out, 16)
                                pool.wait_ge(new_k_out, 16 * (br + 1))
                            if typ in ("v", "kv"):
                                pool.wait_ge(a_copy, AU.index(i) + 1)
                                pool.dma_start(OUT[("av", "bv", "cv")[br]][layer], V[:, CTX, 0:vw]).then_inc(new_v_out, 16)
                                pool.wait_ge(new_v_out, 16 * (br + 1))
                        n = len(units(br))
                        for ui in range(n + 2):
                            if br == 0 and ui >= 2:
                                pool.wait_ge(v_sq, ui - 1)
                                powers(small[:, 8:12], small[:, 0:4])
                            if br == 1 and ui < 7:
                                masked_bias(ui + 1)
                                if ui < 6:
                                    pool.dma_start(WB[:], A["bias"][layer, ui + 2]).then_inc(bias_in, 16)
                    pool.wait_ge(pe_gate, 2 * KB + 1)
                    pool.dma_start(x[:], A["x_state"].rearrange("t p n -> p t n")).then_inc(x_in, 16)
                    pool.dma_start(rows[:], A["rows"][layer][:, 0:6]).then_inc(rows_in, 16)
                    pool.wait_ge(mrow_out, 16 * len(MOD_LATER))

                    def spread(dst, q, s):
                        for v in range(2):
                            pool.dma_start(dst[:, v, :], A["mrows"][v, q].partition_broadcast(128)).then_inc(s, 16)

                    spread(G1, 0, g_in)
                    pool.dma_start(rowsB[:], A["rows"][layer][:, 6:8]).then_inc(g_in, 16)
                    spread(SH, 1, g_in)
                    spread(SC, 2, g_in)
                    for t in range(NT):
                        scale_power(pool, ch, t + 1, t)

                    def gather(e, s):
                        pool.indirect_dma_start(out=xg[:, s, :], out_offset=None, in_=A["h_rows"],
                                                in_offset=bass.IndirectOffsetOnAxis(ap=idx[:, e:e + 1], axis=0)).then_inc(xg_in[s], 16)

                    pool.wait_ge(h_out[0], 16 * ((NT + 1) // 2))
                    pool.wait_ge(h_out[1], 16 * (NT // 2))
                    for e in range(NE):
                        pool.wait_ge(v_idx, e + 1)
                        if e >= 3:
                            pool.wait_ge(pe_xg, e - 2)
                        gather(e, e % 3)
                    pool.wait_ge(v_h2, NT)
                    spread(G2, 3, g2_in)
                    pool.wait_ge(par_in, 16)
                    for s in (cache_k_in, cache_v_in):
                        pool.wait_ge(s, 48)
                    pool.wait_ge(bias_in, 16 * 8)
                    pool.wait_ge(x_in, 16)
                    pool.wait_ge(rows_in, 16)
                    pool.wait_ge(g_in, 16 * 7)
                    pool.wait_ge(g2_in, 32)
                    for s in range(3):
                        pool.wait_ge(xg_in[s], 16 * len(range(s, NE, 3)))
                    pool.dma_reset(all_sems)

                @block.tensor
                def _(pe):
                    piece, owed, waited = [0], [0], set()

                    def take(kind, j=0):
                        i = piece[0] + j
                        assert PIECES[i][0] == kind, (PIECES[i], kind)
                        if i not in waited:
                            waited.add(i)
                            pe.wait_ge(full[i % SLOTS], 16 * (i // SLOTS + 1))
                        return ring[:, i % SLOTS, :]

                    def used(n):
                        owed[0] += n
                        piece[0] += n

                    def mm(out, w, m, start, stop, frees=True, **kw):
                        ins = nc.tensor.matmul(out, w, m, start=start, stop=stop, **kw)
                        if frees and owed[0]:
                            owed[0] -= 1
                            ins.then_inc(freed, 1)
                        return ins

                    n_cg = [0]

                    def mod_sum(cg):
                        i = n_cg[0]
                        if i:
                            pe.wait_ge(a_mod, i)
                        if cg in MOD_LATER and MOD_LATER.index(cg) in (3, 6):
                            pe.wait_ge(v_oev, FIRST_UNIT[1 if MOD_LATER.index(cg) == 3 else 2])
                        for hf in range(2):
                            w = take("mod", hf).rearrange("p (k n) -> p k n", k=4)
                            for j in range(4):
                                last = mm(ps[32 * j:32 * j + 32, 6, :], cs[:, 4 * hf + j, :], w[:, j, :], hf == 0, hf == 1, frees=hf == 0)
                        last.then_inc(pe_mod, 1)
                        n_cg[0] += 1
                        used(2)

                    def mod_columns(cg):
                        pe.wait_ge(a_mod, n_cg[0])
                        k = n_cg[0] - 1
                        if 0 < k <= 4:
                            pe.wait_ge(v_mod, k)
                        if k > 4:
                            pe.wait_ge(a_gs, k - 4)
                        if cg in MOD_FIRST:
                            for b in range(4):
                                last = mm(ps[:, 7, 2 * b:2 * b + 2], modraw[:, 128 * b:128 * b + 128], sel[:, 0:2], True, True, frees=b < 3)
                        else:
                            last = mm(ps[0:2, 7, :], sel[:, 0:2], modraw[:], True, True, frees=False)
                        last.then_inc(pe_ext, 1)

                    for cg in MOD_FIRST:
                        mod_sum(cg)
                        mod_columns(cg)

                    def transpose_x(first):
                        for k in range(KB):
                            if k >= 2:
                                pe.wait_ge(a_hT, 2 * (first + k - 1))
                            for t in range(NT):
                                last = nc.tensor.transpose(ps[:, 2 * (k % 2) + (t == CTX), 128 * (t % LAT):128 * (t % LAT) + 128],
                                                           x[:, t, 128 * k:128 * k + 128], ident[:])
                            last.then_inc(pe_xT, 1)

                    transpose_x(0)
                    pe.wait_ge(a_hT, 2 * KB)

                    def transpose_unit(q):
                        br, c, t = PU[QU[q]]
                        if QU[q] in DU:
                            pe.wait_ge(v_unit, DU.index(QU[q]) + 1)
                        else:
                            pe.wait_ge(a_copy, AU.index(QU[q]) + 1)
                        if q >= 2:
                            pe.wait_ge(a_qk, copies(q - 1))
                        for b in range(2 if c == 7 else 4):
                            last = nc.tensor.transpose(ps[:, 4 + q % 2, 128 * b:128 * b + 128],
                                                       tok[:, q % 2, 128 * b:128 * b + 128], ident[:])
                        last.then_inc(pe_tp, 1)

                    def project(br):
                        if br:
                            pe.wait_ge(v_z, KB * br)
                        for c in CHUNKS[br]:
                            mod_sum(MOD_LATER[c])
                            for t in range(NT):
                                i = PU.index((br, c, t))
                                if i >= 4:
                                    if i - 4 in DU:
                                        pe.wait_ge(v_unit, DU.index(i - 4) + 1)
                                    if i - 4 in AU:
                                        pe.wait_ge(a_copy, AU.index(i - 4) + 1)
                                w = 512 if c < 7 else 256
                                for k in range(KB):
                                    if c < 7:
                                        wk = take("in", k // 4).rearrange("p (k n) -> p k n", k=4)[:, k % 4, :]
                                    else:
                                        wk = take("in").rearrange("p (k n) -> p k n", k=8)[:, k, :]
                                    last = mm(ps[:, i % 4, 0:w], hT[:, k, 128 * t:128 * t + 128], wk, k == 0, k == KB - 1, frees=k < KB - 1)
                                last.then_inc(pe_acc, 1)
                                if t == 0:
                                    mod_columns(MOD_LATER[c])
                                if i and i - 1 in QU and PU[i - 1][0] == br:
                                    transpose_unit(QU.index(i - 1))
                            used(2 if c < 7 else 1)
                        if i in QU:
                            transpose_unit(QU.index(i))

                    def scores(g, r):
                        br, ui, u = UN[g]
                        for m in range(2 if br == 0 else 1):
                            i = sc_at[(g, r, m)]
                            if i >= 2:
                                gg, rr, _ = SCORES[i - 2]
                                if (gg, rr) in bias_at:
                                    pe.wait_ge(v_bias, bias_at[(gg, rr)] + 1)
                                else:
                                    pe.wait_ge(a_exp, i - 1)
                            b = 2 * (i % 2)
                            hh = (u[1] if u[0] == "lat" else r + 4 * u[1]) + 4 * m
                            slot = hh if br < 2 else 2 * (hh // 4) + hh % 2
                            t = r if u[0] == "lat" else CTX
                            q = QT[:, hh // 2, 128 * t:128 * t + 128]
                            if u[0] == "ctx":
                                last = nc.tensor.matmul(ps[:, b, 0:128], q, KT[:, slot, 512:640], start=True, stop=True)
                            else:
                                tiles = key_tiles(br, r)
                                n = 128 * len(tiles)
                                nc.tensor.matmul(ps[:, b, 0:n], q, KT[:, slot, 128 * tiles[0]:128 * tiles[0] + n], start=True, stop=True)
                                last = nc.tensor.matmul(flat(b, 1024)[:, n:n + 128], q, KT[:, slot, 640:768], start=True, stop=True)
                            last.then_inc(pe_score, 1)

                    def transpose_probs(g, j):
                        br, ui, u = UN[g]
                        i = ks_at[(g, j)]
                        if j == 0:
                            pe.wait_ge(v_prow, 4 * g + 4)
                        if i >= 2:
                            pe.wait_ge(a_pt, i - 1)
                        kt, r0, r1 = key_steps(br, u)[j]
                        for r in range(r0, r1):
                            at = tile_at(br, u, r, kt)
                            last = nc.tensor.transpose(ps[:, 4 + i % 2, 128 * r:128 * r + 128],
                                                       P[:, g % 2, r, 128 * at:128 * at + 128], ident[:])
                        last.then_inc(pe_pt, 1)

                    def mix_values(g, j):
                        br, ui, u = UN[g]
                        i = ks_at[(g, j)]
                        pe.wait_ge(a_pt, i + 1)
                        if j == 0 and g >= 2:
                            pe.wait_ge(v_oev, g - 1)
                            if br == 0:
                                pe.wait_ge(a_oT, g - 1)
                        kt, r0, r1 = key_steps(br, u)[j]
                        n = len(key_steps(br, u))
                        ob = 6 + g % 2
                        if br == 0:
                            for r in range(r0, r1):
                                h = u[1] if u[0] == "lat" else r
                                last = nc.tensor.matmul(ps[:, ob, 128 * r:128 * r + 128], PT[:, i % 3, 128 * r:128 * r + 128],
                                                        V[:, kt, 128 * h:128 * h + 128],
                                                        start=j == 0 and r == 0, stop=j == n - 1, skip_group_check=True)
                        elif u[0] == "ctx":
                            for r in range(4):
                                h = 4 * u[1] + r
                                vh = h if br == 1 else h // 4
                                last = nc.tensor.matmul(ps[64 * (h % 2):64 * (h % 2) + 64, ob, 128 * (r // 2):128 * (r // 2) + 128],
                                                        V[:, kt, 64 * vh:64 * vh + 64], PT[:, i % 3, 128 * r:128 * r + 128],
                                                        start=r < 2, stop=True, skip_group_check=True)
                        else:
                            h = u[1]
                            vh = h if br == 1 else h // 4
                            last = nc.tensor.matmul(ps[64 * (h % 2):64 * (h % 2) + 64, ob, 128 * r0:128 * r1],
                                                    V[:, kt, 64 * vh:64 * vh + 64], PT[:, i % 3, 128 * r0:128 * r1],
                                                    start=j == 0, stop=j == n - 1, skip_group_check=True)
                        last.then_inc(pe_pv, 1)

                    def attend(br):
                        us = units(br)
                        n = len(us)
                        pe.wait_ge(a_qk, copies(len([q for q in QU if PU[q][0] <= br])))
                        pe.wait_ge(a_copy, len([a for a in AU if PU[a][0] <= br]))
                        pe.wait_ge(v_unit, len([a for a in DU if PU[a][0] <= br]))
                        pe.wait_ge(g_zero, 8)
                        pe.wait_ge(cache_k_in, 16 * (br + 1))
                        pe.wait_ge(cache_v_in, 16 * (br + 1))
                        pe.wait_ge(a_mod, n_cg[0])
                        pe.wait_ge(a_gs, n_cg[0] - 4)
                        for ui in range(n + 2):
                            g = FIRST_UNIT[br] + ui
                            for i in range(5):
                                if ui < n and i < 4:
                                    scores(g, i)
                                if 1 <= ui <= n:
                                    steps = len(key_steps(br, us[ui - 1]))
                                    if i < steps:
                                        transpose_probs(g - 1, i)
                                    if 1 <= i <= steps:
                                        mix_values(g - 1, i - 1)
                                if br == 0 and ui >= 2 and i == 3:
                                    pe.wait_ge(v_anorm, g - 1)
                                    for r in range(4):
                                        last = nc.tensor.transpose(ps[:, 6 + g % 2, 128 * r:128 * r + 128],
                                                                   tok[:, g % 2, 128 * r:128 * r + 128], ident[:])
                                    last.then_inc(pe_at, 1)
                            if 1 <= ui <= n and len(key_steps(br, us[ui - 1])) == 5:
                                mix_values(g - 1, 4)

                    def merge(br):
                        for mg in range(2):
                            for gate, mm_ in ((True, 0), (True, 1), (False, 0), (False, 1), (True, 2), (True, 3), (False, 2), (False, 3)):
                                i = 8 * br + 4 * mg + mm_
                                b = 4 * (i % 2)
                                if gate:
                                    if i >= 2:
                                        pe.wait_ge(a_sg, i - 1)
                                    if i == 8 * br + 1:
                                        pe.wait_ge(v_oev, FIRST_UNIT[br + 1])
                                        pe.wait_ge(a_oT, 5)
                                    w = take("gate", mm_ // 2).rearrange("p (k n) -> p k n", k=8)
                                    for k in range(KB):
                                        wk = w[:, k, 128 * (mm_ % 2):128 * (mm_ % 2) + 128]
                                        mm(ps[:, b, :], wk, hT[:, k, 0:512], k == 0, k == KB - 1)
                                        last = mm(ps[:, b + 1, 0:128], wk, hT[:, k, 512:640], k == 0, k == KB - 1, frees=False)
                                    last.then_inc(pe_gate, 1)
                                else:
                                    if i >= 2:
                                        pe.wait_ge(v_z, i - 1)
                                    w = take("br", 2).rearrange("p (k n) -> p k n", k=4)
                                    for k in range(4):
                                        wk = w[:, k, 128 * mm_:128 * mm_ + 128]
                                        mm(ps[:, b + 2, :], wk, oT[:, k, 0:512], k == 0, k == 3)
                                        last = mm(ps[:, b + 3, 0:128], wk, oT[:, k, 512:640], k == 0, k == 3, frees=False)
                                    last.then_inc(pe_br, 1)
                            used(3)

                    for br in range(3):
                        project(br)
                        attend(br)
                        merge(br)

                    def transpose_h2(t):
                        pe.wait_ge(v_h2, t + 1)
                        if t:
                            pe.wait_ge(a_hT, 2 * KB + t)
                        for k in range(KB):
                            last = nc.tensor.transpose(ps[:, 6 + k // 4, 128 * (k % 4):128 * (k % 4) + 128],
                                                       h2[:, t % 2, 128 * k:128 * k + 128], ident[:])
                        last.then_inc(pe_xT, 1)

                    pe.wait_ge(v_z, 3 * KB)
                    for n in range(2):
                        for t in range(NT):
                            i = n * NT + t
                            if i >= 4:
                                pe.wait_ge(v_ln, i - 3)
                            for k in range(KB):
                                w = take("o", k // 4).rearrange("p (k n) -> p k n", k=4)[:, k % 4, :]
                                last = mm(ps[:, i % 4, :], zT[:, k, 128 * t:128 * t + 128], w, k == 0, k == KB - 1, frees=k < KB - 1)
                            last.then_inc(pe_y, 1)
                            if n and t >= 3:
                                transpose_h2(t - 3)
                        used(2)
                    transpose_h2(2)

                    def router(t):
                        pe.wait_ge(a_hT, 2 * KB + t + 1)
                        for k in range(KB):
                            last = mm(ps[:, 5, NE * t:NE * t + NE], hT[:, k, 128 * t:128 * t + 128], wr[:, k, :], k == 0, k == KB - 1,
                                      frees=k < KB - 1)
                        last.then_inc(pe_rt, 1)

                    router(0)
                    router(1)
                    transpose_h2(3)
                    router(2)
                    transpose_h2(4)
                    router(3)
                    router(4)
                    pe.wait_ge(v_rt, 1)
                    nc.tensor.matmul(ps[:, 4, 0:NT * NE], lt[:], selbf[:].rearrange("p t e -> p (t e)"), start=True, stop=True)
                    nc.tensor.matmul(ps[:, 4, 256:256 + NT * NE], ones[:], selbf[:].rearrange("p t e -> p (t e)"),
                                     start=True, stop=True).then_inc(pe_rank, 1)

                    def fill_slots(e):
                        pe.wait_ge(v_hot, e + 1)
                        if e:
                            pe.wait_ge(v_idx, e)
                        for t in range(NT):
                            last = nc.tensor.matmul(ps[:, 6, 0:2], hot[:, e % 2, t, :], tokid[:, t, :], start=t == 0, stop=t == NT - 1)
                        last.then_inc(pe_idx, 1)

                    def transpose_tokens(e):
                        pe.wait_ge(xg_in[e % 3], 16 * (e // 3 + 1))
                        if e:
                            pe.wait_ge(a_xg, e)
                        for k in range(KB):
                            last = nc.tensor.transpose(ps[:, 2 + k // 4, 128 * (k % 4):128 * (k % 4) + 128],
                                                       xg[:, e % 3, 128 * k:128 * k + 128], ident[:])
                        last.then_inc(pe_xg, 1)

                    def hidden(e, j, w):
                        w = w.rearrange("p (k n) -> p k n", k=8)
                        for m in range(2):
                            for k in range(KB):
                                last = mm(ps[:, e % 2, 128 * (2 * j + m):128 * (2 * j + m) + 128], w[:, k, 128 * m:128 * m + 128],
                                          xgT[:, e % 2, k, :], k == 0, k == KB - 1, frees=k < KB - 1)
                        return last

                    def expert_out(e, w):
                        pe.wait_ge(v_he, e + 1)
                        if e:
                            pe.wait_ge(a_y, e)
                        w = w.rearrange("p (m n) -> p m n", m=2)
                        for n in range(2):
                            for m in range(2):
                                last = mm(ps[:, 4 + n, :], he[:, e % 2, m, :], w[:, m, 512 * n:512 * n + 512], m == 0, m == 1, frees=False)
                        last.then_inc(pe_e, 1)

                    for e in range(3):
                        fill_slots(e)
                    transpose_tokens(0)
                    for e in range(NE):
                        pe.wait_ge(a_xg, e + 1)
                        if e >= 2:
                            pe.wait_ge(v_he, e - 1)
                        if e == 0:
                            hidden(e, 0, take("w1"))
                            hidden(e, 1, take("w3", 1)).then_inc(pe_h, 1)
                            used(2)
                        else:
                            hidden(e, 0, take("w1", 1))
                            expert_out(e - 1, take("w2"))
                            used(2)
                            hidden(e, 1, take("w3")).then_inc(pe_h, 1)
                            used(1)
                        if e + 1 < NE:
                            transpose_tokens(e + 1)
                        if e + 3 < NE:
                            fill_slots(e + 3)
                    expert_out(NE - 1, take("w2"))
                    used(1)
                    assert piece[0] == NP

                @block.scalar
                def _(act):
                    ch = Chain(act)
                    act.wait_ge(v_lam, 2)
                    ch.step(nc.scalar.activation(small[:, 2:4], small[:, 0:2], ACT.Exp), a_lam)
                    n_cg = [0]

                    def keep_mod(cg):
                        act.wait_ge(pe_mod, n_cg[0] + 1)
                        ch.step(nc.scalar.copy(modraw[:], ps[:, 6, :]), a_mod)
                        n_cg[0] += 1

                    def store_mod(cg):
                        k = MOD_LATER.index(cg)
                        act.wait_ge(pe_ext, 4 + k + 1)
                        if k >= 2:
                            act.wait_ge(mrow_out, 16 * (k - 1))
                        ch.step(nc.scalar.copy(gsm[0:2, k % 2, :], ps[0:2, 7, :]), a_gs)
                        if k:
                            act.wait_ge(mrow_out, 16 * k)
                        act.dma_start(A["mrows"][:, k // 2, 512 * (k % 2):512 * (k % 2) + 512], gsm[0:2, k % 2, :]).then_inc(mrow_out, 16)

                    for cg in MOD_FIRST:
                        keep_mod(cg)

                    def modulate(first, sc, sh):
                        for k in range(KB):
                            act.wait_ge(pe_xT, first + k + 1)
                            b = 2 * (k % 2)
                            for v, (dst, src) in enumerate(((hT[:, k, 0:512], ps[:, b, :]), (hT[:, k, 512:640], ps[:, b + 1, 0:128]))):
                                ch.step(nc.scalar.activation(dst, src, ACT.Identity, scale=modcol[:, sc + k, v:v + 1],
                                                             bias=modcol[:, sh + k, v:v + 1]), a_hT)

                    act.wait_ge(v_mod, 4)
                    modulate(0, 8, 0)
                    act.wait_ge(x_out, 16)
                    act.wait_ge(pe_xT, KB)

                    def tok_free(q):
                        if q >= 2:
                            act.wait_ge(pe_tp, q - 1)
                            n = len([i for i in NEW_K if i in QU and QU.index(i) <= q - 2])
                            if n:
                                act.wait_ge(new_k_out, 16 * n)

                    def keep_unit(q):
                        br, c, t = PU[QU[q]]
                        act.wait_ge(pe_tp, q + 1)
                        nb = 2 if c == 7 else 4
                        src = ps[:, 4 + q % 2, 0:128 * nb].rearrange("p (b t) -> p b t", b=nb)
                        if CHUNK_TYPE[c] == "q":
                            ch.step(nc.scalar.activation(QT[:, :, 128 * t:128 * t + 128], src, ACT.Copy, scale=HD ** -0.5), a_qk)
                        else:
                            for lo in (0, 64):
                                dst = KT[lo:lo + 64, 0:2 * nb, 128 * t:128 * t + 128].rearrange("p (b a) t -> p b a t", a=2)[:, :, lo // 64, :]
                                ch.step(nc.scalar.copy(dst, src[lo:lo + 64]), a_qk)

                    def project(br):
                        for c in CHUNKS[br]:
                            keep_mod(MOD_LATER[c])
                            for t in range(NT):
                                i = PU.index((br, c, t))
                                if i in AU:
                                    act.wait_ge(pe_acc, i + 1)
                                    if CHUNK_TYPE[c] in ("v", "kv"):
                                        if t == CTX and br:
                                            act.wait_ge(new_v_out, 16 * br)
                                        dst, src = (V[:, t, :], ps[:, i % 4, :]) if c < 7 else (V[:, t, 0:128], ps[:, i % 4, 128:256])
                                    else:
                                        q = QU.index(i)
                                        tok_free(q)
                                        dst, src = tok[:, q % 2, :], ps[:, i % 4, :]
                                    ch.step(nc.scalar.copy(dst, src), a_copy)
                                if t == 0:
                                    store_mod(MOD_LATER[c])
                                if i and i - 1 in QU and PU[i - 1][0] == br:
                                    keep_unit(QU.index(i - 1))
                        if i in QU:
                            keep_unit(QU.index(i))

                    def exps(g, r):
                        br, ui, u = UN[g]
                        w = width(br, u, r)
                        for m in range(2 if br == 0 else 1):
                            i = sc_at[(g, r, m)]
                            act.wait_ge(v_max, i + 1)
                            if m == 0:
                                dst = P[:, g % 2, r, 0:w]
                                if g >= 2:
                                    act.wait_ge(pe_pt, last_ks(g - 2) + 1)
                            else:
                                dst = P1[:, rw_at[(g, r)] % 2, 0:w]
                                if rw_at[(g, r)] >= 2:
                                    act.wait_ge(v_prow, rw_at[(g, r)] - 1)
                            src = dst if (g, r) in bias_at else flat(2 * (i % 2), 1024)[:, 0:w]
                            ch.step(nc.scalar.activation(dst, src, ACT.Exp, bias=nmax[:, i % 16:i % 16 + 1],
                                                         accum_out=rsum[:, i % 16:i % 16 + 1]), a_exp)

                    def keep_probs(g, j):
                        br, ui, u = UN[g]
                        i = ks_at[(g, j)]
                        act.wait_ge(pe_pt, i + 1)
                        if i >= 3:
                            act.wait_ge(pe_pv, i - 2)
                        kt, r0, r1 = key_steps(br, u)[j]
                        ch.step(nc.scalar.copy(PT[:, i % 3, 128 * r0:128 * r1], ps[:, 4 + i % 2, 128 * r0:128 * r1]), a_pt)

                    def attend(br):
                        us = units(br)
                        n = len(us)
                        for ui in range(n + 2):
                            g = FIRST_UNIT[br] + ui
                            for i in range(5):
                                if ui < n and i < 4:
                                    exps(g, i)
                                if 1 <= ui <= n and i < len(key_steps(br, us[ui - 1])):
                                    keep_probs(g - 1, i)
                                if br == 0 and ui >= 2 and i == 3:
                                    act.wait_ge(pe_at, g - 1)
                                    src = ps[:, 6 + g % 2, :]
                                    if ui - 2 < 4:
                                        ch.step(nc.scalar.copy(oT[:, ui - 2, 0:512], src), a_oT)
                                    else:
                                        ch.step(nc.scalar.copy(oT[:, :, 512:640], src.rearrange("p (b t) -> p b t", b=4)), a_oT)

                    for br in range(3):
                        project(br)
                        attend(br)
                        for m in range(KB):
                            i = 8 * br + m
                            act.wait_ge(pe_gate, i + 1)
                            if i >= 2:
                                act.wait_ge(v_z, i - 1)
                            ch.step(nc.scalar.activation(sg[br][:, i % 2, :], flat(4 * (i % 2), 640), ACT.Sigmoid,
                                                         bias=bgate[:, i:i + 1]), a_sg)
                    for t in range(NT):
                        scale_tile(act, ch, t, t + 1)
                        if t >= 1:
                            keep_h2 = t - 1
                            act.wait_ge(v_h2, keep_h2 + 1)
                            act.dma_start(A["h_rows"][128 * keep_h2:128 * keep_h2 + 128, :], h2[:, keep_h2 % 2, :]).then_inc(h_out[keep_h2 % 2], 16)
                            act.wait_ge(pe_xT, KB + keep_h2 + 1)
                            ch.step(nc.scalar.copy(hT[:, :, 128 * keep_h2:128 * keep_h2 + 128], flat(6, 1024).rearrange("p (k t) -> p k t", k=KB)), a_hT)
                    act.wait_ge(v_h2, NT)
                    act.dma_start(A["h_rows"][128 * CTX:TOK, :], h2[:, CTX % 2, :]).then_inc(h_out[CTX % 2], 16)
                    act.wait_ge(pe_xT, KB + NT)
                    ch.step(nc.scalar.copy(hT[:, :, 128 * CTX:TOK], flat(6, 1024).rearrange("p (k t) -> p k t", k=KB)), a_hT)
                    act.wait_ge(pe_rt, NT)
                    ch.step(nc.scalar.activation(route[:, 0].rearrange("p t e -> p (t e)"), ps[:, 5, 0:NT * NE], ACT.Sigmoid), a_rt)

                    def keep_tokens(e):
                        act.wait_ge(pe_xg, e + 1)
                        if e >= 2:
                            act.wait_ge(pe_h, e - 1)
                        ch.step(nc.scalar.copy(xgT[:, e % 2].rearrange("p k t -> p (k t)"), flat(2, 1024)), a_xg)

                    def keep_output(e):
                        act.wait_ge(pe_e, e + 1)
                        if e >= 2:
                            act.wait_ge(y_out[e % 2], 16 * (e // 2))
                        ch.step(nc.scalar.copy(ysb[:, e % 2, :], flat(4, 1024)), a_y)
                        act.dma_start(A["y_rows"][e], ysb[:, e % 2, :]).then_inc(y_out[e % 2], 16)

                    keep_tokens(0)
                    for e in range(NE):
                        if e:
                            keep_output(e - 1)
                        act.wait_ge(pe_h, e + 1)
                        if e:
                            act.wait_ge(v_he, e)
                        ch.step(nc.scalar.activation(sig.rearrange("p m t -> p (m t)"), ps[:, e % 2, 0:256], ACT.Sigmoid), a_esg)
                        if e + 1 < NE:
                            keep_tokens(e + 1)
                    keep_output(NE - 1)
                    for s in range(2):
                        act.wait_ge(y_out[s], 16 * NE // 2)

                @block.vector
                def _(dve):
                    ch = Chain(dve)
                    V_ = nc.vector
                    dve.wait_ge(par_in, 16)
                    lv = lam.rearrange("p (a b n) -> p a b n", a=2, b=2)
                    lp = tmpA[:, 0:128].rearrange("p (a n) -> p a n", a=2)
                    ch.step(V_.tensor_tensor(lp, lv[:, :, 0], lv[:, :, 1], ALU.mult), v_lam)
                    ch.step(V_.reduce_sum(small[:, 0:2], lp, axis=AX.X), v_lam)
                    dve.wait_ge(a_lam, 1)
                    ch.step(V_.tensor_tensor(nlam[:], small[:, 3:4], small[:, 2:3], ALU.subtract), v_chain)
                    ch.step(V_.tensor_tensor(nlam[:], nlam[:], laminit[:, 0:1], ALU.subtract), v_chain)
                    ch.step(V_.tensor_scalar(subln, subln, laminit[:, 1:2], None, ALU.mult), v_chain)

                    def mod_columns(cg):
                        k = MOD_FIRST.index(cg)
                        dve.wait_ge(pe_ext, k + 1)
                        dst = modcol[:, 4 * cg:4 * cg + 4, :]
                        b = bmod[:, 4 * cg:4 * cg + 4].unsqueeze(2).to_broadcast([128, 4, 2])
                        scale = cg in (2, 3)
                        ch.step(V_.tensor_tensor(dst, ps[:, 7, 0:8].rearrange("p (b v) -> p b v", v=2), b, ALU.add), v_chain if scale else v_mod)
                        if scale:
                            ch.step(V_.tensor_scalar(dst, dst, 1.0, None, ALU.add), v_mod)

                    for cg in MOD_FIRST:
                        mod_columns(cg)

                    def rope(dst, src, t, nh, s):
                        c = cosT[:, t, :].unsqueeze(1).to_broadcast([128, nh, HD])
                        sn = sinT[:, t, :].rearrange("p (i b) -> p i b", b=2)
                        sp2 = src.rearrange("p h (i b) -> p h i b", b=2)
                        tb = tmpB[:, 0:HD * nh].rearrange("p (h i b) -> p h i b", h=nh, b=2)
                        ch.step(V_.tensor_tensor(dst, src, c, ALU.mult), v_chain)
                        for a in range(2):
                            sa = sn[:, :, a].unsqueeze(1).to_broadcast([128, nh, HD // 2])
                            ch.step(V_.tensor_tensor(tb[:, :, :, a], sp2[:, :, :, 1 - a], sa, ALU.mult), v_chain)
                        ch.step(V_.tensor_tensor(dst, dst, tb.rearrange("p h i b -> p h (i b)"), ALU.add), s)

                    def mean_squares(n, w):
                        ch.step(V_.tensor_tensor(tmpB[:, 0:n * w], tmpA[:, 0:n * w], tmpA[:, 0:n * w], ALU.mult), v_chain)
                        ch.step(V_.reduce_sum(small[:, 0:n], tmpB[:, 0:n * w].rearrange("p (h d) -> p h d", h=n), axis=AX.X), v_chain)
                        ch.step(V_.tensor_scalar(small[:, 0:n], small[:, 0:n], 1.0 / w, RMS_EPS, ALU.mult, ALU.add), v_sq)
                        dve.wait_ge(g_rs, ch.count(v_sq))
                        a = tmpA[:, 0:n * w].rearrange("p (h d) -> p h d", h=n)
                        ch.step(V_.tensor_tensor(a, a, small[:, 8:8 + n].unsqueeze(2).to_broadcast([128, n, w]), ALU.mult), v_chain)
                        return a

                    def unit(i):
                        br, c, t = PU[i]
                        q = QU.index(i)
                        dve.wait_ge(pe_acc, i + 1)
                        if q >= 2:
                            dve.wait_ge(pe_tp, q - 1)
                            n = len([j for j in NEW_K if QU.index(j) <= q - 2])
                            if n:
                                dve.wait_ge(new_k_out, 16 * n)
                        if c in (0, 1):
                            rope(tok[:, q % 2, :].rearrange("p (h d) -> p h d", d=HD), ps[:, i % 4, :].rearrange("p (h d) -> p h d", d=HD), t, 8, v_unit)
                            return
                        nh = 8 if c == 6 else 2
                        w = (qnw if c == 6 else knw).unsqueeze(1).to_broadcast([128, nh, HD])
                        if c == 7:
                            dve.wait_ge(a_copy, AU.index(i) + 1)
                        ch.step(V_.tensor_copy(tmpA[:, 0:nh * HD], ps[:, i % 4, 0:nh * HD]), v_chain)
                        a = mean_squares(nh, HD)
                        if c == 6:
                            dst = tok[:, q % 2, :].rearrange("p (h d) -> p h d", d=HD)
                        else:
                            both = tok[:, q % 2, 0:256].rearrange("p (h a d) -> p h a d", h=2, a=2)
                            dst = both[:, :, 0, :]
                        if t == CTX:
                            ch.step(V_.tensor_tensor(dst, a, w, ALU.mult), v_unit if c == 6 else v_chain)
                        else:
                            ch.step(V_.tensor_tensor(a, a, w, ALU.mult), v_chain)
                            rope(dst, a, t, nh, v_unit if c == 6 else v_chain)
                        if c == 7:
                            ch.step(V_.tensor_copy(both[:, :, 1, :], dst), v_unit)

                    def project(br):
                        for c in CHUNKS[br]:
                            for t in range(NT):
                                i = PU.index((br, c, t))
                                if i in DU:
                                    unit(i)

                    def maxima(g, r):
                        br, ui, u = UN[g]
                        w = width(br, u, r)
                        for m in range(2 if br == 0 else 1):
                            i = sc_at[(g, r, m)]
                            dve.wait_ge(pe_score, i + 1)
                            src = flat(2 * (i % 2), 1024)[:, 0:w]
                            if (g, r) in bias_at:
                                dve.wait_ge(g_mb, 4 * (u[1] + 1))
                                dve.wait_ge(pe_pt, last_ks(g - 2) + 1)
                                n = w - 128
                                row = P[:, g % 2, r, 0:w]
                                ch.step(V_.tensor_tensor(row[:, 0:n], src[:, 0:n], MB[:, u[1] % 2, MB_AT[r]:MB_AT[r] + n], ALU.add), v_chain)
                                ch.step(V_.tensor_copy(row[:, n:w], src[:, n:w]), v_bias)
                                src = row
                            ch.step(V_.tensor_reduce(nmax[:, i % 16:i % 16 + 1], src, axis=AX.X, op=ALU.max, negate=True), v_max)

                    def finish(g, r):
                        br, ui, u = UN[g]
                        w = width(br, u, r)
                        for m in range(2 if br == 0 else 1):
                            i = sc_at[(g, r, m)]
                            dve.wait_ge(a_exp, i + 1)
                            ch.step(V_.reciprocal(rinv[:, i % 16:i % 16 + 1], rsum[:, i % 16:i % 16 + 1]), v_rinv)
                        if br == 0:
                            p1 = P1[:, rw_at[(g, r)] % 2, 0:w]
                            r1 = rinv[:, i % 16:i % 16 + 1]
                            r0 = rinv[:, (i - 1) % 16:(i - 1) % 16 + 1]
                            ch.step(V_.tensor_scalar(p1, p1, r1, nlam[:], ALU.mult, ALU.mult), v_chain)
                            ch.step(V_.scalar_tensor_tensor(P[:, g % 2, r, 0:w], P[:, g % 2, r, 0:w], r0, p1, ALU.mult, ALU.add), v_prow)
                        else:
                            row = P[:, g % 2, r, 0:w]
                            ch.step(V_.tensor_scalar(row, row, rinv[:, i % 16:i % 16 + 1], None, ALU.mult), v_prow)

                    def output(g):
                        br, ui, u = UN[g]
                        dve.wait_ge(pe_pv, last_ks(g) + 1)
                        src = ps[:, 6 + g % 2, :]
                        if br == 0:
                            if g == 0:
                                dve.wait_ge(new_k_out, 16)
                            ch.step(V_.tensor_copy(tmpA[:], src), v_oev)
                            a = mean_squares(4, 128)
                            if g >= 2:
                                dve.wait_ge(pe_at, g - 1)
                            ch.step(V_.tensor_tensor(tok[:, g % 2, :].rearrange("p (h d) -> p h d", h=4), a,
                                                     subln.unsqueeze(1).to_broadcast([128, 4, 128]), ALU.mult), v_anorm)
                        elif u[0] == "lat":
                            lo = 64 * (u[1] % 2)
                            ch.step(V_.tensor_copy(oT[lo:lo + 64, u[1] // 2, 0:512], src[lo:lo + 64, :]), v_oev)
                        else:
                            ch.step(V_.tensor_copy(oT[:, 2 * u[1]:2 * u[1] + 2, 512:640], src[:, 0:256].rearrange("p (b t) -> p b t", b=2)), v_oev)

                    def attend(br):
                        n = len(units(br))
                        for ui in range(n + 2):
                            g = FIRST_UNIT[br] + ui
                            for i in range(4):
                                if ui < n:
                                    maxima(g, i)
                                if ui < n and i:
                                    finish(g, i - 1)
                                elif ui and ui <= n and i == 0:
                                    finish(g - 1, 3)
                                if ui >= 2 and i == 1:
                                    output(g - 2)

                    for br in range(3):
                        project(br)
                        attend(br)
                        for m in range(KB):
                            i = 8 * br + m
                            dve.wait_ge(a_sg, i + 1)
                            dve.wait_ge(pe_br, i + 1)
                            src = flat(4 * (i % 2) + 2, 640)
                            if br == 0:
                                ch.step(V_.tensor_tensor(zT[:, m, :], sg[br][:, i % 2, :], src, ALU.mult), v_z)
                            else:
                                ch.step(V_.tensor_tensor(prod[br], sg[br][:, i % 2, :], src, ALU.mult), v_chain)
                                ch.step(V_.tensor_tensor(zT[:, m, :], zT[:, m, :], prod[br], ALU.add), v_z)

                    dve.wait_ge(rows_in, 16)
                    dve.wait_ge(g_in, 16 * 7)
                    for v in range(2):
                        ch.step(V_.tensor_tensor(G1[:, v, :], G1[:, v, :], rows[:, 0, :], ALU.add), v_G)
                        ch.step(V_.tensor_tensor(SH[:, v, :], SH[:, v, :], rowsB[:, 0, :], ALU.add), v_G)
                        ch.step(V_.scalar_tensor_tensor(SC[:, v, :], SC[:, v, :], 1.0, rowsB[:, 1, :], ALU.add, ALU.add), v_G)
                    dve.wait_ge(x_in, 16)
                    for n in range(2):
                        for t in range(NT):
                            i = n * NT + t
                            v = int(t == CTX)
                            dve.wait_ge(pe_y, i + 1)
                            cols = slice(512 * n, 512 * n + 512)
                            ch.step(V_.tensor_tensor(yg, ps[:, i % 4, :], G1[:, v, cols], ALU.mult), v_chain)
                            ch.step(V_.scalar_tensor_tensor(x[:, t, cols], x[:, t, cols], ALPHA, yg, ALU.mult, ALU.add), v_ln)
                            if n:
                                layer_norm(dve, ch, t, 0, t + 1, 15)
                                if t >= 2:
                                    dve.wait_ge(h_out[t % 2], 16 * (t // 2))
                                    dve.wait_ge(pe_xT, KB + t - 1)
                                ch.step(V_.tensor_tensor(h2[:, t % 2, :], x[:, t, :], SC[:, v, :], ALU.mult), v_chain)
                                ch.step(V_.tensor_tensor(h2[:, t % 2, :], h2[:, t % 2, :], SH[:, v, :], ALU.add), v_h2)

                    dve.wait_ge(a_rt, 1)
                    def plane(k):
                        return route[:, k]

                    def tiny(k):
                        return route[:, 18 + k // 4, :, 4 * (k % 4):4 * (k % 4) + 4]

                    def op2(dst, a, b, op):
                        ch.step(V_.tensor_tensor(dst, a, b, op), v_chain)

                    def wide(a, n):
                        return a.to_broadcast([128, NT, n])

                    score, selv, m_, val, one, two = (plane(k) for k in range(6))
                    op2(selv, score, rbias[:].unsqueeze(1).to_broadcast([128, NT, NE]), ALU.add)
                    grp = selv.rearrange("p t (g e) -> p t g e", g=4)
                    a, b, c, d = (grp[:, :, :, k] for k in range(4))
                    T = [tiny(k) for k in range(8)]
                    op2(T[0], a, b, ALU.max)
                    op2(T[1], a, b, ALU.min)
                    op2(T[2], c, d, ALU.max)
                    op2(T[3], c, d, ALU.min)
                    op2(T[4], T[0], T[2], ALU.max)
                    op2(T[5], T[0], T[2], ALU.min)
                    op2(T[6], T[1], T[3], ALU.max)
                    op2(T[5], T[5], T[6], ALU.max)
                    op2(T[4], T[4], T[5], ALU.add)

                    def first_best(dst, v, idx, n, tmp, top):
                        ch.step(V_.reduce_max(top, v, axis=AX.X), v_chain)
                        op2(tmp, v, wide(top, n), ALU.is_equal)
                        op2(tmp, tmp, idx.unsqueeze(1).to_broadcast([128, NT, n]), ALU.mult)
                        ch.step(V_.reduce_max(top, tmp, axis=AX.X), v_chain)
                        op2(dst, tmp, wide(top, n), ALU.is_equal)

                    top = T[7][:, :, 0:1]
                    first_best(T[0], T[4], eidx[:, NE - 4:NE], 4, T[1], top)
                    ch.step(V_.tensor_scalar(T[1], T[0], -FAR, FAR, ALU.mult, ALU.add), v_chain)
                    m4 = m_.rearrange("p t (g e) -> p t g e", g=4)
                    op2(m4, grp, T[0].unsqueeze(3).to_broadcast([128, NT, 4, 4]), ALU.mult)
                    op2(m4, m4, T[1].unsqueeze(3).to_broadcast([128, NT, 4, 4]), ALU.add)
                    first_best(one, m_, eidx[:], NE, val, top)
                    ch.step(V_.tensor_scalar(val, one, 3 * FAR, None, ALU.mult), v_chain)
                    op2(m_, m_, val, ALU.add)
                    first_best(two, m_, eidx[:], NE, val, top)
                    both, w_, rank1, rk1, before, er = (plane(k) for k in range(6, 12))
                    ch.step(V_.tensor_tensor(selbf[:], one, two, ALU.add), v_rt)
                    op2(both, one, two, ALU.add)
                    op2(w_, both, score, ALU.mult)
                    ch.step(V_.reduce_sum(top, w_, axis=AX.X), v_chain)
                    ch.step(V_.reciprocal(top, top), v_chain)
                    op2(w_, w_, wide(top, NE), ALU.mult)
                    dve.wait_ge(pe_rank, 1)
                    tot = ps[:, 4, 256:256 + NT * NE].rearrange("p (t e) -> p t e", t=NT)
                    ch.step(V_.memset(before[:, 0, :], 1.0), v_chain)
                    for t in range(1, NT):
                        op2(before[:, t, :], before[:, t - 1, :], tot[:, t - 1, :], ALU.add)
                    op2(rank1, before, ps[:, 4, 0:NT * NE].rearrange("p (t e) -> p t e", t=NT), ALU.add)
                    op2(rk1, rank1, both, ALU.mult)

                    def slot_onehot(e):
                        if e >= 2:
                            dve.wait_ge(pe_idx, e - 1)
                        ch.step(V_.tensor_tensor(hot[:, e % 2], rk1[:, :, e:e + 1].to_broadcast([128, NT, 128]),
                                                 iota1[:].unsqueeze(1).to_broadcast([128, NT, 128]), ALU.is_equal), v_hot)

                    def slot_tokens(e):
                        dve.wait_ge(pe_idx, e + 1)
                        ch.step(V_.reduce_sum(small_i[:, 0:1], ps[:, 6, 0:2], axis=AX.X), v_chain)
                        ch.step(V_.tensor_copy(idx[:, e:e + 1], small_i[:, 0:1]), v_idx)

                    slot_onehot(0)
                    slot_onehot(1)
                    slot_tokens(0)
                    slot_onehot(2)
                    slot_tokens(1)
                    slot_onehot(3)
                    slot_tokens(2)
                    n_e, thr = ovq[:, 0, 0:NE], ovq[:, 1, :]
                    flag, pos, pos2, code = (ovq[:, k, :] for k in range(2, 6))
                    op2(n_e, before[:, NT - 1, :], tot[:, NT - 1, :], ALU.add)
                    nb = BLOCKS - 1
                    ch.step(V_.tensor_scalar(thr[:, 0:nb], iota1[:, 0:nb], 128.0, 1.0, ALU.mult, ALU.add), v_chain)
                    op2(flag.rearrange("p (e b) -> p e b", b=nb), n_e.unsqueeze(2).to_broadcast([128, NE, nb]),
                        thr[:, 0:nb].unsqueeze(1).to_broadcast([128, NE, nb]), ALU.is_gt)
                    ch.step(V_.tensor_copy(pos, flag), v_chain)
                    a, b_ = pos, pos2
                    for d in (1, 2, 4, 8, 16, 32):
                        ch.step(V_.tensor_copy(b_[:, 0:d], a[:, 0:d]), v_chain)
                        op2(b_[:, d:64], a[:, d:64], a[:, 0:64 - d], ALU.add)
                        a, b_ = b_, a
                    ch.step(V_.tensor_copy(ovf[:, 0, EXTRA:EXTRA + 1], a[:, 63:64]), v_chain)
                    t0, t1 = ovt[:, 0], ovt[:, 1]
                    op2(t0, a.unsqueeze(1).to_broadcast([128, EXTRA, 64]), iota1[:, 0:EXTRA].unsqueeze(2).to_broadcast([128, EXTRA, 64]), ALU.is_equal)
                    op2(t0, t0, flag.unsqueeze(1).to_broadcast([128, EXTRA, 64]), ALU.mult)
                    c3 = code.rearrange("p (e b) -> p e b", b=nb)
                    for k in range(2):
                        if k == 0:
                            ch.step(V_.tensor_scalar(c3, ebase[:, 1, :].unsqueeze(2).to_broadcast([128, NE, nb]), 3.0, None, ALU.mult), v_chain)
                        else:
                            op2(c3, thr[:, 0:nb].unsqueeze(1).to_broadcast([128, NE, nb]), thr[:, 0:nb].unsqueeze(1).to_broadcast([128, NE, nb]), ALU.max)
                            ch.step(V_.tensor_scalar(c3, c3, -1.0, None, ALU.add), v_chain)
                        op2(t1, t0, code.unsqueeze(1).to_broadcast([128, EXTRA, 64]), ALU.mult)
                        ch.step(V_.reduce_sum(ovf[:, k, 0:EXTRA].unsqueeze(2), t1, axis=AX.X), v_chain)
                    ch.step(V_.tensor_copy(ovi[:], ovf[:, 0]), v_ov)
                    delta = ovq[:, 5, 0:NE]
                    of1 = [v.rearrange("p (e b) -> p e b", b=nb)[:, :, 0] for v in (a, flag)]
                    op2(delta, of1[0], of1[1], ALU.subtract)
                    op2(delta, delta, ebase[:, 1, :], ALU.subtract)
                    ch.step(V_.tensor_scalar(delta, delta, float(NE - 1), 128.0, ALU.add, ALU.mult), v_chain)
                    op2(er, rank1, ebase[:, 0, :].unsqueeze(1).to_broadcast([128, NT, NE]), ALU.add)
                    ch.step(V_.tensor_scalar(rank1, rank1, 128.0, None, ALU.is_gt), v_chain)
                    op2(rank1, rank1, delta.unsqueeze(1).to_broadcast([128, NT, NE]), ALU.mult)
                    op2(er, er, rank1, ALU.add)
                    for k, hot1 in enumerate((one, two)):
                        op2(val, er, hot1, ALU.mult)
                        ch.step(V_.reduce_sum(T[0][:, :, 0:1], val, axis=AX.X), v_chain)
                        ch.step(V_.tensor_copy(yrow[:, k, :], T[0][:, :, 0]), v_chain)
                        op2(val, w_, hot1, ALU.mult)
                        ch.step(V_.reduce_sum(wts[:, k, :].unsqueeze(2), val, axis=AX.X), v_yrow)
                    for e in range(NE):
                        dve.wait_ge(a_esg, e + 1)
                        bank = ps[:, e % 2, :].rearrange("p (j m t) -> p j m t", j=2, m=2)
                        ch.step(V_.tensor_tensor(sig, sig, bank[:, 0], ALU.mult), v_chain)
                        if e >= 2:
                            dve.wait_ge(pe_e, e - 1)
                        ch.step(V_.tensor_tensor(he[:, e % 2], sig, bank[:, 1], ALU.mult), v_he)
                        if e + 3 < NE:
                            if e + 4 < NE:
                                slot_onehot(e + 4)
                            slot_tokens(e + 3)

            n_extra = nc.values_load(ovi[0:1, EXTRA:EXTRA + 1], min_val=0, max_val=EXTRA)
            nc.all_engine_barrier(sems_to_clear=all_sems)
            with nc.If(n_extra > 0):
                with nc.Fori(0, n_extra) as j:
                    with nc.Block() as block:
                        @block.sync
                        def _(sp):
                            first = sp.value_load(ovi[0:1, bass.ds(j, 1)], min_val=0, max_val=3 * (NE - 1))
                            for s in range(3):
                                sp.dma_start(ring[:, s, :], A["wall"][layer, first + (MOE0 + s)]).then_inc(full[s], 16)
                            for s in range(3):
                                sp.wait_ge(full[s], 16)

                        @block.gpsimd
                        def _(pool):
                            pool.wait_ge(v_idx, 1)
                            pool.indirect_dma_start(out=xg[:, 0, :], out_offset=None, in_=A["h_rows"],
                                                    in_offset=bass.IndirectOffsetOnAxis(ap=idx[:, NE:NE + 1], axis=0)).then_inc(xg_in[0], 16)
                            pool.wait_ge(xg_in[0], 16)
                            pool.dma_reset(all_sems)

                        @block.tensor
                        def _(pe):
                            pe.wait_ge(v_hot, 1)
                            for t in range(NT):
                                last = nc.tensor.matmul(ps[:, 6, 0:2], hot[:, 0, t, :], tokid[:, t, :], start=t == 0, stop=t == NT - 1)
                            last.then_inc(pe_idx, 1)
                            pe.wait_ge(xg_in[0], 16)
                            for k in range(KB):
                                last = nc.tensor.transpose(ps[:, 2 + k // 4, 128 * (k % 4):128 * (k % 4) + 128],
                                                           xg[:, 0, 128 * k:128 * k + 128], ident[:])
                            last.then_inc(pe_xg, 1)
                            pe.wait_ge(a_xg, 1)
                            for s in range(2):
                                pe.wait_ge(full[s], 16)
                                w = ring[:, s, :].rearrange("p (k n) -> p k n", k=KB)
                                for m in range(2):
                                    for k in range(KB):
                                        last = nc.tensor.matmul(ps[:, 0, 128 * (2 * s + m):128 * (2 * s + m) + 128], w[:, k, 128 * m:128 * m + 128],
                                                                xgT[:, 0, k, :], start=k == 0, stop=k == KB - 1)
                            last.then_inc(pe_h, 1)
                            pe.wait_ge(v_he, 1)
                            pe.wait_ge(full[2], 16)
                            w = ring[:, 2, :].rearrange("p (m n) -> p m n", m=2)
                            for n in range(2):
                                for m in range(2):
                                    last = nc.tensor.matmul(ps[:, 4 + n, :], he[:, 0, m, :], w[:, m, 512 * n:512 * n + 512], start=m == 0, stop=m == 1)
                            last.then_inc(pe_e, 1)

                        @block.scalar
                        def _(act):
                            act.wait_ge(pe_xg, 1)
                            nc.scalar.copy(xgT[:, 0].rearrange("p k t -> p (k t)"), flat(2, 1024)).then_inc(a_xg, 1)
                            act.wait_ge(pe_h, 1)
                            nc.scalar.activation(sig.rearrange("p m t -> p (m t)"), ps[:, 0, 0:256], ACT.Sigmoid).then_inc(a_esg, 1)
                            act.wait_ge(pe_e, 1)
                            nc.scalar.copy(ysb[:, 0, :], flat(4, 1024)).then_inc(a_y, 1)
                            act.wait_ge(a_y, 1)
                            act.dma_start(A["y_rows"][NE + j], ysb[:, 0, :]).then_inc(y_out[0], 16)
                            act.wait_ge(y_out[0], 16)

                        @block.vector
                        def _(dve):
                            ch = Chain(dve)
                            emask, rk = route[:, 12, 0, :], route[:, 13, :, 0]
                            ch.step(nc.vector.tensor_scalar(emask, ebase[:, 1, :], 3.0, None, ALU.mult), v_chain)
                            ch.step(nc.vector.tensor_scalar(emask, emask, ovf[:, 0, bass.ds(j, 1)], None, ALU.is_equal), v_chain)
                            ch.step(nc.vector.tensor_tensor(route[:, 14], route[:, 9], emask.unsqueeze(1).to_broadcast([128, NT, NE]), ALU.mult), v_chain)
                            ch.step(nc.vector.reduce_sum(rk.unsqueeze(2), route[:, 14], axis=AX.X), v_chain)
                            ch.step(nc.vector.tensor_scalar(rk, rk, ovf[:, 1, bass.ds(j, 1)], None, ALU.subtract), v_chain)
                            ch.step(nc.vector.tensor_tensor(hot[:, 0], rk.unsqueeze(2).to_broadcast([128, NT, 128]),
                                                            iota1[:].unsqueeze(1).to_broadcast([128, NT, 128]), ALU.is_equal), v_hot)
                            dve.wait_ge(pe_idx, 1)
                            ch.step(nc.vector.reduce_sum(small_i[:, 0:1], ps[:, 6, 0:2], axis=AX.X), v_chain)
                            ch.step(nc.vector.tensor_copy(idx[:, NE:NE + 1], small_i[:, 0:1]), v_idx)
                            dve.wait_ge(a_esg, 1)
                            bank = ps[:, 0, :].rearrange("p (j m t) -> p j m t", j=2, m=2)
                            ch.step(nc.vector.tensor_tensor(sig, sig, bank[:, 0], ALU.mult), v_chain)
                            ch.step(nc.vector.tensor_tensor(he[:, 0], sig, bank[:, 1], ALU.mult), v_he)

                    nc.all_engine_barrier(sems_to_clear=all_sems)

            with nc.Block() as block:
                @block.gpsimd
                def _(pool):
                    ch = Chain(pool)
                    y_all = A["y_rows"].rearrange("b p n -> (b p) n")
                    pool.wait_ge(y_init, 16 * len(range(0, EXTRA, NT)))
                    for t in range(NT):
                        for k, Y in enumerate((Y1, Y2)):
                            pool.indirect_dma_start(out=Y[:, t, :], out_offset=None, in_=y_all,
                                                    in_offset=bass.IndirectOffsetOnAxis(ap=yrow[:, k, t:t + 1], axis=0)).then_inc(yt_in[t], 16)
                    for t in range(NT):
                        scale_power(pool, ch, t + 1, t)
                    pool.dma_reset(all_sems)

                @block.scalar
                def _(act):
                    ch = Chain(act)
                    for t in range(NT + 1):
                        if t < NT:
                            act.wait_ge(yt_in[t], 32)
                            ch.step(nc.scalar.activation(Y1[:, t, :], Y1[:, t, :], ACT.Copy, scale=wts[:, 0, t:t + 1]), a_w)
                        if t:
                            scale_tile(act, ch, t - 1, t)

                @block.vector
                def _(dve):
                    ch = Chain(dve)
                    for v in range(2):
                        ch.step(nc.vector.tensor_tensor(G2[:, v, :], G2[:, v, :], rows[:, 1, :], ALU.add), v_G)
                    for t in range(NT):
                        v = int(t == CTX)
                        dve.wait_ge(a_w, t + 1)
                        ch.step(nc.vector.scalar_tensor_tensor(Y1[:, t, :], Y2[:, t, :], wts[:, 1, t:t + 1], Y1[:, t, :], ALU.mult, ALU.add), v_chain)
                        ch.step(nc.vector.tensor_tensor(Y1[:, t, :], Y1[:, t, :], G2[:, v, :], ALU.mult), v_chain)
                        ch.step(nc.vector.scalar_tensor_tensor(x[:, t, :], x[:, t, :], ALPHA, Y1[:, t, :], ALU.mult, ALU.add), v_chain)
                        layer_norm(dve, ch, t, 1, t + 1, 0)

            nc.all_engine_barrier(sems_to_clear=all_sems)

        with nc.Block() as block:
            @block.sync
            def _(sp):
                sp.dma_start(OUT["y"].rearrange("t p n -> p t n"), x[:]).then_inc(x_out, 16)
                sp.wait_ge(x_out, 16)


def positions():
    g, r, c = np.meshgrid(np.arange(LAT), np.arange(ROWS), np.arange(GW), indexing="ij")
    return (r * GRID_W + g * GW + c).ravel()


def rope_tables():
    t = positions()
    n = HD // 4
    freqs = (np.float32(10000.0) ** (-np.arange(n, dtype=np.float32) / np.float32(n))).astype(np.float32)
    ang = np.concatenate([(t // GRID_W).astype(np.float32)[:, None] * freqs,
                          (t % GRID_W).astype(np.float32)[:, None] * freqs], -1)
    cos, sin = np.cos(ang), np.sin(ang)
    c = np.stack([cos, cos], -1).reshape(LAT, 128, HD)
    s = np.stack([-sin, sin], -1).reshape(LAT, 128, HD)
    return (np.ascontiguousarray(a.transpose(1, 0, 2).astype(np.float32)) for a in (c, s))


def window_mask():
    m = np.full((128, LAT, 3 * GW), FAR, np.float32)
    for g in range(LAT):
        for ci in range(GW):
            c = g * GW + ci
            cs = min(max(c - NA_KW // 2, 0), GRID_W - NA_KW)
            for u in range(3 * GW):
                k = GW * (g - 1) + u
                if cs <= k < cs + NA_KW:
                    m[ci::GW, g, u] = 0
    return m


def lay_out(i):
    f = np.float32
    L = DEPTH
    pos = positions()
    a = {}
    a["x"] = np.concatenate([i["x_sample"][0][pos], i["x_prompt"][0]]).reshape(NT, 128, D)
    cs = np.zeros((128, KB, 32), f)
    cs[:, :, 0] = i["c"][0].reshape(KB, 128).T
    cs[:, :, 1] = i["c_ctx"].reshape(KB, 128).T
    a["cs"] = cs
    a["ident"] = np.eye(128, dtype=f)
    sel = np.zeros((128, 2), f)
    for j in range(4):
        for v in range(2):
            sel[32 * j + v, v] = 1
    a["sel"] = sel
    a["cosT"], a["sinT"] = rope_tables()
    a["mask"] = window_mask()
    a["wr"] = i["w_router"].reshape(KB, 128, NE).transpose(1, 0, 2)
    a["rbias"] = np.broadcast_to(i["router_bias"], (128, NE))
    a["eidx"] = np.broadcast_to(np.arange(NE, 0, -1).astype(f), (128, NE))

    a["iota1"] = np.broadcast_to(np.arange(1, 129).astype(f), (128, 128))
    a["ebase"] = np.broadcast_to(np.stack([np.arange(NE) * 128 - 1, np.arange(NE)]).astype(f), (128, 2, NE))
    counting = np.ones((128, 256 + 2 * NT), f)
    counting[:, 0:128] = np.arange(128)[:, None] < np.arange(128)[None]
    for t in range(NT):
        counting[:, 256 + 2 * t] = np.arange(128)
        counting[:, 257 + 2 * t] = 128 * t
    a["counting"] = counting

    def kparts(w, n0, n1):
        w = w[:, n0:n1]
        return w.reshape(-1, 128, n1 - n0).transpose(1, 0, 2).reshape(128, -1)

    wall = np.empty((L, NP, 128, PIECE), f)
    for l in range(L):
        for n, p in enumerate(PIECES):
            if p[0] == "mod":
                w = i["w_mod"][l][512 * p[2]:512 * p[2] + 512]
                wall[l, n] = kparts(w, 512 * p[1], 512 * p[1] + 512)
            elif p[0] == "in":
                if p[1] < 7:
                    wall[l, n] = kparts(i["w_in"][l][512 * p[2]:512 * p[2] + 512], 512 * p[1], 512 * p[1] + 512)
                else:
                    wall[l, n] = kparts(i["w_in"][l], 3584, 3840)
            elif p[0] == "gate":
                n0 = D * p[1] + 256 * p[2]
                wall[l, n] = kparts(i["w_gate"][l], n0, n0 + 256)
            elif p[0] == "br":
                wall[l, n] = kparts(i["w_br"][l, p[1]], 512 * p[2], 512 * p[2] + 512)
            elif p[0] == "o":
                wall[l, n] = kparts(i["w_o"][l][512 * p[2]:512 * p[2] + 512], 512 * p[1], 512 * p[1] + 512)
            elif p[0] == "w1":
                wall[l, n] = kparts(i["moe_w1"][l, p[1]], 0, DE)
            elif p[0] == "w3":
                wall[l, n] = kparts(i["moe_w3"][l, p[1]], 0, DE)
            else:
                wall[l, n] = kparts(i["moe_w2"][l, p[1]], 0, D)
    a["wall"] = wall

    par = np.empty((L, 128, 586), f)
    par[:, :, 0:48] = i["b_mod"].reshape(L, 48, 128).transpose(0, 2, 1)
    par[:, :, 48:72] = i["b_gate"].reshape(L, 24, 128).transpose(0, 2, 1)
    par[:, :, 72:200] = i["a_subln"][:, None, :]
    par[:, :, 200:264] = i["c_qnorm"][:, None, :]
    par[:, :, 264:328] = i["c_knorm"][:, None, :]
    par[:, :, 328:584] = i["lam"].reshape(L, 1, 256)
    for l in range(L):
        init = 0.8 - 0.6 * math.exp(-0.3 * l)
        par[l, :, 584], par[l, :, 585] = init, 1.0 - init
    a["par"] = par
    rows = np.empty((L, 128, 8, D), f)
    rows[:, :, 6] = i["b_mod"][:, None, 3 * D:4 * D]
    rows[:, :, 7] = i["b_mod"][:, None, 4 * D:5 * D]
    rows[:, :, 0] = i["b_mod"][:, None, 2 * D:3 * D]
    rows[:, :, 1] = i["b_mod"][:, None, 5 * D:6 * D]
    rows[:, :, 2:4] = i["ln_g"][:, None]
    rows[:, :, 4:6] = i["ln_b"][:, None]
    a["rows"] = rows

    ck = np.zeros((L, 3, 128, 8, 128), f)
    cv = np.zeros((L, 3, 128, 512), f)
    ka = i["cache_a_k"][0].reshape(L, 128, 8, HD)
    kb = i["cache_b_k"][0]
    kc = i["cache_c_k"][0]
    for h in range(8):
        lo = 64 * (h % 2)
        ck[:, 0, lo:lo + 64, h] = ka[:, :, h].transpose(0, 2, 1)
        ck[:, 1, lo:lo + 64, h] = kb[:, :, h].transpose(0, 2, 1)
        if h < 4:
            ck[:, 2, lo:lo + 64, h] = kc[:, :, h // 2].transpose(0, 2, 1)
    cv[:, 0] = i["cache_a_v"][0].reshape(L, 128, 512)
    cv[:, 1] = i["cache_b_v"][0].reshape(L, 128, 512)
    cv[:, 2, :, 0:128] = i["cache_c_v"][0].reshape(L, 128, 128)
    a["cache_kT"], a["cache_v"] = ck, cv

    pad = np.full((L, 8, 15, 3 * GW + GW + 15), FAR, f)
    pad[:, :, :, 16:47] = i["rpb"]
    bias = np.empty((L, 8, ROWS, GW, ROWS, 3 * GW), f)
    for r in range(ROWS):
        for ci in range(GW):
            bias[:, :, r, ci] = pad[:, :, 7 - r:15 - r, 15 - ci:15 - ci + 3 * GW]
    a["bias"] = bias.reshape(L, 8, 128, ROWS, 3 * GW)
    return {k: np.ascontiguousarray(v) for k, v in a.items()}


def kernel(**inputs):
    import concourse.bacc as bacc
    from concourse.bass_utils import run_bass_kernel_spmd

    arrays = {"in_" + k: v for k, v in lay_out({k: np.asarray(v) for k, v in inputs.items()}).items()}
    f32 = mybir.dt.float32
    nc = bacc.Bacc("TRN2", target_bir_lowering=False, num_devices=1)
    A = {k[3:]: nc.dram_tensor(k, v.shape, f32, kind="ExternalInput").ap() for k, v in arrays.items()}
    A["x_state"] = nc.dram_tensor("x_state", (NT, 128, D), f32, kind="Internal").ap()
    A["h_rows"] = nc.dram_tensor("h_rows", (TOK, D), f32, kind="Internal").ap()
    A["y_rows"] = nc.dram_tensor("y_rows", (NE + EXTRA, 128, D), f32, kind="Internal").ap()
    A["mrows"] = nc.dram_tensor("mrows", (2, 4, D), f32, kind="Internal").ap()
    shapes = {"y": (NT, 128, D), "ak": (DEPTH, 128, 512), "av": (DEPTH, 128, 512), "bk": (DEPTH, 128, 512),
              "bv": (DEPTH, 128, 512), "ck": (DEPTH, 128, 128), "cv": (DEPTH, 128, 128)}
    OUT = {k: nc.dram_tensor("out_" + k, s, f32, kind="ExternalOutput").ap() for k, s in shapes.items()}
    build_kernel(nc, A, OUT)
    r = run_bass_kernel_spmd(nc, [arrays], core_ids=[0]).results[0]
    y = r["out_y"].reshape(TOK, D)
    ys = np.empty((LTOK, D), np.float32)
    ys[positions()] = y[:LTOK]
    return (y[LTOK:][None], ys[None],
            r["out_ak"].reshape(1, DEPTH, 128, 2, 4, HD), r["out_av"].reshape(1, DEPTH, 128, 4, 2 * HD),
            r["out_bk"].reshape(1, DEPTH, 128, 8, HD), r["out_bv"].reshape(1, DEPTH, 128, 8, HD),
            r["out_ck"].reshape(1, DEPTH, 128, 2, HD), r["out_cv"].reshape(1, DEPTH, 128, 2, HD))
```

```python
import math
import numpy as np
import concourse.bass as bass
from concourse import mybir
from contextlib import ExitStack

D = 1024
KB = D // 128
DEPTH = 2
LAT = 4
NT = LAT + 1
CTX = LAT
TOK = NT * 128
LTOK = LAT * 128
HD = 64
NE = 16
DE = 256
GRID_W, ROWS, NA_KW = 64, 8, 16
GW = GRID_W // LAT
LN_EPS, RMS_EPS = 1e-5, 1e-6
ALPHA = (2.0 * DEPTH) ** 0.25
SLOTS = 6
AT_FINISH = (1, 1, 1)
AT_PT = (6, 6, 6)
AT_PV = (8, 8, 8)
AT_OUT = (15, 14, 15)
AT_NORM = (16, 16, 16)
AT_OT = (17, 16, 16)
PIECE = 2048
FAR = -1e30

MOD_FIRST, MOD_LATER = (0, 1, 2, 3), (4, 5, 6, 7, 8, 9, 10, 11)
CHUNKS = {0: (0, 1, 2), 1: (3, 4, 5), 2: (6, 7)}
CHUNK_TYPE = ("q", "k", "v", "q", "k", "v", "q", "kv")


def piece_order():
    order = []
    for br in range(3):
        for c in CHUNKS[br]:
            order += [("mod", MOD_LATER[c], 0), ("mod", MOD_LATER[c], 1)]
            order += [("in", c, 0)] + [("in", c, 1)] * (c < 7)
        for mg in range(2):
            order += [("gate", br, 2 * mg), ("gate", br, 2 * mg + 1), ("br", br, mg)]
    order += [("o", n, h) for n in range(2) for h in range(2)]
    for e in range(NE):
        order += [("w1", e), ("w3", e), ("w2", e)]
    return order


BLOCKS = TOK // 128
EXTRA = (2 * TOK - 1) // 128


MOD_PIECES = [("mod", cg, hf) for cg in MOD_FIRST for hf in range(2)]
PIECES = piece_order()
WALL = MOD_PIECES + PIECES
NM, NP = len(MOD_PIECES), len(PIECES)
AHEAD = 2
POOL_GATES, POOL_OFFSETS = 2, NT - 2
OPEN_AT = NT + 2 - len(MOD_FIRST)
PIECES += [("w1", NE), ("w3", NE), ("w2", NE)]
NB = NE + 1
MOE0 = WALL.index(("w1", 0))


def loads_by(i):
    return i // SLOTS + (i % SLOTS >= AHEAD)


def key_tiles(br, r):
    return list(range(max(r - 1, 0), min(r + 2, LAT))) if br == 1 else list(range(LAT))


def units(br):
    if br == 0:
        return [("lat", h) for h in range(4)] + [("ctx", 0)]
    return [("lat", h) for h in range(8)] + [("ctx", 0), ("ctx", 1)]


def key_steps(br, u):
    if u[0] == "ctx":
        return [(CTX, 0, 4)]
    steps = [(5, 0, LAT)]
    for kt in range(LAT):
        rs = [r for r in range(LAT) if kt in key_tiles(br, r)]
        steps.append((kt, rs[0], rs[-1] + 1))
    return steps


def build_kernel(nc, A, OUT):
    f32, bf16, u32, i32 = mybir.dt.float32, mybir.dt.bfloat16, mybir.dt.uint32, mybir.dt.int32
    ALU, ACT, AX = mybir.AluOpType, mybir.ActivationFunctionType, mybir.AxisListType
    ctx = ExitStack()

    def sb(name, shape):
        return ctx.enter_context(nc.sbuf_tensor(name, shape, f32))

    sems = []

    def sem(name):
        s = ctx.enter_context(nc.semaphore(name))
        sems.append(s)
        return s

    with ctx:
        ring = sb("ring", [128, SLOTS, PIECE])
        hT = sb("hT", [128, KB, TOK])
        zT = sb("zT", [128, KB, TOK])
        ident = sb("ident", [128, 128])
        sel = sb("sel", [128, 2])
        cosT = sb("cosT", [128, LAT, HD])
        sinT = sb("sinT", [128, LAT, HD])
        mask = sb("mask", [128, LAT, 3 * GW])
        cs = sb("cs", [128, KB, 32])
        half = sb("half", [128, 16])
        wr = sb("wr", [128, KB, NE])
        rbias = sb("rbias", [128, NE])
        eidx = sb("eidx", [128, NE])
        par = sb("par", [128, 48 + 24 + 128 + 64 + 64 + 256 + 2])
        bmod, bgate = par[:, 0:48], par[:, 48:72]
        subln, qnw, knw = par[:, 72:200], par[:, 200:264], par[:, 264:328]
        lam, laminit = par[:, 328:584], par[:, 584:586]
        nlam = sb("nlam", [128, 1])
        modcol = sb("modcol", [128, 48, 2])
        gsm = sb("gsm", [128, 2, 512])
        lt = ctx.enter_context(nc.sbuf_tensor("lt", [128, 128], bf16))
        ones = ctx.enter_context(nc.sbuf_tensor("ones", [128, 128], bf16))
        tokid = ctx.enter_context(nc.sbuf_tensor("tokid", [128, NT, 2], bf16))
        selbf = ctx.enter_context(nc.sbuf_tensor("selbf", [128, NT, NE], bf16))
        iota1 = sb("iota1", [128, 128])
        ebase = sb("ebase", [128, 2, NE])
        idx = ctx.enter_context(nc.sbuf_tensor("idx", [128, NE + 1], u32))
        yrow = ctx.enter_context(nc.sbuf_tensor("yrow", [128, 2, NT], u32))
        ovi = ctx.enter_context(nc.sbuf_tensor("ovi", [128, EXTRA + 1], i32))
        small_i = sb("small_i", [128, 2])
        nmax = sb("nmax", [128, 16])
        rsum = sb("rsum", [128, 16])
        rinv = sb("rinv", [128, 32])
        ratio = sb("ratio", [128, 2])
        small = sb("small", [128, 64])

        R = sb("R", [128, 26112])

        def area(start, size):
            return R[:, start:start + size]

        QT = area(0, 2560).rearrange("p (b t) -> p b t", b=4)
        KT = area(2560, 6144).rearrange("p (s t) -> p s t", s=8)
        V = area(8704, 3072).rearrange("p (t e) -> p t e", t=6)
        oT = area(11776, 2560).rearrange("p (b t) -> p b t", b=4)
        P = area(14336, 5120).rearrange("p (s r k) -> p s r k", s=2, r=4)
        PT = area(19456, 1536).rearrange("p (s k) -> p s k", s=3)
        P1 = area(20992, 1280).rearrange("p (s k) -> p s k", s=2)
        MB = area(20992, 3072).rearrange("p (s k) -> p s k", s=2)
        WB = area(25088, 384).rearrange("p (r u) -> p r u", r=ROWS)
        tok = area(24064, 1024).rearrange("p (s k) -> p s k", s=2)
        tmpA, tmpB = area(25088, 512), area(25600, 512)
        modraw = area(19456, 512)
        sg = [area(a, 1280).rearrange("p (s k) -> p s k", s=2) for a in (14336, 14336, 20992)]
        prod = [area(a, 640) for a in (15616, 15616, 22272)]
        x = area(0, 5120).rearrange("p (t n) -> p t n", t=NT)
        rows = area(5120, 6144).rearrange("p (a n) -> p a n", a=6)
        rowsB = area(22912, 2048).rearrange("p (a n) -> p a n", a=2)
        SH = area(14336, 2048).rearrange("p (v n) -> p v n", v=2)
        SC = area(16384, 2048).rearrange("p (v n) -> p v n", v=2)
        G1 = area(18432, 2048).rearrange("p (v n) -> p v n", v=2)
        h2 = area(20992, 2048).rearrange("p (s n) -> p s n", s=2)
        yg = area(25472, 512)
        route = area(11776, 20 * NT * NE).rearrange("p (a t e) -> p a t e", a=20, t=NT)
        lnst = area(13376, 32)
        wts = area(13408, 2 * NT).rearrange("p (k t) -> p k t", k=2)
        ovf = area(13424, 2 * (EXTRA + 1)).rearrange("p (a j) -> p a j", a=2)
        ovq = area(13472, 6 * 64).rearrange("p (a c) -> p a c", a=6)
        ovt = area(16384, 2 * EXTRA * 64).rearrange("p (a j c) -> p a j c", a=2, j=EXTRA)
        G2 = area(14336, 2048).rearrange("p (v n) -> p v n", v=2)
        zf = zT[:].rearrange("p k t -> p (k t)")
        xg = zf[:, 0:3072].rearrange("p (s n) -> p s n", s=3)
        xgT = zf[:, 3072:5120].rearrange("p (s k t) -> p s k t", s=2, k=KB)
        ysb = area(18432, 2048).rearrange("p (s n) -> p s n", s=2)
        he = area(23040, 512).rearrange("p (s m t) -> p s m t", s=2, m=2)
        sig = area(23552, 256).rearrange("p (m t) -> p m t", m=2)
        hot = area(23808, 640).bitcast(bf16).rearrange("p (s t n) -> p s t n", s=2, t=NT)
        Y1 = zf.rearrange("p (t n) -> p t n", t=NT)
        Y2 = area(20480, 5120).rearrange("p (t n) -> p t n", t=NT)

        ps = ctx.enter_context(nc.psum_tensor("ps", [128, 8, 512], f32))

        def flat(bank, n):
            return ps[:, bank:bank + 2, :].rearrange("p b n -> p (b n)")[:, 0:n]

        y_init = ctx.enter_context(nc.semaphore("output_rows_filled"))
        full = [sem(f"piece_loaded_{s}") for s in range(SLOTS)]
        freed = sem("pieces_used")
        consts_in, cs_in, sel_in = sem("constants_loaded"), sem("conditions_loaded"), sem("selector_loaded")
        par_in = sem("layer_parameters_loaded")
        cache_k_in, cache_v_in = sem("cache_k_loaded"), sem("cache_v_loaded")
        bias_in = sem("bias_loaded")
        x_in, rows_in = sem("x_loaded"), sem("rows_loaded")
        x_out, new_k_out, new_v_out = sem("x_stored"), sem("new_k_stored"), sem("new_v_stored")
        pe_mod, pe_ext = sem("mod_rows_summed"), sem("mod_columns_summed")
        pe_xT, pe_acc, pe_tp = sem("x_transposed"), sem("projected"), sem("qk_transposed")
        pe_score, pe_pt, pe_pv = sem("scores_ready"), sem("probs_transposed"), sem("values_mixed")
        pe_at = sem("diff_out_transposed")
        pe_gate, pe_br, pe_y = sem("gate_ready"), sem("branch_ready"), sem("y_ready")
        pe_rt, pe_h, pe_e = sem("router_ready"), sem("hidden_ready"), sem("expert_ready")
        v_chain = sem("dve_chain")
        a_mod, a_hT, a_copy, a_qk = sem("mod_rows_kept"), sem("hT_ready"), sem("unit_copied"), sem("qk_kept")
        a_exp, a_pt, a_oT, a_sg = sem("exp_ready"), sem("probsT_kept"), sem("diff_oT_kept"), sem("sigmoid_ready")
        a_rt, a_esg = sem("router_sigmoid"), sem("expert_sigmoid")
        a_gs, mrow_out = sem("mod_rows_summed_kept"), sem("mod_rows_stored")
        g_in, g2_in = sem("modulation_rows_loaded"), sem("second_gate_loaded")
        h_out, y_out = [sem("expert_inputs_stored_0"), sem("expert_inputs_stored_1")], [sem("expert_outputs_stored_0"), sem("expert_outputs_stored_1")]
        xg_in = [sem(f"tokens_gathered_{s}") for s in range(3)]
        yt_in = [sem(f"outputs_gathered_{t}") for t in range(NT)]
        a_xg, a_y, a_ln = sem("expert_input_kept"), sem("expert_output_kept"), sem("x_scaled")
        a_w, pe_rank, pe_idx, pe_xg = sem("first_output_weighed"), sem("ranks_counted"), sem("slots_filled"), sem("tokens_transposed")
        v_h2, v_rt, v_hot, v_idx, v_nmr = sem("h2_ready"), sem("chosen_ready"), sem("slot_onehot_ready"), sem("slot_tokens_ready"), sem("mean_ready")
        v_yrow, v_ov = sem("output_rows_ready"), sem("extra_blocks_ready")
        v_mod, v_unit, v_bias, v_max = sem("mod_columns_ready"), sem("unit_normed"), sem("bias_added"), sem("max_ready")
        v_rinv, v_prow, v_oev, v_anorm = sem("rinv_ready"), sem("probs_normed"), sem("o_kept"), sem("diff_out_normed")
        v_sq, v_z, v_G, v_ln = sem("squares_summed"), sem("z_ready"), sem("gate_rows_kept"), sem("x_normed")
        v_lnv, v_he = sem("variance_ready"), sem("expert_hidden_kept")
        v_sum, g_gated = sem("outputs_summed"), sem("outputs_gated")
        v_gain, g_x = sem("gain_applied"), sem("offset_added")
        v_lam, v_x = sem("lambda_dots"), sem("x_final")
        a_lam = sem("lambda_exps")
        g_rs, g_mb, g_zero = sem("rstd_ready"), sem("bias_masked"), sem("kT_zeroed")
        all_sems = range(sems[0].num, sems[-1].num + 1)

        class Chain:

            def __init__(self, eng):
                self.eng, self.n = eng, {}

            def step(self, ins, s, wait=True):
                ins.then_inc(s, 1)
                self.n[s.num] = self.n.get(s.num, 0) + 1
                if wait:
                    self.eng.wait_ge(s, self.n[s.num])

            def count(self, s):
                return self.n.get(s.num, 0)

        PU = [(br, c, t) for br in range(3) for c in CHUNKS[br] for t in range(NT)]
        QU = [i for i, (br, c, t) in enumerate(PU) if CHUNK_TYPE[c] != "v"]

        def by_dve(c, t):
            return c in (6, 7) or (c in (0, 1) and t < LAT)

        DU = [i for i, (br, c, t) in enumerate(PU) if by_dve(c, t)]
        AU = [i for i, (br, c, t) in enumerate(PU) if not by_dve(c, t) or c == 7]

        def copies(n):
            return sum(1 if CHUNK_TYPE[PU[QU[j]][1]] == "q" else 2 for j in range(n))

        NEW_K = [i for i, (br, c, t) in enumerate(PU) if t == CTX and CHUNK_TYPE[c] in ("k", "kv")]

        UN = [(br, i, u) for br in range(3) for i, u in enumerate(units(br))]
        FIRST_UNIT = [0, 5, 15, 25]
        RW = [(g, r) for g in range(len(UN)) for r in range(4)]
        SCORES = [(g, r, m) for g, r in RW for m in range(2 if UN[g][0] == 0 else 1)]
        BIAS = [(g, r) for g, r in RW if UN[g][0] == 1 and UN[g][2][0] == "lat"]
        KS = [(g, j) for g in range(len(UN)) for j in range(len(key_steps(UN[g][0], UN[g][2])))]
        sc_at = {k: i for i, k in enumerate(SCORES)}
        ks_at = {k: i for i, k in enumerate(KS)}
        rw_at = {k: i for i, k in enumerate(RW)}
        bias_at = {k: i for i, k in enumerate(BIAS)}

        def last_ks(g):
            return ks_at[(g, len(key_steps(UN[g][0], UN[g][2])) - 1)]


        def turn(br, s, lag, n=0):
            u, i = divmod(s - lag, 5)
            us = units(br)
            if 0 <= u < len(us) and i < (n or len(key_steps(br, us[u]))):
                return FIRST_UNIT[br] + u, i
            return None

        def slots(br):
            return 5 * (len(units(br)) - 1) + AT_OT[br] + 1

        def score_bank(i):
            return i % 4 if UN[SCORES[i][0]][0] == 1 else 2 * (i % 2)

        def score_before(i):
            j = i - (4 if UN[SCORES[i][0]][0] == 1 else 2)
            return j if j >= 0 and UN[SCORES[j][0]][0] == UN[SCORES[i][0]][0] else None

        def width(br, u, r):
            return 128 if u[0] == "ctx" else 128 * (len(key_tiles(br, r)) + 1)

        def cache_first(br, r):
            return br == 1 and r % 2 == 1

        def tile_at(br, u, r, kt):
            if u[0] == "ctx":
                return 0
            tiles = key_tiles(br, r)
            if cache_first(br, r):
                return 0 if kt == 5 else 1 + kt - tiles[0]
            return len(tiles) if kt == 5 else kt - tiles[0]

        MB_AT = [0, 384, 768, 1280]
        MB_ZERO = (256, 1152)
        MB_ROW = [0, 256, 768, 1152]


        def further_ranks(ch, j):
            emask, rk = route[:, 12, 0, :], route[:, 13, :, 0]
            col = slice(j, j + 1) if isinstance(j, int) else j
            ch.step(nc.vector.tensor_scalar(emask, ebase[:, 1, :], 3.0, None, ALU.mult), v_chain)
            ch.step(nc.vector.tensor_scalar(emask, emask, ovf[:, 0, col], None, ALU.is_equal), v_chain)
            ch.step(nc.vector.tensor_tensor(route[:, 14], route[:, 9], emask.unsqueeze(1).to_broadcast([128, NT, NE]), ALU.mult), v_chain)
            ch.step(nc.vector.reduce_sum(rk.unsqueeze(2), route[:, 14], axis=AX.X), v_chain)
            ch.step(nc.vector.tensor_scalar(rk, rk, ovf[:, 1, col], None, ALU.subtract), v_chain)

        def norm_stats(ch, t):
            st = lnst[:, 16 * (t % 2):16 * (t % 2) + 16]
            o = 4 * (t % 2)
            for n in range(2):
                ch.step(nc.vector.bn_stats(st[:, 6 * n:6 * n + 6], x[:, t, 512 * n:512 * n + 512]), v_chain)
            ch.step(nc.vector.bn_aggr(st[:, 12:14], st[:, 0:12]), v_chain)
            ch.step(nc.vector.tensor_scalar(small[:, 34 + o:35 + o], st[:, 13:14], LN_EPS, None, ALU.add), v_lnv)

        def norm_shift(dve, ch, t, n_pow):
            st = lnst[:, 16 * (t % 2):16 * (t % 2) + 16]
            o = 4 * (t % 2)
            dve.wait_ge(g_rs, n_pow + t + 1)
            ch.step(nc.vector.tensor_scalar(st[:, 14:15], st[:, 12:13], small[:, 32 + o:33 + o], -1.0, ALU.mult, ALU.mult), v_nmr)

        def norm_gain(ch, t, k):
            ch.step(nc.vector.tensor_tensor(x[:, t, :], x[:, t, :], rows[:, 2 + k, :], ALU.mult), v_chain)
            ch.step(nc.vector.tensor_tensor(x[:, t, :], x[:, t, :], rows[:, 4 + k, :], ALU.add), v_x)

        def scale_tile(act, ch, t, n):
            act.wait_ge(v_nmr, n)
            ch.step(nc.scalar.activation(x[:, t, :], x[:, t, :], ACT.Identity, scale=small[:, 32 + 4 * (t % 2):33 + 4 * (t % 2)],
                                         bias=lnst[:, 16 * (t % 2) + 14:16 * (t % 2) + 15]), a_ln)

        def scale_power(pool, ch, n, t):
            pool.wait_ge(v_lnv, n)
            o = 4 * (t % 2)
            ch.step(nc.gpsimd.tensor_tensor(small[:, 32 + o:33 + o], small[:, 34 + o:35 + o], half[:, 0:1], ALU.pow), g_rs)


        def open_sp(sp, lay):
            for i in range(NM):
                if i >= SLOTS:
                    sp.wait_ge(freed, i - SLOTS + 1)
                sp.dma_start(ring[:, i % SLOTS, :], A["wall"][lay, i]).then_inc(full[i % SLOTS], 16)
            last_in = {j: max(i for i in range(NM) if i % SLOTS == j) for j in range(AHEAD)}
            for j in sorted(last_in, key=last_in.get):
                sp.wait_ge(freed, last_in[j] + 1)
                sp.dma_start(ring[:, j, :], A["wall"][lay, NM + j]).then_inc(full[j], 16)
            for s in range(SLOTS):
                sp.wait_ge(full[s], 16 * (len(range(s, NM, SLOTS)) + (s < AHEAD)))

        def open_pe(pe):
            for i, cg in enumerate(MOD_FIRST):
                if i:
                    pe.wait_ge(a_mod, i)
                for hf in range(2):
                    n = 2 * i + hf
                    pe.wait_ge(full[n % SLOTS], 16 * (n // SLOTS + 1))
                    w = ring[:, n % SLOTS, :].rearrange("p (k n) -> p k n", k=4)
                    for j in range(4):
                        last = nc.tensor.matmul(ps[32 * j:32 * j + 32, 6, :], cs[:, 4 * hf + j, :], w[:, j, :], start=hf == 0, stop=hf == 1)
                last.then_inc(pe_mod, 1)
                pe.wait_ge(a_mod, i + 1)
                if i:
                    pe.wait_ge(v_mod, i)
                for b in range(4):
                    last = nc.tensor.matmul(ps[:, 7, 2 * b:2 * b + 2], modraw[:, 128 * b:128 * b + 128], sel[:, 0:2], start=True, stop=True)
                    if b in (1, 2):
                        last.then_inc(freed, 1)
                last.then_inc(pe_ext, 1)

        def open_act(act, ch, i):
            act.wait_ge(pe_mod, i + 1)
            ch.step(nc.scalar.copy(modraw[:], ps[:, 6, :]), a_mod)

        def open_dve(dve, ch, i):
            cg = MOD_FIRST[i]
            if i == 0:
                dve.wait_ge(par_in, 16)
            dve.wait_ge(pe_ext, i + 1)
            dst = modcol[:, 4 * cg:4 * cg + 4, :]
            b = bmod[:, 4 * cg:4 * cg + 4].unsqueeze(2).to_broadcast([128, 4, 2])
            scale = cg in (2, 3)
            ch.step(nc.vector.tensor_tensor(dst, ps[:, 7, 0:8].rearrange("p (b v) -> p b v", v=2), b, ALU.add), v_chain if scale else v_mod)
            if scale:
                ch.step(nc.vector.tensor_scalar(dst, dst, 1.0, None, ALU.add), v_mod)

        with nc.Block() as block:
            names = [("ident", ident), ("cosT", cosT), ("sinT", sinT),
                     ("mask", mask), ("wr", wr), ("rbias", rbias), ("eidx", eidx), ("iota1", iota1), ("ebase", ebase)]

            @block.sync
            def _(sp):
                sp.dma_start(cs[:], A["cs"]).then_inc(cs_in, 16)
                sp.dma_start(sel[:], A["sel"]).then_inc(sel_in, 16)
                sp.dma_start(par[:], A["par"][0]).then_inc(par_in, 16)
                open_sp(sp, 0)

            @block.gpsimd
            def _(pool):
                nc.gpsimd.memset(half[:], -0.5).then_inc(g_rs, 1)

            @block.tensor
            def _(pe):
                pe.wait_ge(sel_in, 16)
                pe.wait_ge(v_z, 1)
                open_pe(pe)

            @block.scalar
            def _(act):
                ch = Chain(act)
                act.wait_ge(cs_in, 16)
                nc.scalar.activation(hT[:, :, 0:32], cs[:], ACT.Sigmoid).then_inc(a_sg, 1)
                act.dma_start(zf[:, 0:256 + 2 * NT], A["counting"]).then_inc(rows_in, 16)
                act.dma_start(x[:], A["x"].rearrange("t p n -> p t n")).then_inc(x_in, 16)
                for n, t in names:
                    act.dma_start(t[:], A[n]).then_inc(consts_in, 16)
                for i in range(len(MOD_FIRST)):
                    open_act(act, ch, i)
                act.wait_ge(x_in, 16)
                act.wait_ge(consts_in, 16 * len(names))
                for s in range(SLOTS):
                    act.wait_ge(full[s], 16 * (len(range(s, NM, SLOTS)) + (s < AHEAD)))
                for lo in range(NE + 1, NE + EXTRA, 4):
                    n = min(4, NE + EXTRA - lo)
                    act.dma_start(A["y_rows"][lo:lo + n], A["x"][0:n]).then_inc(y_init, 16)

            @block.vector
            def _(dve):
                ch = Chain(dve)
                dve.wait_ge(cs_in, 16)
                dve.wait_ge(a_sg, 1)
                nc.vector.tensor_tensor(cs[:], cs[:], hT[:, :, 0:32], ALU.mult).then_inc(v_z, 1)
                dve.wait_ge(rows_in, 16)
                nc.vector.tensor_copy(lt[:], zf[:, 0:128]).then_inc(v_z, 1)
                nc.vector.tensor_copy(ones[:], zf[:, 128:256]).then_inc(v_z, 1)
                nc.vector.tensor_copy(tokid[:].rearrange("p t k -> p (t k)"), zf[:, 256:256 + 2 * NT]).then_inc(v_z, 1)
                for i in range(len(MOD_FIRST)):
                    open_dve(dve, ch, i)

        nc.all_engine_barrier(sems_to_clear=all_sems)

        with nc.Fori(0, DEPTH) as layer:
            with nc.Block() as block:

                @block.sync
                def _(sp):
                    for s in range(AHEAD, SLOTS):
                        sp.dma_start(ring[:, s, :], A["wall"][layer, NM + s]).then_inc(full[s], 16)
                    groups = NP // SLOTS
                    with sp.Fori(1, groups) as g:
                        for s in range(SLOTS):
                            sp.wait_ge(freed, (g - 1) * SLOTS + s + 1)
                            sp.dma_start(ring[:, s, :], A["wall"][layer, g * SLOTS + (NM + s)]).then_inc(full[s], 16)
                    for i in range(groups * SLOTS, NP):
                        sp.wait_ge(freed, i - SLOTS + 1)
                        sp.dma_start(ring[:, i % SLOTS, :], A["wall"][layer, NM + i]).then_inc(full[i % SLOTS], 16)
                    sp.wait_ge(v_ov, 1)
                    first = sp.value_load(ovi[0:1, 0:1], min_val=0, max_val=3 * (NE - 1))
                    for i in range(NP, NP + 3):
                        sp.wait_ge(freed, i - SLOTS + 1)
                        sp.dma_start(ring[:, i % SLOTS, :], A["wall"][layer, first + (MOE0 + i - NP)]).then_inc(full[i % SLOTS], 16)
                    for i in range(NP + 3 - SLOTS, NP + 3):
                        sp.wait_ge(full[i % SLOTS], 16 * loads_by(i))

                @block.gpsimd
                def _(pool):
                    ch = Chain(pool)
                    pool.dma_start(A["x_state"].rearrange("t p n -> p t n"), x[:]).then_inc(x_out, 16)
                    pool.wait_ge(pe_xT, KB)
                    pool.wait_ge(x_out, 16)
                    for lo, par_ in ((0, 1), (64, 0)):
                        for sl in range(par_, 8, 2):
                            ch.step(nc.gpsimd.memset(KT[lo:lo + 64, sl, 0:640], 0.0), g_zero)

                    def powers(dst, src):
                        ch.step(nc.gpsimd.tensor_tensor(dst, src, half[:, 0:dst.shape[1]], ALU.pow), g_rs)

                    def masked_bias(h):
                        pool.wait_ge(bias_in, 16 * (h + 1))
                        if h >= 2:
                            pool.wait_ge(v_bias, 4 * (h - 1))
                        for g in range(LAT):
                            tiles = key_tiles(1, g)
                            n, u0 = len(tiles), GW * (tiles[0] - g + 1)
                            o = MB[:, h % 2, MB_AT[g]:MB_AT[g] + 128 * n].rearrange("p (k r c) -> p k r c", k=n, r=ROWS)
                            w = WB[:, :, u0:u0 + GW * n].rearrange("p r (k c) -> p k r c", c=GW)
                            m = mask[:, g, u0:u0 + GW * n].rearrange("p (k c) -> p k c", c=GW).unsqueeze(2).to_broadcast([128, n, ROWS, GW])
                            ch.step(nc.gpsimd.tensor_tensor(o, w, m, ALU.add), g_mb)

                    for br in range(3):
                        ns, vw = (8, 512) if br < 2 else (4, 128)
                        if br:
                            pool.wait_ge(pe_pv, last_ks(FIRST_UNIT[br] - 1) + 1)
                        pool.dma_start(KT[:, 0:ns, 640:768], A["cache_kT"][layer, br][:, 0:ns, :]).then_inc(cache_k_in, 16)
                        pool.dma_start(V[:, 5, 0:vw], A["cache_v"][layer, br][:, 0:vw]).then_inc(cache_v_in, 16)
                        if br == 1:
                            pool.wait_ge(v_prow, 4 * FIRST_UNIT[1])
                            pool.wait_ge(v_anorm, FIRST_UNIT[1])
                            for lo in MB_ZERO:
                                ch.step(nc.gpsimd.memset(MB[:, :, lo:lo + 128], 0.0), g_zero)
                            pool.dma_start(WB[:], A["bias"][layer, 0]).then_inc(bias_in, 16)
                            masked_bias(0)
                            pool.dma_start(WB[:], A["bias"][layer, 1]).then_inc(bias_in, 16)
                        for c in CHUNKS[br]:
                            if c in (6, 7):
                                for t in range(NT):
                                    pool.wait_ge(v_sq, 5 + 5 * (c - 6) + t + 1)
                                    nh = 8 if c == 6 else 2
                                    powers(small[:, 8:8 + nh], small[:, 0:nh])
                            i = PU.index((br, c, CTX))
                            typ = CHUNK_TYPE[c]
                            if typ in ("k", "kv"):
                                q = QU.index(i)
                                if i in DU:
                                    pool.wait_ge(v_unit, DU.index(i) + 1)
                                else:
                                    pool.wait_ge(a_copy, AU.index(i) + 1)
                                if typ == "k":
                                    pool.dma_start(OUT[("ak", "bk")[br]][layer], tok[:, q % 2, 0:512]).then_inc(new_k_out, 16)
                                else:
                                    pool.dma_start(OUT["ck"][layer].rearrange("t (h d) -> t h d", h=2),
                                                   tok[:, q % 2, 0:256].rearrange("p (h a d) -> p h a d", h=2, a=2)[:, :, 0, :]).then_inc(new_k_out, 16)
                                pool.wait_ge(new_k_out, 16 * (br + 1))
                            if typ in ("v", "kv"):
                                pool.wait_ge(a_copy, AU.index(i) + 1)
                                pool.dma_start(OUT[("av", "bv", "cv")[br]][layer], V[:, CTX, 0:vw]).then_inc(new_v_out, 16)
                                pool.wait_ge(new_v_out, 16 * (br + 1))
                        n = len(units(br))
                        for ui in range(n + 2):
                            if br == 0 and ui >= 2:
                                pool.wait_ge(v_sq, ui - 1)
                                powers(small[:, 8:12], small[:, 0:4])
                            if br == 1 and ui < 7:
                                masked_bias(ui + 1)
                                if ui < 6:
                                    pool.dma_start(WB[:], A["bias"][layer, ui + 2]).then_inc(bias_in, 16)
                    pool.wait_ge(pe_gate, 2 * KB + 1)
                    pool.dma_start(x[:], A["x_state"].rearrange("t p n -> p t n")).then_inc(x_in, 16)
                    pool.dma_start(rows[:], A["rows"][layer][:, 0:6]).then_inc(rows_in, 16)
                    pool.wait_ge(mrow_out, 16 * len(MOD_LATER))

                    def spread(dst, q, s):
                        for v in range(2):
                            pool.dma_start(dst[:, v, :], A["mrows"][v, q].partition_broadcast(128)).then_inc(s, 16)

                    spread(G1, 0, g_in)
                    pool.dma_start(rowsB[:], A["rows"][layer][:, 6:8]).then_inc(g_in, 16)
                    spread(SH, 1, g_in)
                    spread(SC, 2, g_in)
                    for t in range(NT):
                        scale_power(pool, ch, t + 1, t)

                    def gather(e, s):
                        pool.indirect_dma_start(out=xg[:, s, :], out_offset=None, in_=A["h_rows"],
                                                in_offset=bass.IndirectOffsetOnAxis(ap=idx[:, e:e + 1], axis=0)).then_inc(xg_in[s], 16)

                    pool.wait_ge(h_out[0], 16 * ((NT + 1) // 2))
                    pool.wait_ge(h_out[1], 16 * (NT // 2))
                    for e in range(NB):
                        pool.wait_ge(v_idx, e + 1)
                        if e >= 3:
                            pool.wait_ge(pe_xg, e - 2)
                        gather(e, e % 3)
                    pool.wait_ge(v_h2, NT)
                    spread(G2, 3, g2_in)
                    for s in (cache_k_in, cache_v_in):
                        pool.wait_ge(s, 48)
                    pool.wait_ge(bias_in, 16 * 8)
                    pool.wait_ge(x_in, 16)
                    pool.wait_ge(rows_in, 16)
                    pool.wait_ge(g_in, 16 * 7)
                    pool.wait_ge(g2_in, 32)
                    for s in range(3):
                        pool.wait_ge(xg_in[s], 16 * len(range(s, NB, 3)))
                    pool.dma_reset(all_sems)

                @block.tensor
                def _(pe):
                    piece, owed, waited = [0], [0], set()

                    def take(kind, j=0):
                        i = piece[0] + j
                        assert PIECES[i][0] == kind, (PIECES[i], kind)
                        if i not in waited and i >= AHEAD:
                            waited.add(i)
                            pe.wait_ge(full[i % SLOTS], 16 * loads_by(i))
                        return ring[:, i % SLOTS, :]

                    def used(n):
                        owed[0] += n
                        piece[0] += n

                    def mm(out, w, m, start, stop, frees=True, **kw):
                        ins = nc.tensor.matmul(out, w, m, start=start, stop=stop, **kw)
                        if frees and owed[0]:
                            owed[0] -= 1
                            ins.then_inc(freed, 1)
                        return ins

                    n_cg = [0]

                    def mod_sum(cg):
                        i = n_cg[0]
                        if i:
                            pe.wait_ge(a_mod, i)
                        if MOD_LATER.index(cg) in (3, 6):
                            pe.wait_ge(v_oev, FIRST_UNIT[1 if MOD_LATER.index(cg) == 3 else 2])
                        for hf in range(2):
                            w = take("mod", hf).rearrange("p (k n) -> p k n", k=4)
                            for j in range(4):
                                last = mm(ps[32 * j:32 * j + 32, 6, :], cs[:, 4 * hf + j, :], w[:, j, :], hf == 0, hf == 1, frees=hf == 0)
                        last.then_inc(pe_mod, 1)
                        n_cg[0] += 1
                        used(2)

                    def mod_rows(cg):
                        pe.wait_ge(a_mod, n_cg[0])
                        if n_cg[0] > 1:
                            pe.wait_ge(a_gs, n_cg[0] - 1)
                        mm(ps[0:2, 7, :], sel[:, 0:2], modraw[:], True, True, frees=False).then_inc(pe_ext, 1)

                    def transpose_x(first):
                        for k in range(KB):
                            if k >= 2:
                                pe.wait_ge(a_hT, 2 * (first + k - 1))
                            for t in range(NT):
                                last = nc.tensor.transpose(ps[:, 2 * (k % 2) + (t == CTX), 128 * (t % LAT):128 * (t % LAT) + 128],
                                                           x[:, t, 128 * k:128 * k + 128], ident[:])
                            last.then_inc(pe_xT, 1)

                    transpose_x(0)
                    pe.wait_ge(a_hT, 2 * KB)

                    def transpose_unit(q):
                        br, c, t = PU[QU[q]]
                        if QU[q] in DU:
                            pe.wait_ge(v_unit, DU.index(QU[q]) + 1)
                        else:
                            pe.wait_ge(a_copy, AU.index(QU[q]) + 1)
                        if q >= 2:
                            pe.wait_ge(a_qk, copies(q - 1))
                        for b in range(2 if c == 7 else 4):
                            last = nc.tensor.transpose(ps[:, 4 + q % 2, 128 * b:128 * b + 128],
                                                       tok[:, q % 2, 128 * b:128 * b + 128], ident[:])
                        last.then_inc(pe_tp, 1)

                    def project(br):
                        if br:
                            pe.wait_ge(v_z, KB * br)
                        for c in CHUNKS[br]:
                            mod_sum(MOD_LATER[c])
                            for t in range(NT):
                                i = PU.index((br, c, t))
                                if i >= 4:
                                    if i - 4 in DU:
                                        pe.wait_ge(v_unit, DU.index(i - 4) + 1)
                                    if i - 4 in AU:
                                        pe.wait_ge(a_copy, AU.index(i - 4) + 1)
                                w = 512 if c < 7 else 256
                                for k in range(KB):
                                    if c < 7:
                                        wk = take("in", k // 4).rearrange("p (k n) -> p k n", k=4)[:, k % 4, :]
                                    else:
                                        wk = take("in").rearrange("p (k n) -> p k n", k=8)[:, k, :]
                                    last = mm(ps[:, i % 4, 0:w], hT[:, k, 128 * t:128 * t + 128], wk, k == 0, k == KB - 1, frees=k < KB - 1)
                                last.then_inc(pe_acc, 1)
                                if t == 0:
                                    mod_rows(MOD_LATER[c])
                                if i and i - 1 in QU and PU[i - 1][0] == br:
                                    transpose_unit(QU.index(i - 1))
                            used(2 if c < 7 else 1)
                        if i in QU:
                            transpose_unit(QU.index(i))

                    def scores(g, r):
                        br, ui, u = UN[g]
                        for m in range(2 if br == 0 else 1):
                            i = sc_at[(g, r, m)]
                            j = score_before(i)
                            if j is not None:
                                gg, rr, _ = SCORES[j]
                                if (gg, rr) in bias_at:
                                    pe.wait_ge(v_bias, bias_at[(gg, rr)] + 1)
                                else:
                                    pe.wait_ge(a_exp, j + 1)
                            b = score_bank(i)
                            hh = (u[1] if u[0] == "lat" else r + 4 * u[1]) + 4 * m
                            slot = hh if br < 2 else 2 * (hh // 4) + hh % 2
                            t = r if u[0] == "lat" else CTX
                            q = QT[:, hh // 2, 128 * t:128 * t + 128]
                            if u[0] == "ctx":
                                last = nc.tensor.matmul(ps[:, b, 0:128], q, KT[:, slot, 512:640], start=True, stop=True)
                            else:
                                tiles = key_tiles(br, r)
                                n = 128 * len(tiles)
                                at, c = (128, 0) if cache_first(br, r) else (0, n)
                                nc.tensor.matmul(ps[:, b, at:at + n], q, KT[:, slot, 128 * tiles[0]:128 * tiles[0] + n], start=True, stop=True)
                                last = nc.tensor.matmul(flat(b, c + 128)[:, c:c + 128], q, KT[:, slot, 640:768], start=True, stop=True)
                            last.then_inc(pe_score, 1)

                    def transpose_probs(g, j):
                        br, ui, u = UN[g]
                        i = ks_at[(g, j)]
                        if j == 0:
                            pe.wait_ge(v_prow, 4 * g + 4)
                        if i >= 2:
                            pe.wait_ge(a_pt, i - 1)
                        kt, r0, r1 = key_steps(br, u)[j]
                        for r in range(r0, r1):
                            at = tile_at(br, u, r, kt)
                            last = nc.tensor.transpose(ps[:, 4 + i % 2, 128 * r:128 * r + 128],
                                                       P[:, g % 2, r, 128 * at:128 * at + 128], ident[:])
                        last.then_inc(pe_pt, 1)

                    def mix_values(g, j):
                        br, ui, u = UN[g]
                        i = ks_at[(g, j)]
                        pe.wait_ge(a_pt, i + 1)
                        if j == 0 and g >= 2:
                            pe.wait_ge(v_oev, g - 1)
                            if br == 0:
                                pe.wait_ge(a_oT, g - 1)
                        kt, r0, r1 = key_steps(br, u)[j]
                        n = len(key_steps(br, u))
                        ob = 6 + g % 2
                        if br == 0:
                            for r in range(r0, r1):
                                h = u[1] if u[0] == "lat" else r
                                last = nc.tensor.matmul(ps[:, ob, 128 * r:128 * r + 128], PT[:, i % 3, 128 * r:128 * r + 128],
                                                        V[:, kt, 128 * h:128 * h + 128],
                                                        start=j == 0 and r == 0, stop=j == n - 1, skip_group_check=True)
                        elif u[0] == "ctx":
                            for r in range(4):
                                h = 4 * u[1] + r
                                vh = h if br == 1 else h // 4
                                last = nc.tensor.matmul(ps[64 * (h % 2):64 * (h % 2) + 64, ob, 128 * (r // 2):128 * (r // 2) + 128],
                                                        V[:, kt, 64 * vh:64 * vh + 64], PT[:, i % 3, 128 * r:128 * r + 128],
                                                        start=r < 2, stop=True, skip_group_check=True)
                        else:
                            h = u[1]
                            vh = h if br == 1 else h // 4
                            last = nc.tensor.matmul(ps[64 * (h % 2):64 * (h % 2) + 64, ob, 128 * r0:128 * r1],
                                                    V[:, kt, 64 * vh:64 * vh + 64], PT[:, i % 3, 128 * r0:128 * r1],
                                                    start=j == 0, stop=j == n - 1, skip_group_check=True)
                        last.then_inc(pe_pv, 1)

                    def attend(br):
                        pe.wait_ge(a_qk, copies(len([q for q in QU if PU[q][0] <= br])))
                        pe.wait_ge(a_copy, len([a for a in AU if PU[a][0] <= br]))
                        pe.wait_ge(v_unit, len([a for a in DU if PU[a][0] <= br]))
                        pe.wait_ge(g_zero, 8)
                        pe.wait_ge(cache_k_in, 16 * (br + 1))
                        pe.wait_ge(cache_v_in, 16 * (br + 1))
                        pe.wait_ge(a_mod, n_cg[0])
                        pe.wait_ge(a_gs, n_cg[0])
                        for s in range(slots(br)):
                            if turn(br, s, 0, 4):
                                scores(*turn(br, s, 0, 4))
                            if turn(br, s, AT_PT[br]):
                                transpose_probs(*turn(br, s, AT_PT[br]))
                            if turn(br, s, AT_PV[br]):
                                mix_values(*turn(br, s, AT_PV[br]))
                            if br == 0 and turn(br, s, AT_OT[br], 1):
                                g, _ = turn(br, s, AT_OT[br], 1)
                                pe.wait_ge(v_anorm, g + 1)
                                for r in range(4):
                                    last = nc.tensor.transpose(ps[:, 6 + g % 2, 128 * r:128 * r + 128],
                                                               tok[:, g % 2, 128 * r:128 * r + 128], ident[:])
                                last.then_inc(pe_at, 1)

                    def merge(br):
                        for mg in range(2):
                            for gate, mm_ in ((True, 0), (True, 1), (False, 0), (False, 1), (True, 2), (True, 3), (False, 2), (False, 3)):
                                i = 8 * br + 4 * mg + mm_
                                b = 4 * (i % 2)
                                if gate:
                                    if i >= 2:
                                        pe.wait_ge(a_sg, i - 1)
                                    if i == 8 * br + 1:
                                        pe.wait_ge(v_oev, FIRST_UNIT[br + 1])
                                        pe.wait_ge(a_oT, 5)
                                    w = take("gate", mm_ // 2).rearrange("p (k n) -> p k n", k=8)
                                    for k in range(KB):
                                        wk = w[:, k, 128 * (mm_ % 2):128 * (mm_ % 2) + 128]
                                        mm(ps[:, b, :], wk, hT[:, k, 0:512], k == 0, k == KB - 1)
                                        last = mm(ps[:, b + 1, 0:128], wk, hT[:, k, 512:640], k == 0, k == KB - 1, frees=False)
                                    last.then_inc(pe_gate, 1)
                                else:
                                    if i >= 2:
                                        pe.wait_ge(v_z, i - 1)
                                    w = take("br", 2).rearrange("p (k n) -> p k n", k=4)
                                    for k in range(4):
                                        wk = w[:, k, 128 * mm_:128 * mm_ + 128]
                                        mm(ps[:, b + 2, :], wk, oT[:, k, 0:512], k == 0, k == 3)
                                        last = mm(ps[:, b + 3, 0:128], wk, oT[:, k, 512:640], k == 0, k == 3, frees=False)
                                    last.then_inc(pe_br, 1)
                            used(3)

                    for br in range(3):
                        project(br)
                        attend(br)
                        merge(br)

                    def transpose_h2(t):
                        pe.wait_ge(v_h2, t + 1)
                        if t:
                            pe.wait_ge(a_hT, 2 * KB + t)
                        for k in range(KB):
                            last = nc.tensor.transpose(ps[:, 6 + k // 4, 128 * (k % 4):128 * (k % 4) + 128],
                                                       h2[:, t % 2, 128 * k:128 * k + 128], ident[:])
                        last.then_inc(pe_xT, 1)

                    pe.wait_ge(v_z, 3 * KB)
                    def router(t):
                        pe.wait_ge(a_hT, 2 * KB + t + 1)
                        for k in range(KB):
                            last = mm(ps[:, 5, NE * t:NE * t + NE], hT[:, k, 128 * t:128 * t + 128], wr[:, k, :], k == 0, k == KB - 1,
                                      frees=k < KB - 1)
                        last.then_inc(pe_rt, 1)

                    for t in range(NT):
                        for n in range(2):
                            i = 2 * t + n
                            if i >= 4:
                                pe.wait_ge(v_ln, i - 3)
                            for k in range(KB):
                                w = take("o", 2 * n + k // 4).rearrange("p (k n) -> p k n", k=4)[:, k % 4, :]
                                last = mm(ps[:, i % 4, :], zT[:, k, 128 * t:128 * t + 128], w, k == 0, k == KB - 1, frees=k < KB - 1)
                            last.then_inc(pe_y, 1)
                        if t:
                            transpose_h2(t - 1)
                            if t > 1:
                                router(t - 2)
                    used(4)
                    router(NT - 2)
                    transpose_h2(NT - 1)
                    router(NT - 1)
                    pe.wait_ge(v_rt, 1)
                    nc.tensor.matmul(ps[:, 4, 0:NT * NE], lt[:], selbf[:].rearrange("p t e -> p (t e)"), start=True, stop=True)
                    nc.tensor.matmul(ps[:, 4, 256:256 + NT * NE], ones[:], selbf[:].rearrange("p t e -> p (t e)"),
                                     start=True, stop=True).then_inc(pe_rank, 1)

                    def fill_slots(e):
                        pe.wait_ge(v_hot, e + 1)
                        if e:
                            pe.wait_ge(v_idx, e)
                        for t in range(NT):
                            last = nc.tensor.matmul(ps[:, 6, 0:2], hot[:, e % 2, t, :], tokid[:, t, :], start=t == 0, stop=t == NT - 1)
                        last.then_inc(pe_idx, 1)

                    def transpose_tokens(e):
                        pe.wait_ge(xg_in[e % 3], 16 * (e // 3 + 1))
                        if e:
                            pe.wait_ge(a_xg, e)
                        for k in range(KB):
                            last = nc.tensor.transpose(ps[:, 2 + k // 4, 128 * (k % 4):128 * (k % 4) + 128],
                                                       xg[:, e % 3, 128 * k:128 * k + 128], ident[:])
                        last.then_inc(pe_xg, 1)

                    def hidden(e, j, w):
                        w = w.rearrange("p (k n) -> p k n", k=8)
                        for m in range(2):
                            for k in range(KB):
                                last = mm(ps[:, e % 2, 128 * (2 * j + m):128 * (2 * j + m) + 128], w[:, k, 128 * m:128 * m + 128],
                                          xgT[:, e % 2, k, :], k == 0, k == KB - 1, frees=k < KB - 1)
                        return last

                    def expert_out(e, w):
                        pe.wait_ge(v_he, e + 1)
                        if e:
                            pe.wait_ge(a_y, e)
                        w = w.rearrange("p (m n) -> p m n", m=2)
                        for n in range(2):
                            for m in range(2):
                                last = mm(ps[:, 4 + n, :], he[:, e % 2, m, :], w[:, m, 512 * n:512 * n + 512], m == 0, m == 1, frees=False)
                        last.then_inc(pe_e, 1)

                    for e in range(3):
                        fill_slots(e)
                    transpose_tokens(0)
                    for e in range(NB):
                        pe.wait_ge(a_xg, e + 1)
                        if e >= 2:
                            pe.wait_ge(v_he, e - 1)
                        hidden(e, 0, take("w1", int(e > 0)))
                        if e + 1 < NB:
                            transpose_tokens(e + 1)
                        if e:
                            expert_out(e - 1, take("w2"))
                            used(2)
                            hidden(e, 1, take("w3")).then_inc(pe_h, 1)
                            used(1)
                        else:
                            hidden(e, 1, take("w3", 1)).then_inc(pe_h, 1)
                            used(2)
                        if e + 3 < NB:
                            fill_slots(e + 3)
                    expert_out(NB - 1, take("w2"))
                    used(1)
                    assert piece[0] == len(PIECES)

                @block.scalar
                def _(act):
                    ch = Chain(act)
                    act.wait_ge(v_lam, 2)
                    ch.step(nc.scalar.activation(small[:, 2:4], small[:, 0:2], ACT.Exp), a_lam)
                    n_cg = [0]

                    def keep_mod(cg):
                        act.wait_ge(pe_mod, n_cg[0] + 1)
                        ch.step(nc.scalar.copy(modraw[:], ps[:, 6, :]), a_mod)
                        n_cg[0] += 1

                    def store_mod(cg):
                        k = MOD_LATER.index(cg)
                        act.wait_ge(pe_ext, k + 1)
                        if k >= 2:
                            act.wait_ge(mrow_out, 16 * (k - 1))
                        ch.step(nc.scalar.copy(gsm[0:2, k % 2, :], ps[0:2, 7, :]), a_gs)
                        if k:
                            act.wait_ge(mrow_out, 16 * k)
                        act.dma_start(A["mrows"][:, k // 2, 512 * (k % 2):512 * (k % 2) + 512], gsm[0:2, k % 2, :]).then_inc(mrow_out, 16)

                    def modulate(first, sc, sh):
                        for k in range(KB):
                            act.wait_ge(pe_xT, first + k + 1)
                            b = 2 * (k % 2)
                            for v, (dst, src) in enumerate(((hT[:, k, 0:512], ps[:, b, :]), (hT[:, k, 512:640], ps[:, b + 1, 0:128]))):
                                ch.step(nc.scalar.activation(dst, src, ACT.Identity, scale=modcol[:, sc + k, v:v + 1],
                                                             bias=modcol[:, sh + k, v:v + 1]), a_hT)

                    modulate(0, 8, 0)
                    act.wait_ge(x_out, 16)
                    act.wait_ge(pe_xT, KB)

                    def tok_free(q):
                        if q >= 2:
                            act.wait_ge(pe_tp, q - 1)
                            n = len([i for i in NEW_K if i in QU and QU.index(i) <= q - 2])
                            if n:
                                act.wait_ge(new_k_out, 16 * n)

                    def keep_unit(q):
                        br, c, t = PU[QU[q]]
                        act.wait_ge(pe_tp, q + 1)
                        nb = 2 if c == 7 else 4
                        src = ps[:, 4 + q % 2, 0:128 * nb].rearrange("p (b t) -> p b t", b=nb)
                        if CHUNK_TYPE[c] == "q":
                            ch.step(nc.scalar.activation(QT[:, :, 128 * t:128 * t + 128], src, ACT.Copy, scale=HD ** -0.5), a_qk)
                        else:
                            for lo in (0, 64):
                                dst = KT[lo:lo + 64, 0:2 * nb, 128 * t:128 * t + 128].rearrange("p (b a) t -> p b a t", a=2)[:, :, lo // 64, :]
                                ch.step(nc.scalar.copy(dst, src[lo:lo + 64]), a_qk)

                    def project(br):
                        for c in CHUNKS[br]:
                            keep_mod(MOD_LATER[c])
                            for t in range(NT):
                                i = PU.index((br, c, t))
                                if i in AU:
                                    act.wait_ge(pe_acc, i + 1)
                                    if CHUNK_TYPE[c] in ("v", "kv"):
                                        if t == CTX and br:
                                            act.wait_ge(new_v_out, 16 * br)
                                        dst, src = (V[:, t, :], ps[:, i % 4, :]) if c < 7 else (V[:, t, 0:128], ps[:, i % 4, 128:256])
                                    else:
                                        q = QU.index(i)
                                        tok_free(q)
                                        dst, src = tok[:, q % 2, :], ps[:, i % 4, :]
                                    ch.step(nc.scalar.copy(dst, src), a_copy)
                                if t == 0:
                                    store_mod(MOD_LATER[c])
                                if i and i - 1 in QU and PU[i - 1][0] == br:
                                    keep_unit(QU.index(i - 1))
                        if i in QU:
                            keep_unit(QU.index(i))

                    def exps(g, r):
                        br, ui, u = UN[g]
                        w = width(br, u, r)
                        for m in range(2 if br == 0 else 1):
                            i = sc_at[(g, r, m)]
                            act.wait_ge(v_max, i + 1)
                            if m == 0:
                                dst = P[:, g % 2, r, 0:w]
                                if g >= 2:
                                    act.wait_ge(pe_pt, last_ks(g - 2) + 1)
                            else:
                                dst = P1[:, rw_at[(g, r)] % 2, 0:w]
                                if rw_at[(g, r)] >= 2:
                                    act.wait_ge(v_prow, rw_at[(g, r)] - 1)
                            src = dst if (g, r) in bias_at else flat(score_bank(i), w)
                            ch.step(nc.scalar.activation(dst, src, ACT.Exp, bias=nmax[:, i % 16:i % 16 + 1],
                                                         accum_out=rsum[:, i % 16:i % 16 + 1]), a_exp)

                    def keep_probs(g, j):
                        br, ui, u = UN[g]
                        i = ks_at[(g, j)]
                        act.wait_ge(pe_pt, i + 1)
                        if i >= 3:
                            act.wait_ge(pe_pv, i - 2)
                        kt, r0, r1 = key_steps(br, u)[j]
                        ch.step(nc.scalar.copy(PT[:, i % 3, 128 * r0:128 * r1], ps[:, 4 + i % 2, 128 * r0:128 * r1]), a_pt)

                    def attend(br):
                        for s in range(slots(br)):
                            if turn(br, s, 0, 4):
                                exps(*turn(br, s, 0, 4))
                            if turn(br, s, AT_PT[br]):
                                keep_probs(*turn(br, s, AT_PT[br]))
                            if br == 0 and turn(br, s, AT_OT[br], 1):
                                g, _ = turn(br, s, AT_OT[br], 1)
                                act.wait_ge(pe_at, g + 1)
                                src = ps[:, 6 + g % 2, :]
                                if g < 4:
                                    ch.step(nc.scalar.copy(oT[:, g, 0:512], src), a_oT)
                                else:
                                    ch.step(nc.scalar.copy(oT[:, :, 512:640], src.rearrange("p (b t) -> p b t", b=4)), a_oT)

                    for br in range(3):
                        project(br)
                        attend(br)
                        for m in range(KB):
                            i = 8 * br + m
                            act.wait_ge(pe_gate, i + 1)
                            if i >= 2:
                                act.wait_ge(v_z, i - 1)
                            ch.step(nc.scalar.activation(sg[br][:, i % 2, :], flat(4 * (i % 2), 640), ACT.Sigmoid,
                                                         bias=bgate[:, i:i + 1]), a_sg)
                    def keep_h2(t):
                        act.wait_ge(v_h2, t + 1)
                        act.dma_start(A["h_rows"][128 * t:128 * t + 128, :], h2[:, t % 2, :]).then_inc(h_out[t % 2], 16)
                        act.wait_ge(pe_xT, KB + t + 1)
                        ch.step(nc.scalar.copy(hT[:, :, 128 * t:128 * t + 128], flat(6, 1024).rearrange("p (k t) -> p k t", k=KB)), a_hT)

                    for t in range(NT):
                        if t:
                            keep_h2(t - 1)
                        scale_tile(act, ch, t, t + 1)
                    keep_h2(NT - 1)
                    act.wait_ge(pe_rt, NT)
                    ch.step(nc.scalar.activation(route[:, 0].rearrange("p t e -> p (t e)"), ps[:, 5, 0:NT * NE], ACT.Sigmoid), a_rt)

                    def keep_tokens(e):
                        act.wait_ge(pe_xg, e + 1)
                        if e >= 2:
                            act.wait_ge(pe_h, e - 1)
                        ch.step(nc.scalar.copy(xgT[:, e % 2].rearrange("p k t -> p (k t)"), flat(2, 1024)), a_xg)

                    def keep_output(e):
                        act.wait_ge(pe_e, e + 1)
                        if e >= 2:
                            act.wait_ge(y_out[e % 2], 16 * (e // 2))
                        ch.step(nc.scalar.copy(ysb[:, e % 2, :], flat(4, 1024)), a_y)
                        act.dma_start(A["y_rows"][e], ysb[:, e % 2, :]).then_inc(y_out[e % 2], 16)

                    keep_tokens(0)
                    for e in range(NB):
                        if e + 1 < NB:
                            keep_tokens(e + 1)
                        if e:
                            keep_output(e - 1)
                        act.wait_ge(pe_h, e + 1)
                        if e:
                            act.wait_ge(v_he, e)
                        ch.step(nc.scalar.activation(sig.rearrange("p m t -> p (m t)"), ps[:, e % 2, 0:256], ACT.Sigmoid), a_esg)
                    keep_output(NB - 1)
                    for s in range(2):
                        act.wait_ge(y_out[s], 16 * len(range(s, NB, 2)))

                @block.vector
                def _(dve):
                    ch = Chain(dve)
                    V_ = nc.vector
                    lv = lam.rearrange("p (a b n) -> p a b n", a=2, b=2)
                    lp = tmpA[:, 0:128].rearrange("p (a n) -> p a n", a=2)
                    ch.step(V_.tensor_tensor(lp, lv[:, :, 0], lv[:, :, 1], ALU.mult), v_lam)
                    ch.step(V_.reduce_sum(small[:, 0:2], lp, axis=AX.X), v_lam)
                    dve.wait_ge(a_lam, 1)
                    ch.step(V_.tensor_tensor(nlam[:], small[:, 3:4], small[:, 2:3], ALU.subtract), v_chain)
                    ch.step(V_.tensor_tensor(nlam[:], nlam[:], laminit[:, 0:1], ALU.subtract), v_chain)
                    ch.step(V_.tensor_scalar(subln, subln, laminit[:, 1:2], None, ALU.mult), v_chain)

                    def rope(dst, src, t, nh, s):
                        c = cosT[:, t, :].unsqueeze(1).to_broadcast([128, nh, HD])
                        sn = sinT[:, t, :].rearrange("p (i b) -> p i b", b=2)
                        sp2 = src.rearrange("p h (i b) -> p h i b", b=2)
                        tb = tmpB[:, 0:HD * nh].rearrange("p (h i b) -> p h i b", h=nh, b=2)
                        ch.step(V_.tensor_tensor(dst, src, c, ALU.mult), v_chain)
                        for a in range(2):
                            sa = sn[:, :, a].unsqueeze(1).to_broadcast([128, nh, HD // 2])
                            ch.step(V_.tensor_tensor(tb[:, :, :, a], sp2[:, :, :, 1 - a], sa, ALU.mult), v_chain)
                        ch.step(V_.tensor_tensor(dst, dst, tb.rearrange("p h i b -> p h (i b)"), ALU.add), s)

                    def mean_squares(n, w):
                        ch.step(V_.tensor_tensor(tmpB[:, 0:n * w], tmpA[:, 0:n * w], tmpA[:, 0:n * w], ALU.mult), v_chain)
                        ch.step(V_.reduce_sum(small[:, 0:n], tmpB[:, 0:n * w].rearrange("p (h d) -> p h d", h=n), axis=AX.X), v_chain)
                        ch.step(V_.tensor_scalar(small[:, 0:n], small[:, 0:n], 1.0 / w, RMS_EPS, ALU.mult, ALU.add), v_sq)

                    def rms_scaled(n, w):
                        dve.wait_ge(g_rs, ch.count(v_sq))
                        a = tmpA[:, 0:n * w].rearrange("p (h d) -> p h d", h=n)
                        ch.step(V_.tensor_tensor(a, a, small[:, 8:8 + n].unsqueeze(2).to_broadcast([128, n, w]), ALU.mult), v_chain)
                        return a

                    def unit(i):
                        br, c, t = PU[i]
                        q = QU.index(i)
                        dve.wait_ge(pe_acc, i + 1)
                        if q >= 2:
                            dve.wait_ge(pe_tp, q - 1)
                            n = len([j for j in NEW_K if QU.index(j) <= q - 2])
                            if n:
                                dve.wait_ge(new_k_out, 16 * n)
                        if c in (0, 1):
                            rope(tok[:, q % 2, :].rearrange("p (h d) -> p h d", d=HD), ps[:, i % 4, :].rearrange("p (h d) -> p h d", d=HD), t, 8, v_unit)
                            return
                        nh = 8 if c == 6 else 2
                        w = (qnw if c == 6 else knw).unsqueeze(1).to_broadcast([128, nh, HD])
                        if c == 7:
                            dve.wait_ge(a_copy, AU.index(i) + 1)
                        ch.step(V_.tensor_copy(tmpA[:, 0:nh * HD], ps[:, i % 4, 0:nh * HD]), v_chain)
                        mean_squares(nh, HD)
                        a = rms_scaled(nh, HD)
                        if c == 6:
                            dst = tok[:, q % 2, :].rearrange("p (h d) -> p h d", d=HD)
                        else:
                            both = tok[:, q % 2, 0:256].rearrange("p (h a d) -> p h a d", h=2, a=2)
                            dst = both[:, :, 0, :]
                        if t == CTX:
                            ch.step(V_.tensor_tensor(dst, a, w, ALU.mult), v_unit if c == 6 else v_chain)
                        else:
                            ch.step(V_.tensor_tensor(a, a, w, ALU.mult), v_chain)
                            rope(dst, a, t, nh, v_unit if c == 6 else v_chain)
                        if c == 7:
                            ch.step(V_.tensor_copy(both[:, :, 1, :], dst), v_unit)

                    def project(br):
                        for c in CHUNKS[br]:
                            for t in range(NT):
                                i = PU.index((br, c, t))
                                if i in DU:
                                    unit(i)

                    def maxima(g, r):
                        br, ui, u = UN[g]
                        w = width(br, u, r)
                        for m in range(2 if br == 0 else 1):
                            i = sc_at[(g, r, m)]
                            dve.wait_ge(pe_score, i + 1)
                            src = flat(score_bank(i), w)
                            if (g, r) in bias_at:
                                dve.wait_ge(g_mb, 4 * (u[1] + 1))
                                dve.wait_ge(pe_pt, last_ks(g - 2) + 1)
                                row = P[:, g % 2, r, 0:w]
                                ch.step(V_.tensor_tensor(row, src, MB[:, u[1] % 2, MB_ROW[r]:MB_ROW[r] + w], ALU.add), v_bias)
                                src = row
                            ch.step(V_.tensor_reduce(nmax[:, i % 16:i % 16 + 1], src, axis=AX.X, op=ALU.max, negate=True), v_max)

                    def finish(g, r):
                        br, ui, u = UN[g]
                        w = width(br, u, r)
                        row = P[:, g % 2, r, 0:w]
                        if br == 0:
                            i = sc_at[(g, r, 0)]
                            k = r % 2
                            dve.wait_ge(a_exp, i + 2)
                            ch.step(V_.reciprocal(rinv[:, i % 32:i % 32 + 2], rsum[:, i % 16:i % 16 + 2]), v_rinv)
                            ch.step(V_.tensor_scalar(ratio[:, k:k + 1], rinv[:, i % 32 + 1:i % 32 + 2], rsum[:, i % 16:i % 16 + 1], nlam[:],
                                                     ALU.mult, ALU.mult), v_chain)
                            ch.step(V_.scalar_tensor_tensor(row, P1[:, rw_at[(g, r)] % 2, 0:w], ratio[:, k:k + 1], row, ALU.mult, ALU.add), v_prow)
                        else:
                            i = sc_at[(g, r, 0)]
                            dve.wait_ge(a_exp, i + 1)
                            ch.step(V_.reciprocal(rinv[:, i % 32:i % 32 + 1], rsum[:, i % 16:i % 16 + 1]), v_rinv)
                            ch.step(V_.tensor_scalar(row, row, rinv[:, i % 32:i % 32 + 1], None, ALU.mult), v_prow)

                    def output(g):
                        br, ui, u = UN[g]
                        dve.wait_ge(pe_pv, last_ks(g) + 1)
                        src = ps[:, 6 + g % 2, :]
                        if br == 0:
                            if g == 0:
                                dve.wait_ge(new_k_out, 16)
                            r0 = rinv[:, 8 * (g % 4):8 * (g % 4) + 8].rearrange("p (r m) -> p r m", m=2)[:, :, 0:1]
                            ch.step(V_.tensor_tensor(tmpA.rearrange("p (r n) -> p r n", r=4), src.rearrange("p (r n) -> p r n", r=4),
                                                     r0.to_broadcast([128, 4, 128]), ALU.mult), v_oev)
                            mean_squares(4, 128)
                        elif u[0] == "lat":
                            lo = 64 * (u[1] % 2)
                            ch.step(V_.tensor_copy(oT[lo:lo + 64, u[1] // 2, 0:512], src[lo:lo + 64, :]), v_oev)
                        else:
                            ch.step(V_.tensor_copy(oT[:, 2 * u[1]:2 * u[1] + 2, 512:640], src[:, 0:256].rearrange("p (b t) -> p b t", b=2)), v_oev)

                    def norm_output(g):
                        a = rms_scaled(4, 128)
                        if g >= 2:
                            dve.wait_ge(pe_at, g - 1)
                        ch.step(V_.tensor_tensor(tok[:, g % 2, :].rearrange("p (h d) -> p h d", h=4), a,
                                                 subln.unsqueeze(1).to_broadcast([128, 4, 128]), ALU.mult), v_anorm)

                    def attend(br):
                        for s in range(slots(br)):
                            if turn(br, s, 0, 4):
                                maxima(*turn(br, s, 0, 4))
                            if turn(br, s, AT_FINISH[br], 4):
                                finish(*turn(br, s, AT_FINISH[br], 4))
                            if turn(br, s, AT_OUT[br], 1):
                                output(turn(br, s, AT_OUT[br], 1)[0])
                            if br == 0 and turn(br, s, AT_NORM[br], 1):
                                norm_output(turn(br, s, AT_NORM[br], 1)[0])

                    for br in range(3):
                        project(br)
                        attend(br)
                        for m in range(KB):
                            i = 8 * br + m
                            dve.wait_ge(a_sg, i + 1)
                            dve.wait_ge(pe_br, i + 1)
                            src = flat(4 * (i % 2) + 2, 640)
                            if br == 0:
                                ch.step(V_.tensor_tensor(zT[:, m, :], sg[br][:, i % 2, :], src, ALU.mult), v_z)
                            else:
                                ch.step(V_.tensor_tensor(prod[br], sg[br][:, i % 2, :], src, ALU.mult), v_chain)
                                ch.step(V_.tensor_tensor(zT[:, m, :], zT[:, m, :], prod[br], ALU.add), v_z)

                    dve.wait_ge(rows_in, 16)
                    dve.wait_ge(g_in, 16 * 7)
                    for v in range(2):
                        ch.step(V_.tensor_tensor(G1[:, v, :], G1[:, v, :], rows[:, 0, :], ALU.add), v_G)
                    for v in range(2):
                        ch.step(V_.tensor_tensor(SH[:, v, :], SH[:, v, :], rowsB[:, 0, :], ALU.add), v_G)
                        ch.step(V_.scalar_tensor_tensor(SC[:, v, :], SC[:, v, :], 1.0, rowsB[:, 1, :], ALU.add, ALU.add), v_G)
                        ch.step(V_.tensor_tensor(h2[:, v, :], rows[:, 4, :], SC[:, v, :], ALU.mult), v_G)
                        ch.step(V_.tensor_tensor(SH[:, v, :], SH[:, v, :], h2[:, v, :], ALU.add), v_G)
                        ch.step(V_.tensor_tensor(SC[:, v, :], SC[:, v, :], rows[:, 2, :], ALU.mult), v_G)
                    dve.wait_ge(x_in, 16)
                    for t in range(NT):
                        v = int(t == CTX)
                        for n in range(2):
                            i = 2 * t + n
                            dve.wait_ge(pe_y, i + 1)
                            cols = slice(512 * n, 512 * n + 512)
                            ch.step(V_.tensor_tensor(yg, ps[:, i % 4, :], G1[:, v, cols], ALU.mult), v_chain)
                            ch.step(V_.scalar_tensor_tensor(x[:, t, cols], x[:, t, cols], ALPHA, yg, ALU.mult, ALU.add), v_ln)
                        norm_stats(ch, t)
                        norm_shift(dve, ch, t, 15)
                        dve.wait_ge(a_ln, t + 1)
                        if t >= 2:
                            dve.wait_ge(h_out[t % 2], 16 * (t // 2))
                            dve.wait_ge(pe_xT, KB + t - 1)
                        ch.step(V_.tensor_tensor(h2[:, t % 2, :], x[:, t, :], SC[:, v, :], ALU.mult), v_chain)
                        ch.step(V_.tensor_tensor(h2[:, t % 2, :], h2[:, t % 2, :], SH[:, v, :], ALU.add), v_h2)

                    dve.wait_ge(a_rt, 1)
                    def plane(k):
                        return route[:, k]

                    def tiny(k):
                        return route[:, 18 + k // 4, :, 4 * (k % 4):4 * (k % 4) + 4]

                    def op2(dst, a, b, op):
                        ch.step(V_.tensor_tensor(dst, a, b, op), v_chain)

                    def wide(a, n):
                        return a.to_broadcast([128, NT, n])

                    score, selv, m_, val, one, two = (plane(k) for k in range(6))
                    op2(selv, score, rbias[:].unsqueeze(1).to_broadcast([128, NT, NE]), ALU.add)
                    grp = selv.rearrange("p t (g e) -> p t g e", g=4)
                    a, b, c, d = (grp[:, :, :, k] for k in range(4))
                    T = [tiny(k) for k in range(8)]
                    op2(T[0], a, b, ALU.max)
                    op2(T[1], a, b, ALU.min)
                    op2(T[2], c, d, ALU.max)
                    op2(T[3], c, d, ALU.min)
                    op2(T[4], T[0], T[2], ALU.max)
                    op2(T[5], T[0], T[2], ALU.min)
                    op2(T[6], T[1], T[3], ALU.max)
                    op2(T[5], T[5], T[6], ALU.max)
                    op2(T[4], T[4], T[5], ALU.add)

                    def first_best(dst, v, idx, n, tmp, top):
                        ch.step(V_.reduce_max(top, v, axis=AX.X), v_chain)
                        op2(tmp, v, wide(top, n), ALU.is_equal)
                        op2(tmp, tmp, idx.unsqueeze(1).to_broadcast([128, NT, n]), ALU.mult)
                        ch.step(V_.reduce_max(top, tmp, axis=AX.X), v_chain)
                        op2(dst, tmp, wide(top, n), ALU.is_equal)

                    top = T[7][:, :, 0:1]
                    first_best(T[0], T[4], eidx[:, NE - 4:NE], 4, T[1], top)
                    ch.step(V_.tensor_scalar(T[1], T[0], -FAR, FAR, ALU.mult, ALU.add), v_chain)
                    m4 = m_.rearrange("p t (g e) -> p t g e", g=4)
                    op2(m4, grp, T[0].unsqueeze(3).to_broadcast([128, NT, 4, 4]), ALU.mult)
                    op2(m4, m4, T[1].unsqueeze(3).to_broadcast([128, NT, 4, 4]), ALU.add)
                    first_best(one, m_, eidx[:], NE, val, top)
                    ch.step(V_.tensor_scalar(val, one, 3 * FAR, None, ALU.mult), v_chain)
                    op2(m_, m_, val, ALU.add)
                    first_best(two, m_, eidx[:], NE, val, top)
                    both, w_, rank1, rk1, before, er = (plane(k) for k in range(6, 12))
                    ch.step(V_.tensor_tensor(selbf[:], one, two, ALU.add), v_rt)
                    op2(both, one, two, ALU.add)
                    ch.step(V_.memset(before[:, 0, :], 1.0), v_chain)
                    dve.wait_ge(pe_rank, 1)
                    tot = ps[:, 4, 256:256 + NT * NE].rearrange("p (t e) -> p t e", t=NT)
                    for t in range(1, NT):
                        op2(before[:, t, :], before[:, t - 1, :], tot[:, t - 1, :], ALU.add)
                    op2(rank1, before, ps[:, 4, 0:NT * NE].rearrange("p (t e) -> p t e", t=NT), ALU.add)
                    op2(rk1, rank1, both, ALU.mult)

                    def slot_onehot(e):
                        if e >= 2:
                            dve.wait_ge(pe_idx, e - 1)
                        if e == NE:
                            further_ranks(ch, 0)
                            ch.step(V_.tensor_tensor(hot[:, e % 2], route[:, 13, :, 0:1].to_broadcast([128, NT, 128]),
                                                     iota1[:].unsqueeze(1).to_broadcast([128, NT, 128]), ALU.is_equal), v_hot)
                            return
                        ch.step(V_.tensor_tensor(hot[:, e % 2], rk1[:, :, e:e + 1].to_broadcast([128, NT, 128]),
                                                 iota1[:].unsqueeze(1).to_broadcast([128, NT, 128]), ALU.is_equal), v_hot)

                    def slot_tokens(e):
                        dve.wait_ge(pe_idx, e + 1)
                        ch.step(V_.reduce_sum(small_i[:, 0:1], ps[:, 6, 0:2], axis=AX.X), v_chain)
                        ch.step(V_.tensor_copy(idx[:, e:e + 1], small_i[:, 0:1]), v_idx)

                    slot_onehot(0)
                    slot_tokens(0)
                    slot_onehot(1)
                    slot_tokens(1)
                    slot_onehot(2)
                    slot_tokens(2)
                    slot_onehot(3)
                    op2(w_, both, score, ALU.mult)
                    ch.step(V_.reduce_sum(top, w_, axis=AX.X), v_chain)
                    ch.step(V_.reciprocal(top, top), v_chain)
                    op2(w_, w_, wide(top, NE), ALU.mult)
                    n_e, thr = ovq[:, 0, 0:NE], ovq[:, 1, :]
                    flag, pos, pos2, code = (ovq[:, k, :] for k in range(2, 6))
                    op2(n_e, before[:, NT - 1, :], tot[:, NT - 1, :], ALU.add)
                    nb = BLOCKS - 1
                    ch.step(V_.tensor_scalar(thr[:, 0:nb], iota1[:, 0:nb], 128.0, 1.0, ALU.mult, ALU.add), v_chain)
                    op2(flag.rearrange("p (e b) -> p e b", b=nb), n_e.unsqueeze(2).to_broadcast([128, NE, nb]),
                        thr[:, 0:nb].unsqueeze(1).to_broadcast([128, NE, nb]), ALU.is_gt)
                    ch.step(V_.tensor_copy(pos, flag), v_chain)
                    a, b_ = pos, pos2
                    for d in (1, 2, 4, 8, 16, 32):
                        ch.step(V_.tensor_copy(b_[:, 0:d], a[:, 0:d]), v_chain)
                        op2(b_[:, d:64], a[:, d:64], a[:, 0:64 - d], ALU.add)
                        a, b_ = b_, a
                    ch.step(V_.tensor_copy(ovf[:, 0, EXTRA:EXTRA + 1], a[:, 63:64]), v_chain)
                    t0, t1 = ovt[:, 0], ovt[:, 1]
                    op2(t0, a.unsqueeze(1).to_broadcast([128, EXTRA, 64]), iota1[:, 0:EXTRA].unsqueeze(2).to_broadcast([128, EXTRA, 64]), ALU.is_equal)
                    op2(t0, t0, flag.unsqueeze(1).to_broadcast([128, EXTRA, 64]), ALU.mult)
                    c3 = code.rearrange("p (e b) -> p e b", b=nb)
                    for k in range(2):
                        if k == 0:
                            ch.step(V_.tensor_scalar(c3, ebase[:, 1, :].unsqueeze(2).to_broadcast([128, NE, nb]), 3.0, None, ALU.mult), v_chain)
                        else:
                            op2(c3, thr[:, 0:nb].unsqueeze(1).to_broadcast([128, NE, nb]), thr[:, 0:nb].unsqueeze(1).to_broadcast([128, NE, nb]), ALU.max)
                            ch.step(V_.tensor_scalar(c3, c3, -1.0, None, ALU.add), v_chain)
                        op2(t1, t0, code.unsqueeze(1).to_broadcast([128, EXTRA, 64]), ALU.mult)
                        ch.step(V_.reduce_sum(ovf[:, k, 0:EXTRA].unsqueeze(2), t1, axis=AX.X), v_chain)
                    ch.step(V_.tensor_copy(ovi[:], ovf[:, 0]), v_ov)
                    delta = ovq[:, 5, 0:NE]
                    of1 = [v.rearrange("p (e b) -> p e b", b=nb)[:, :, 0] for v in (a, flag)]
                    op2(delta, of1[0], of1[1], ALU.subtract)
                    op2(delta, delta, ebase[:, 1, :], ALU.subtract)
                    ch.step(V_.tensor_scalar(delta, delta, float(NE - 1), 128.0, ALU.add, ALU.mult), v_chain)
                    op2(er, rank1, ebase[:, 0, :].unsqueeze(1).to_broadcast([128, NT, NE]), ALU.add)
                    ch.step(V_.tensor_scalar(rank1, rank1, 128.0, None, ALU.is_gt), v_chain)
                    op2(rank1, rank1, delta.unsqueeze(1).to_broadcast([128, NT, NE]), ALU.mult)
                    op2(er, er, rank1, ALU.add)
                    for k, hot1 in enumerate((one, two)):
                        op2(val, er, hot1, ALU.mult)
                        ch.step(V_.reduce_sum(T[0][:, :, 0:1], val, axis=AX.X), v_chain)
                        ch.step(V_.tensor_copy(yrow[:, k, :], T[0][:, :, 0]), v_chain)
                        op2(val, w_, hot1, ALU.mult)
                        ch.step(V_.reduce_sum(wts[:, k, :].unsqueeze(2), val, axis=AX.X), v_yrow)
                    for e in range(NB):
                        dve.wait_ge(a_esg, e + 1)
                        bank = ps[:, e % 2, :].rearrange("p (j m t) -> p j m t", j=2, m=2)
                        ch.step(V_.tensor_tensor(sig, sig, bank[:, 0], ALU.mult), v_chain)
                        if e >= 2:
                            dve.wait_ge(pe_e, e - 1)
                        ch.step(V_.tensor_tensor(he[:, e % 2], sig, bank[:, 1], ALU.mult), v_he)
                        if e + 3 < NB:
                            if e + 4 < NB:
                                slot_onehot(e + 4)
                            slot_tokens(e + 3)
                        if 3 <= e < 3 + NT:
                            norm_gain(ch, e - 3, 0)
                    dve.wait_ge(g2_in, 32)
                    for v in range(2):
                        ch.step(V_.tensor_tensor(G2[:, v, :], G2[:, v, :], rows[:, 1, :], ALU.add), v_G)

            n_extra = nc.values_load(ovi[0:1, EXTRA:EXTRA + 1], min_val=0, max_val=EXTRA)
            nc.all_engine_barrier(sems_to_clear=all_sems)
            with nc.If(n_extra > 1):
                with nc.Fori(1, n_extra) as j:
                    with nc.Block() as block:
                        @block.sync
                        def _(sp):
                            first = sp.value_load(ovi[0:1, bass.ds(j, 1)], min_val=0, max_val=3 * (NE - 1))
                            for s in range(3):
                                sp.dma_start(ring[:, s, :], A["wall"][layer, first + (MOE0 + s)]).then_inc(full[s], 16)
                            for s in range(3):
                                sp.wait_ge(full[s], 16)

                        @block.gpsimd
                        def _(pool):
                            pool.wait_ge(v_idx, 1)
                            pool.indirect_dma_start(out=xg[:, 0, :], out_offset=None, in_=A["h_rows"],
                                                    in_offset=bass.IndirectOffsetOnAxis(ap=idx[:, NE:NE + 1], axis=0)).then_inc(xg_in[0], 16)
                            pool.wait_ge(xg_in[0], 16)
                            pool.dma_reset(all_sems)

                        @block.tensor
                        def _(pe):
                            pe.wait_ge(v_hot, 1)
                            for t in range(NT):
                                last = nc.tensor.matmul(ps[:, 6, 0:2], hot[:, 0, t, :], tokid[:, t, :], start=t == 0, stop=t == NT - 1)
                            last.then_inc(pe_idx, 1)
                            pe.wait_ge(xg_in[0], 16)
                            for k in range(KB):
                                last = nc.tensor.transpose(ps[:, 2 + k // 4, 128 * (k % 4):128 * (k % 4) + 128],
                                                           xg[:, 0, 128 * k:128 * k + 128], ident[:])
                            last.then_inc(pe_xg, 1)
                            pe.wait_ge(a_xg, 1)
                            for s in range(2):
                                pe.wait_ge(full[s], 16)
                                w = ring[:, s, :].rearrange("p (k n) -> p k n", k=KB)
                                for m in range(2):
                                    for k in range(KB):
                                        last = nc.tensor.matmul(ps[:, 0, 128 * (2 * s + m):128 * (2 * s + m) + 128], w[:, k, 128 * m:128 * m + 128],
                                                                xgT[:, 0, k, :], start=k == 0, stop=k == KB - 1)
                            last.then_inc(pe_h, 1)
                            pe.wait_ge(v_he, 1)
                            pe.wait_ge(full[2], 16)
                            w = ring[:, 2, :].rearrange("p (m n) -> p m n", m=2)
                            for n in range(2):
                                for m in range(2):
                                    last = nc.tensor.matmul(ps[:, 4 + n, :], he[:, 0, m, :], w[:, m, 512 * n:512 * n + 512], start=m == 0, stop=m == 1)
                            last.then_inc(pe_e, 1)

                        @block.scalar
                        def _(act):
                            act.wait_ge(pe_xg, 1)
                            nc.scalar.copy(xgT[:, 0].rearrange("p k t -> p (k t)"), flat(2, 1024)).then_inc(a_xg, 1)
                            act.wait_ge(pe_h, 1)
                            nc.scalar.activation(sig.rearrange("p m t -> p (m t)"), ps[:, 0, 0:256], ACT.Sigmoid).then_inc(a_esg, 1)
                            act.wait_ge(pe_e, 1)
                            nc.scalar.copy(ysb[:, 0, :], flat(4, 1024)).then_inc(a_y, 1)
                            act.wait_ge(a_y, 1)
                            act.dma_start(A["y_rows"][NE + j], ysb[:, 0, :]).then_inc(y_out[0], 16)
                            act.wait_ge(y_out[0], 16)

                        @block.vector
                        def _(dve):
                            ch = Chain(dve)
                            further_ranks(ch, bass.ds(j, 1))
                            ch.step(nc.vector.tensor_tensor(hot[:, 0], route[:, 13, :, 0:1].to_broadcast([128, NT, 128]),
                                                            iota1[:].unsqueeze(1).to_broadcast([128, NT, 128]), ALU.is_equal), v_hot)
                            dve.wait_ge(pe_idx, 1)
                            ch.step(nc.vector.reduce_sum(small_i[:, 0:1], ps[:, 6, 0:2], axis=AX.X), v_chain)
                            ch.step(nc.vector.tensor_copy(idx[:, NE:NE + 1], small_i[:, 0:1]), v_idx)
                            dve.wait_ge(a_esg, 1)
                            bank = ps[:, 0, :].rearrange("p (j m t) -> p j m t", j=2, m=2)
                            ch.step(nc.vector.tensor_tensor(sig, sig, bank[:, 0], ALU.mult), v_chain)
                            ch.step(nc.vector.tensor_tensor(he[:, 0], sig, bank[:, 1], ALU.mult), v_he)

                    nc.all_engine_barrier(sems_to_clear=all_sems)

            following = (layer + 1) % DEPTH
            with nc.Block() as block:
                @block.sync
                def _(sp):
                    sp.dma_start(par[:], A["par"][following]).then_inc(par_in, 16)
                    sp.wait_ge(yt_in[NT // 2], 32)
                    open_sp(sp, following)

                @block.tensor
                def _(pe):
                    open_pe(pe)

                @block.gpsimd
                def _(pool):
                    ch = Chain(pool)
                    y_all = A["y_rows"].rearrange("b p n -> (b p) n")
                    pool.wait_ge(y_init, 16 * len(range(1, EXTRA, 4)))
                    for t in range(NT):
                        for k, Y in enumerate((Y1, Y2)):
                            pool.indirect_dma_start(out=Y[:, t, :], out_offset=None, in_=y_all,
                                                    in_offset=bass.IndirectOffsetOnAxis(ap=yrow[:, k, t:t + 1], axis=0)).then_inc(yt_in[t], 16)
                    for s in range(NT + 2):
                        if POOL_GATES <= s < NT:
                            pool.wait_ge(v_sum, s + 1)
                            ch.step(nc.gpsimd.tensor_tensor(Y1[:, s, :], Y1[:, s, :], G2[:, int(s == CTX), :], ALU.mult), g_gated)
                        if 1 <= s <= NT:
                            scale_power(pool, ch, s, s - 1)
                        if 2 <= s < POOL_OFFSETS + 2:
                            pool.wait_ge(v_gain, s - 1)
                            ch.step(nc.gpsimd.tensor_tensor(x[:, s - 2, :], x[:, s - 2, :], rows[:, 5, :], ALU.add), g_x)
                    pool.dma_reset(all_sems)

                @block.scalar
                def _(act):
                    ch = Chain(act)
                    for s in range(NT + 2):
                        if s < NT:
                            act.wait_ge(yt_in[s], 32)
                            ch.step(nc.scalar.activation(Y1[:, s, :], Y1[:, s, :], ACT.Copy, scale=wts[:, 0, s:s + 1]), a_w)
                        if s >= 2:
                            scale_tile(act, ch, s - 2, s - 1)
                        if s >= OPEN_AT:
                            open_act(act, ch, s - OPEN_AT)

                @block.vector
                def _(dve):
                    ch = Chain(dve)
                    for s in range(NT + 2):
                        if s < NT:
                            dve.wait_ge(a_w, s + 1)
                            ch.step(nc.vector.scalar_tensor_tensor(Y1[:, s, :], Y2[:, s, :], wts[:, 1, s:s + 1], Y1[:, s, :], ALU.mult, ALU.add), v_sum)
                        if s >= 2:
                            norm_shift(dve, ch, s - 2, 0)
                        if 1 <= s <= NT:
                            t = s - 1
                            if t < POOL_GATES:
                                ch.step(nc.vector.tensor_tensor(Y1[:, t, :], Y1[:, t, :], G2[:, int(t == CTX), :], ALU.mult), v_chain)
                            else:
                                dve.wait_ge(g_gated, t + 1 - POOL_GATES)
                            ch.step(nc.vector.scalar_tensor_tensor(x[:, t, :], x[:, t, :], ALPHA, Y1[:, t, :], ALU.mult, ALU.add), v_chain)
                            norm_stats(ch, t)
                        if s >= 2:
                            dve.wait_ge(a_ln, s - 1)
                            if s - 2 < POOL_OFFSETS:
                                ch.step(nc.vector.tensor_tensor(x[:, s - 2, :], x[:, s - 2, :], rows[:, 3, :], ALU.mult), v_gain)
                            else:
                                norm_gain(ch, s - 2, 1)
                        if s >= OPEN_AT:
                            open_dve(dve, ch, s - OPEN_AT)

            nc.all_engine_barrier(sems_to_clear=all_sems)

        with nc.Block() as block:
            @block.sync
            def _(sp):
                sp.dma_start(OUT["y"].rearrange("t p n -> p t n"), x[:]).then_inc(x_out, 16)
                sp.wait_ge(x_out, 16)


def positions():
    g, r, c = np.meshgrid(np.arange(LAT), np.arange(ROWS), np.arange(GW), indexing="ij")
    return (r * GRID_W + g * GW + c).ravel()


def rope_tables():
    t = positions()
    n = HD // 4
    freqs = (np.float32(10000.0) ** (-np.arange(n, dtype=np.float32) / np.float32(n))).astype(np.float32)
    ang = np.concatenate([(t // GRID_W).astype(np.float32)[:, None] * freqs,
                          (t % GRID_W).astype(np.float32)[:, None] * freqs], -1)
    cos, sin = np.cos(ang), np.sin(ang)
    c = np.stack([cos, cos], -1).reshape(LAT, 128, HD)
    s = np.stack([-sin, sin], -1).reshape(LAT, 128, HD)
    return (np.ascontiguousarray(a.transpose(1, 0, 2).astype(np.float32)) for a in (c, s))


def window_mask():
    m = np.full((128, LAT, 3 * GW), FAR, np.float32)
    for g in range(LAT):
        for ci in range(GW):
            c = g * GW + ci
            cs = min(max(c - NA_KW // 2, 0), GRID_W - NA_KW)
            for u in range(3 * GW):
                k = GW * (g - 1) + u
                if cs <= k < cs + NA_KW:
                    m[ci::GW, g, u] = 0
    return m


def lay_out(i):
    f = np.float32
    L = DEPTH
    pos = positions()
    a = {}
    a["x"] = np.concatenate([i["x_sample"][0][pos], i["x_prompt"][0]]).reshape(NT, 128, D)
    cs = np.zeros((128, KB, 32), f)
    cs[:, :, 0] = i["c"][0].reshape(KB, 128).T
    cs[:, :, 1] = i["c_ctx"].reshape(KB, 128).T
    a["cs"] = cs
    a["ident"] = np.eye(128, dtype=f)
    sel = np.zeros((128, 2), f)
    for j in range(4):
        for v in range(2):
            sel[32 * j + v, v] = 1
    a["sel"] = sel
    a["cosT"], a["sinT"] = rope_tables()
    a["mask"] = window_mask()
    a["wr"] = i["w_router"].reshape(KB, 128, NE).transpose(1, 0, 2)
    a["rbias"] = np.broadcast_to(i["router_bias"], (128, NE))
    a["eidx"] = np.broadcast_to(np.arange(NE, 0, -1).astype(f), (128, NE))

    a["iota1"] = np.broadcast_to(np.arange(1, 129).astype(f), (128, 128))
    a["ebase"] = np.broadcast_to(np.stack([np.arange(NE) * 128 - 1, np.arange(NE)]).astype(f), (128, 2, NE))
    counting = np.ones((128, 256 + 2 * NT), f)
    counting[:, 0:128] = np.arange(128)[:, None] < np.arange(128)[None]
    for t in range(NT):
        counting[:, 256 + 2 * t] = np.arange(128)
        counting[:, 257 + 2 * t] = 128 * t
    a["counting"] = counting

    def kparts(w, n0, n1):
        w = w[:, n0:n1]
        return w.reshape(-1, 128, n1 - n0).transpose(1, 0, 2).reshape(128, -1)

    wall = np.empty((L, len(WALL), 128, PIECE), f)
    for l in range(L):
        for n, p in enumerate(WALL):
            if p[0] == "mod":
                w = i["w_mod"][l][512 * p[2]:512 * p[2] + 512]
                wall[l, n] = kparts(w, 512 * p[1], 512 * p[1] + 512)
            elif p[0] == "in":
                if p[1] < 7:
                    wall[l, n] = kparts(i["w_in"][l][512 * p[2]:512 * p[2] + 512], 512 * p[1], 512 * p[1] + 512)
                else:
                    wall[l, n] = kparts(i["w_in"][l], 3584, 3840)
            elif p[0] == "gate":
                n0 = D * p[1] + 256 * p[2]
                wall[l, n] = kparts(i["w_gate"][l], n0, n0 + 256)
            elif p[0] == "br":
                wall[l, n] = kparts(i["w_br"][l, p[1]], 512 * p[2], 512 * p[2] + 512)
            elif p[0] == "o":
                wall[l, n] = kparts(i["w_o"][l][512 * p[2]:512 * p[2] + 512], 512 * p[1], 512 * p[1] + 512)
            elif p[0] == "w1":
                wall[l, n] = kparts(i["moe_w1"][l, p[1]], 0, DE)
            elif p[0] == "w3":
                wall[l, n] = kparts(i["moe_w3"][l, p[1]], 0, DE)
            else:
                wall[l, n] = kparts(i["moe_w2"][l, p[1]], 0, D)
    a["wall"] = wall

    par = np.empty((L, 128, 586), f)
    par[:, :, 0:48] = i["b_mod"].reshape(L, 48, 128).transpose(0, 2, 1)
    par[:, :, 48:72] = i["b_gate"].reshape(L, 24, 128).transpose(0, 2, 1)
    par[:, :, 72:200] = i["a_subln"][:, None, :]
    par[:, :, 200:264] = i["c_qnorm"][:, None, :]
    par[:, :, 264:328] = i["c_knorm"][:, None, :]
    par[:, :, 328:584] = i["lam"].reshape(L, 1, 256)
    for l in range(L):
        init = 0.8 - 0.6 * math.exp(-0.3 * l)
        par[l, :, 584], par[l, :, 585] = init, 1.0 - init
    a["par"] = par
    rows = np.empty((L, 128, 8, D), f)
    rows[:, :, 6] = i["b_mod"][:, None, 3 * D:4 * D]
    rows[:, :, 7] = i["b_mod"][:, None, 4 * D:5 * D]
    rows[:, :, 0] = i["b_mod"][:, None, 2 * D:3 * D]
    rows[:, :, 1] = i["b_mod"][:, None, 5 * D:6 * D]
    rows[:, :, 2:4] = i["ln_g"][:, None]
    rows[:, :, 4:6] = i["ln_b"][:, None]
    a["rows"] = rows

    ck = np.zeros((L, 3, 128, 8, 128), f)
    cv = np.zeros((L, 3, 128, 512), f)
    ka = i["cache_a_k"][0].reshape(L, 128, 8, HD)
    kb = i["cache_b_k"][0]
    kc = i["cache_c_k"][0]
    for h in range(8):
        lo = 64 * (h % 2)
        ck[:, 0, lo:lo + 64, h] = ka[:, :, h].transpose(0, 2, 1)
        ck[:, 1, lo:lo + 64, h] = kb[:, :, h].transpose(0, 2, 1)
        if h < 4:
            ck[:, 2, lo:lo + 64, h] = kc[:, :, h // 2].transpose(0, 2, 1)
    cv[:, 0] = i["cache_a_v"][0].reshape(L, 128, 512)
    cv[:, 1] = i["cache_b_v"][0].reshape(L, 128, 512)
    cv[:, 2, :, 0:128] = i["cache_c_v"][0].reshape(L, 128, 128)
    a["cache_kT"], a["cache_v"] = ck, cv

    pad = np.full((L, 8, 15, 3 * GW + GW + 15), FAR, f)
    pad[:, :, :, 16:47] = i["rpb"]
    bias = np.empty((L, 8, ROWS, GW, ROWS, 3 * GW), f)
    for r in range(ROWS):
        for ci in range(GW):
            bias[:, :, r, ci] = pad[:, :, 7 - r:15 - r, 15 - ci:15 - ci + 3 * GW]
    a["bias"] = bias.reshape(L, 8, 128, ROWS, 3 * GW)
    return {k: np.ascontiguousarray(v) for k, v in a.items()}


def kernel(**inputs):
    import concourse.bacc as bacc
    from concourse.bass_utils import run_bass_kernel_spmd

    arrays = {"in_" + k: v for k, v in lay_out({k: np.asarray(v) for k, v in inputs.items()}).items()}
    f32 = mybir.dt.float32
    nc = bacc.Bacc("TRN2", target_bir_lowering=False, num_devices=1)
    A = {k[3:]: nc.dram_tensor(k, v.shape, f32, kind="ExternalInput").ap() for k, v in arrays.items()}
    A["x_state"] = nc.dram_tensor("x_state", (NT, 128, D), f32, kind="Internal").ap()
    A["h_rows"] = nc.dram_tensor("h_rows", (TOK, D), f32, kind="Internal").ap()
    A["y_rows"] = nc.dram_tensor("y_rows", (NE + EXTRA, 128, D), f32, kind="Internal").ap()
    A["mrows"] = nc.dram_tensor("mrows", (2, 4, D), f32, kind="Internal").ap()
    shapes = {"y": (NT, 128, D), "ak": (DEPTH, 128, 512), "av": (DEPTH, 128, 512), "bk": (DEPTH, 128, 512),
              "bv": (DEPTH, 128, 512), "ck": (DEPTH, 128, 128), "cv": (DEPTH, 128, 128)}
    OUT = {k: nc.dram_tensor("out_" + k, s, f32, kind="ExternalOutput").ap() for k, s in shapes.items()}
    build_kernel(nc, A, OUT)
    r = run_bass_kernel_spmd(nc, [arrays], core_ids=[0]).results[0]
    y = r["out_y"].reshape(TOK, D)
    ys = np.empty((LTOK, D), np.float32)
    ys[positions()] = y[:LTOK]
    return (y[LTOK:][None], ys[None],
            r["out_ak"].reshape(1, DEPTH, 128, 2, 4, HD), r["out_av"].reshape(1, DEPTH, 128, 4, 2 * HD),
            r["out_bk"].reshape(1, DEPTH, 128, 8, HD), r["out_bv"].reshape(1, DEPTH, 128, 8, HD),
            r["out_ck"].reshape(1, DEPTH, 128, 2, HD), r["out_cv"].reshape(1, DEPTH, 128, 2, HD))
```
